# Optimizing a Trainium2 kernel written in Bass

```python
import math
import jax, jax.numpy as jnp
from jax import lax
import numpy as np

D_MODEL = 2048
BATCH = 1
SEQ = 256
DEPTH = 1

D_MIX = D_MODEL
D_ATTN = D_MIX // 2
D_SSM = D_MIX - D_ATTN
HEAD_DIM = 64
N_Q_HEADS = D_ATTN // HEAD_DIM
N_KV_HEADS = 2
Q_PER_KV = N_Q_HEADS // N_KV_HEADS
D_KV = N_KV_HEADS * HEAD_DIM
WINDOW = 128
BLOCK = 128
NUM_BUCKETS = 32
MAX_DISTANCE = 128
SSM_GROUP = 16
N_SSM_GROUPS = D_SSM // SSM_GROUP
SSM_STATE = 64
DT_MIN = 0.001
DT_MAX = 0.1
N_EXPERT_GROUPS = 4
EXPERTS_PER_GROUP = 8
TOP_K = 2
D_FF_EXPERT = 512

D_IN_PROJ = D_ATTN + 2 * D_KV + D_SSM
EPS = 1e-6
NEG_INF = -1e30

kernel_name = "hymba_swa_s5_hiermoe_block"

def rmsnorm(x, g):
    x32 = x.astype(jnp.float32)
    y = x32 * lax.rsqrt(jnp.mean(x32 * x32, axis=-1, keepdims=True) + EPS)
    return (y * g.astype(jnp.float32)).astype(x.dtype)

def t5_bucket(n):
    max_exact = NUM_BUCKETS // 2
    nf = jnp.maximum(n, 1).astype(jnp.float32)
    large = max_exact + (jnp.log(nf / max_exact) / math.log(MAX_DISTANCE / max_exact)
                         * (NUM_BUCKETS - max_exact)).astype(jnp.int32)
    large = jnp.minimum(large, NUM_BUCKETS - 1)
    return jnp.where(n < max_exact, n, large)

def band_offsets():
    i = jnp.arange(BLOCK)[:, None]
    j = jnp.arange(2 * BLOCK)[None, :]
    return i + BLOCK - j, j

def t5_block_bias(table):
    dist, _ = band_offsets()
    bias = table[t5_bucket(jnp.maximum(dist, 0))]
    return jnp.transpose(bias, (2, 0, 1)).astype(jnp.float32)

def sliding_window_attention(q, k, v, sinks, bias_table):
    bsz, seq = q.shape[0], q.shape[1]
    nb = seq // BLOCK
    qb = q.reshape(bsz, nb, BLOCK, N_KV_HEADS, Q_PER_KV, HEAD_DIM)

    def band(t):
        prev = jnp.pad(t, ((0, 0), (BLOCK, 0), (0, 0), (0, 0)))[:, :seq]
        prev = prev.reshape(bsz, nb, BLOCK, N_KV_HEADS, HEAD_DIM)
        cur = t.reshape(bsz, nb, BLOCK, N_KV_HEADS, HEAD_DIM)
        return jnp.concatenate([prev, cur], axis=2)

    kb, vb = band(k), band(v)
    scores = jnp.einsum('bnqkgd,bnskd->bnkgqs', qb, kb,
                        preferred_element_type=jnp.float32) * (HEAD_DIM ** -0.5)
    bias = t5_block_bias(bias_table).reshape(N_KV_HEADS, Q_PER_KV, BLOCK, 2 * BLOCK)
    scores = scores + bias
    dist, j = band_offsets()
    kpos = jnp.arange(nb)[:, None, None] * BLOCK - BLOCK + j[None]
    valid = (dist >= 0)[None] & (dist < WINDOW)[None] & (kpos >= 0)
    scores = jnp.where(valid[None, :, None, None], scores, NEG_INF)
    sink = jnp.broadcast_to(sinks.astype(jnp.float32).reshape(N_KV_HEADS, Q_PER_KV, 1, 1),
                            scores.shape[:-1] + (1,))
    probs = jax.nn.softmax(jnp.concatenate([scores, sink], axis=-1), axis=-1)[..., :-1]
    out = jnp.einsum('bnkgqs,bnskd->bnqkgd', probs.astype(vb.dtype), vb)
    return out.reshape(bsz, seq, N_Q_HEADS * HEAD_DIM)

def complex_affine_combine(c1, c2):
    a1r, a1i, b1r, b1i = c1
    a2r, a2i, b2r, b2i = c2
    return (a2r * a1r - a2i * a1i,
            a2r * a1i + a2i * a1r,
            a2r * b1r - a2i * b1i + b2r,
            a2r * b1i + a2i * b1r + b2i)

def s5_mixer(u, lam_re, lam_im, log_dt, b_re, b_im, c_re, c_im, d_skip, w_glu, b_glu):
    f32 = jnp.float32
    bsz, seq = u.shape[0], u.shape[1]
    ug = u.astype(f32).reshape(bsz, seq, N_SSM_GROUPS, SSM_GROUP)
    dt = jnp.exp(log_dt.astype(f32))[:, None]
    lr, li = lam_re.astype(f32), lam_im.astype(f32)
    mag = jnp.exp(lr * dt)
    ar, ai = mag * jnp.cos(li * dt), mag * jnp.sin(li * dt)
    den = lr * lr + li * li
    cr = ((ar - 1.0) * lr + ai * li) / den
    ci = (ai * lr - (ar - 1.0) * li) / den
    bu_r = jnp.einsum('blgh,gph->blgp', ug, b_re.astype(f32))
    bu_i = jnp.einsum('blgh,gph->blgp', ug, b_im.astype(f32))
    br = cr * bu_r - ci * bu_i
    bi = cr * bu_i + ci * bu_r
    a_r = jnp.broadcast_to(ar, br.shape)
    a_i = jnp.broadcast_to(ai, br.shape)
    _, _, xr, xi = lax.associative_scan(complex_affine_combine, (a_r, a_i, br, bi), axis=1)
    y = (jnp.einsum('ghp,blgp->blgh', c_re.astype(f32), xr)
         - jnp.einsum('ghp,blgp->blgh', c_im.astype(f32), xi)
         + d_skip.astype(f32) * ug)
    y = jax.nn.gelu(y.reshape(bsz, seq, D_SSM))
    y = y * jax.nn.sigmoid(y @ w_glu.astype(f32) + b_glu.astype(f32))
    return y.astype(u.dtype)

def hierarchical_moe(h, w_router_group, b_router_group, w_router_expert, b_router_expert,
                     w_gate, w_up, w_down):
    f32 = jnp.float32
    bsz, seq, d = h.shape
    t = h.reshape(bsz * seq, d)
    g_probs = jax.nn.softmax((t @ w_router_group).astype(f32) + b_router_group.astype(f32), axis=-1)
    g_idx = jnp.argmax(g_probs, axis=-1)
    g_gate = jnp.take_along_axis(g_probs, g_idx[:, None], axis=-1)
    e_logits = (jnp.einsum('td,gde->tge', t, w_router_expert).astype(f32)
                + b_router_expert.astype(f32))
    e_sel = jnp.take_along_axis(e_logits, g_idx[:, None, None], axis=1)[:, 0]
    top_vals, top_idx = lax.top_k(e_sel, TOP_K)
    top_w = jax.nn.softmax(top_vals, axis=-1) * g_gate
    expert_w = jnp.sum(jax.nn.one_hot(top_idx, EXPERTS_PER_GROUP, dtype=f32)
                       * top_w[..., None], axis=1)
    group_mask = jax.nn.one_hot(g_idx, N_EXPERT_GROUPS, dtype=f32)
    out = jnp.zeros((bsz * seq, d), f32)
    for g in range(N_EXPERT_GROUPS):
        gate = jnp.einsum('td,edf->tef', t, w_gate[g])
        up = jnp.einsum('td,edf->tef', t, w_up[g])
        wgt = (expert_w * group_mask[:, g:g + 1])[..., None]
        hid = (jax.nn.silu(gate) * up).astype(f32) * wgt
        out = out + jnp.einsum('tef,efd->td', hid.astype(t.dtype), w_down[g],
                               preferred_element_type=f32)
    return out.reshape(bsz, seq, d).astype(h.dtype)

def hybrid_layer(x, rel_bias_table, g_norm_mix, w_in, attn_sinks, lam_re, lam_im, log_dt,
                 ssm_b_re, ssm_b_im, ssm_c_re, ssm_c_im, ssm_d, w_glu, b_glu,
                 g_attn_out, g_ssm_out, w_out, g_norm_ffn, w_router_group, b_router_group,
                 w_router_expert, b_router_expert, w_gate, w_up, w_down):
    bsz, seq, _ = x.shape
    h = rmsnorm(x, g_norm_mix)
    proj = h @ w_in
    q, k, v, u = jnp.split(proj, [D_ATTN, D_ATTN + D_KV, D_ATTN + 2 * D_KV], axis=-1)
    q = q.reshape(bsz, seq, N_Q_HEADS, HEAD_DIM)
    k = k.reshape(bsz, seq, N_KV_HEADS, HEAD_DIM)
    v = v.reshape(bsz, seq, N_KV_HEADS, HEAD_DIM)
    attn = sliding_window_attention(q, k, v, attn_sinks, rel_bias_table)
    ssm = s5_mixer(u, lam_re, lam_im, log_dt, ssm_b_re, ssm_b_im, ssm_c_re, ssm_c_im,
                   ssm_d, w_glu, b_glu)
    mixed = jnp.concatenate([rmsnorm(attn, g_attn_out), rmsnorm(ssm, g_ssm_out)], axis=-1)
    x = x + mixed @ w_out
    x = x + hierarchical_moe(rmsnorm(x, g_norm_ffn), w_router_group, b_router_group,
                             w_router_expert, b_router_expert, w_gate, w_up, w_down)
    return x

def setup_inputs(seed: int = 0) -> dict:
    key = jax.random.key(seed)
    ks = jax.random.split(key, 32)
    f32 = jnp.float32
    nrm = lambda k, shape, scale: jax.random.normal(k, shape, f32) * scale
    L = DEPTH
    G, P, HG = N_SSM_GROUPS, SSM_STATE, SSM_GROUP
    NG, E, F = N_EXPERT_GROUPS, EXPERTS_PER_GROUP, D_FF_EXPERT
    lam_im = (jnp.pi * jnp.arange(P, dtype=f32))[None, None, :] + nrm(ks[6], (L, G, P), 0.01)
    log_dt = jax.random.uniform(ks[7], (L, G), f32, math.log(DT_MIN), math.log(DT_MAX))
    return {
        "x": nrm(ks[0], (BATCH, SEQ, D_MODEL), 1.0),
        "rel_bias_table": nrm(ks[1], (NUM_BUCKETS, N_Q_HEADS), 0.5),
        "g_norm_mix": 1.0 + nrm(ks[2], (L, D_MODEL), 0.02),
        "w_in": nrm(ks[3], (L, D_MODEL, D_IN_PROJ), D_MODEL ** -0.5),
        "attn_sinks": nrm(ks[4], (L, N_Q_HEADS), 0.5),
        "lam_re": -0.5 + nrm(ks[5], (L, G, P), 0.01),
        "lam_im": lam_im,
        "log_dt": log_dt,
        "ssm_b_re": nrm(ks[8], (L, G, P, HG), (2.0 * HG) ** -0.5),
        "ssm_b_im": nrm(ks[9], (L, G, P, HG), (2.0 * HG) ** -0.5),
        "ssm_c_re": nrm(ks[10], (L, G, HG, P), (2.0 * P) ** -0.5),
        "ssm_c_im": nrm(ks[11], (L, G, HG, P), (2.0 * P) ** -0.5),
        "ssm_d": nrm(ks[12], (L, G, HG), 1.0),
        "w_glu": nrm(ks[13], (L, D_SSM, D_SSM), D_SSM ** -0.5),
        "b_glu": nrm(ks[14], (L, D_SSM), 0.02),
        "g_attn_out": 1.0 + nrm(ks[15], (L, D_ATTN), 0.02),
        "g_ssm_out": 1.0 + nrm(ks[16], (L, D_SSM), 0.02),
        "w_out": nrm(ks[17], (L, D_MIX, D_MODEL), D_MIX ** -0.5),
        "g_norm_ffn": 1.0 + nrm(ks[18], (L, D_MODEL), 0.02),
        "w_router_group": nrm(ks[19], (L, D_MODEL, NG), D_MODEL ** -0.5),
        "b_router_group": nrm(ks[20], (L, NG), 0.01),
        "w_router_expert": nrm(ks[21], (L, NG, D_MODEL, E), D_MODEL ** -0.5),
        "b_router_expert": nrm(ks[22], (L, NG, E), 0.01),
        "w_gate": nrm(ks[23], (L, NG, E, D_MODEL, F), D_MODEL ** -0.5),
        "w_up": nrm(ks[24], (L, NG, E, D_MODEL, F), D_MODEL ** -0.5),
        "w_down": nrm(ks[25], (L, NG, E, F, D_MODEL), F ** -0.5),
        "g_final": 1.0 + nrm(ks[26], (D_MODEL,), 0.02),
    }

def reference(x, rel_bias_table, g_norm_mix, w_in, attn_sinks, lam_re, lam_im, log_dt,
              ssm_b_re, ssm_b_im, ssm_c_re, ssm_c_im, ssm_d, w_glu, b_glu,
              g_attn_out, g_ssm_out, w_out, g_norm_ffn, w_router_group, b_router_group,
              w_router_expert, b_router_expert, w_gate, w_up, w_down, g_final):
    for l in range(DEPTH):
        x = hybrid_layer(x, rel_bias_table, g_norm_mix[l], w_in[l], attn_sinks[l],
                         lam_re[l], lam_im[l], log_dt[l], ssm_b_re[l], ssm_b_im[l],
                         ssm_c_re[l], ssm_c_im[l], ssm_d[l], w_glu[l], b_glu[l],
                         g_attn_out[l], g_ssm_out[l], w_out[l], g_norm_ffn[l],
                         w_router_group[l], b_router_group[l], w_router_expert[l],
                         b_router_expert[l], w_gate[l], w_up[l], w_down[l])
    return rmsnorm(x, g_final)


_drawn_inputs = setup_inputs


def setup_inputs(seed=0):
    import zlib

    import numpy as np

    out = dict(_drawn_inputs(seed))
    spreads = {}
    factors = {'attn_sinks': 3.529,
     'lam_re': 8.0,
     'b_glu': 6.556,
     'g_attn_out': 4.316,
     'g_ssm_out': 4.005,
     'g_norm_ffn': 3.786,
     'b_router_group': 4.876,
     'b_router_expert': 7.642,
     'g_final': 2.902}
    for name, (base, spread) in spreads.items():
        noise = np.random.default_rng([zlib.crc32(name.encode()), seed]).standard_normal(out[name].shape)
        drawn = base * np.exp(spread * noise) if base else spread * noise
        out[name] = __import__('jax').numpy.asarray(drawn.astype(out[name].dtype))
    for name, factor in factors.items():
        out[name] = (out[name] * factor).astype(out[name].dtype)
    return out
```

```python
from contextlib import ExitStack

import concourse.bass as bass
from concourse import mybir

F32 = mybir.dt.float32
I32 = mybir.dt.int32
ALU = mybir.AluOpType
ACT = mybir.ActivationFunctionType
AX = mybir.AxisListType.X

P = 128
D, T, TB = 2048, 256, 2
DC = D // P
NH, HD = 16, 64
W = 128
G, SC, NS = 64, 16, 64
NPAIR = G // 2
Q = 4
NCH = T // Q
HP = NPAIR // 2
NE, NG, EG, FF = 32, 4, 8, 512
SLOTS = 2 * T
CAP = 64
XMAX = SLOTS // CAP
PADDED = SLOTS + CAP
RING, SLOT = 6, 4096
PRE = 3
N_WIN, N_GLU, N_OUT = 9, 2, 8
NPRE = N_WIN + N_GLU + N_OUT
EPS = 1e-6
NEG = -1e30
PI = 3.14159265358979
MAGIC = 12582912.0
TWO_PI_HI = 6.28125
TWO_PI_LO = 2 * PI - TWO_PI_HI


def bcast(ap, axis, n):
    v = ap.unsqueeze(axis)
    shape = list(v.shape)
    shape[axis] = n
    return v.broadcast_to(shape)


class Count:

    def __init__(self, sem):
        self.sem, self.n = sem, 0

    def inc(self, ins, by=1):
        self.n += by
        ins.then_inc(self.sem, by)
        return self.n


def hymba_block(nc, a, out):
    with ExitStack() as ctx:
        def sem(name):
            return ctx.enter_context(nc.semaphore(name))

        arena = ctx.enter_context(nc.sbuf_tensor("arena", [P, RING * SLOT + 2 * 9216 + 2 * 4096], F32))
        psum = ctx.enter_context(nc.psum_tensor("psum", [P, 8, 512], F32))
        skew = nc.dram_tensor("bias_skew", [NH, P, 384], F32, kind="Internal")

        def view(start, shape):
            n = 1
            for s in shape:
                n *= s
            v = arena[:, start:start + n]
            if len(shape) > 1:
                names = ["a", "b", "c", "d"][:len(shape)]
                v = v.rearrange(f"p ({' '.join(names)}) -> p {' '.join(names)}",
                                **dict(zip(names[1:], shape[1:])))
            return v

        def small(name, shape, dt=F32):
            return ctx.enter_context(nc.sbuf_tensor(name, [P] + shape, dt))

        ssm_params = ctx.enter_context(nc.sbuf_tensor("ssm_params", [P, 42 * NPAIR], F32))
        at = [0]

        def param(*shape):
            n = 1
            for k in shape:
                n *= k
            v = ssm_params[:, at[0]:at[0] + n]
            at[0] += n
            return v.rearrange("p (k j) -> p k j", k=shape[0]) if len(shape) > 1 else v

        ring = [view(SLOT * k, [SLOT]) for k in range(RING)]
        C0 = PRE * SLOT
        bias = view(C0, [NH, 2 * W])
        scores = view(C0 + 4096, [4, 3 * W])
        attn = view(C0 + 5632, [TB, NH * HD])
        kk = view(C0 + 7680, [2, T])
        vv = view(C0 + 8192, [TB, 2 * HD])
        bbar_r = view(C0 + 8448, [NPAIR, 2 * SC])
        bbar_i = view(C0 + 9472, [NPAIR, 2 * SC])
        craw_r = view(C0 + 10496, [NPAIR, SC])
        craw_i = view(C0 + 11008, [NPAIR, SC])
        bias_row = view(C0 + 11520, [2, 384])
        braw_r = view(C0 + 4096, [NPAIR, SC])
        braw_i = view(C0 + 4608, [NPAIR, SC])
        tab_wide = view(C0, [NH, P])
        onehot = view(C0 + 2048, [384])
        table = view(C0 + 2432, [NH])

        M0 = RING * SLOT
        u4 = view(M0, [NPAIR, NCH])
        bp_r = view(M0 + 2048, [HP, Q, 2 * SC])
        bp_i = view(M0 + 4096, [HP, Q, 2 * SC])
        z_r, z_i, tmp_a, tmp_b = (view(M0 + 2048 + 1024 * k, [HP, NCH]) for k in range(4))
        bt_r = view(M0 + 6144, [HP, P])
        bt_i = view(M0 + 8192, [HP, P])
        decay = view(M0 + 6144, [HP, NCH])
        cp_r = view(M0 + 10240, [HP, Q, 2 * SC])
        cp_i = view(M0 + 12288, [HP, Q, 2 * SC])
        toep = view(M0 + 14336, [HP, Q, 2 * SC])
        cos_t = view(M0 + 16384, [HP, NCH])
        sin_t = view(M0 + 17408, [HP, NCH])
        full_tmp = view(M0 + 10240, [NPAIR, SC])

        h_sorted = view(M0, [DC, PADDED])
        y_sorted = view(M0 + 9216, [DC, PADDED])
        h2 = view(M0 + 9216, [TB, D])
        h2T = view(M0 + 9216 + 4096, [DC, T])
        rt = M0 + 9216 + 8192
        wr = view(M0, [DC, NG + NE])

        R1 = M0 + 18432
        x1 = view(R1, [TB, D])
        uT = view(R1, [8, T])
        qT = view(R1 + 2048, [8, T])
        R2 = R1 + 4096
        hT = view(R2, [DC, T])
        mixT = view(R2, [DC, T])
        sel = view(R2, [TB, SLOTS])
        selw = view(R2 + 1024, [TB, SLOTS])
        selT = view(R2 + 2048, [4, T])
        wrow = view(R2 + 3072, [PADDED])
        keep = R2 + 3072 + PADDED
        hs = view(R2, [DC, CAP])
        gated_h = view(R2 + 1024, [FF])
        hid = view(R2 + 1536, [4, CAP])
        wmask = view(R2 + 1792, [CAP])
        y_tok = view(0, [4, D])
        g_fin = view(M0, [D])
        result = view(M0 + 2048, [TB, D])
        sgate = view(M0 + 4096, [8, T])
        ysq = view(M0 + 6144, [8, T])
        ssm = view(M0, [8, T])
        ssm_rs = view(M0 + 8192, [T])

        ident, ones = small("ident", [P]), small("ones", [P])
        g_mix, g_ffn = small("g_mix", [DC]), small("g_ffn", [DC])
        g_attn, g_ssm = small("g_attn", [8]), small("g_ssm", [8])
        d_skip, b_glu = small("d_skip", [8]), small("b_glu", [8])
        sinks, b_rt = small("sinks", [NH]), small("b_rt", [NG + NE])
        lam_r, lam_i, dt = param(NPAIR), param(NPAIR), param(NPAIR)
        pw_r, pw_i = param(Q + 1, NPAIR), param(Q + 1, NPAIR)
        rev_r, rev_i = param(Q, NPAIR), param(Q, NPAIR)
        e_r, e_i = param(6, NPAIR), param(6, NPAIR)
        mag, ang, rot, sn, cs, c1, c2, c3, c4 = (param(NPAIR) for _ in range(9))
        y_rows = ssm_params[:, 0:2 * 512].rearrange("p (b n) -> p b n", b=2)
        stat = small("stat", [32])
        mxs, sums, recs, esink = (small(n, [4, 2]) for n in ("mxs", "sums", "recs", "esink"))

        landed = [sem(f"ring{k}_landed") for k in range(RING)]
        consumed = sem("ring_consumed")
        x_in, x_again = sem("x_in"), sem("x_again")
        small_in, ssm_in, t5_in = sem("small_in"), sem("ssm_in"), sem("t5_in")
        router_in, gfin_in = sem("router_in"), sem("gfin_in")
        const_ready = sem("const_ready")
        pool_self = sem("pool_self")
        dve, act = sem("dve_self"), sem("act_self")
        x_sq = sem("x_sq")
        h_ready = sem("h_ready")
        hT_t, hT_ready = sem("hT_t"), sem("hT_ready")
        proj_out = sem("proj_out")
        wide_ready, row_done, row_out = sem("wide_ready"), sem("row_done"), sem("row_out")
        row_dma = [sem("row_dma0"), sem("row_dma1")]
        bias_in = sem("bias_in")
        ssm_mag, ssm_sin = sem("ssm_mag"), sem("ssm_sin")
        dt_ready, ang_ready = sem("dt_ready"), sem("ang_ready")
        u4_ready = sem("u4_ready")
        bp_ready, cp_ready = sem("bp_ready"), sem("cp_ready")
        bt_t, bt_out = sem("bt_t"), sem("bt_out")
        toep_zero, toep_mm, toep_out = sem("toep_zero"), sem("toep_mm"), sem("toep_out")
        v_mm, v_read = sem("v_mm"), sem("v_read")
        w_ready, y_mm, y_out = sem("w_ready"), sem("y_mm"), sem("y_out")
        sc_mm, sc_ready, sink_in = sem("sc_mm"), sem("sc_ready"), sem("sink_in")
        probs = sem("probs")
        pt_t, pt_out, pv_mm, pv_out = sem("pt_t"), sem("pt_out"), sem("pv_mm"), sem("pv_out")
        attn_sq, attn_rs, attn_ready, attn_t, attn_out = (sem(n) for n in (
            "attn_sq", "attn_rs", "attn_ready", "attn_t", "attn_out"))
        gelu_in, gelu_out = sem("gelu_in"), sem("gelu_out")
        glu_mm, glu_sig, ssq_ready, ssq_mm, ssq_rt, ssm_out = (sem(n) for n in (
            "glu_mm", "glu_sig", "ssq_ready", "ssq_mm", "ssq_rt", "ssm_out"))
        x1_out, x1_sq, x1_rt, h2_ready = (sem(n) for n in (
            "x1_out", "x1_sq", "x1_rt", "h2_ready"))
        h2_t, h2_out, router_mm = sem("h2_t"), sem("h2_out"), sem("router_mm")
        logit, gexp, eexp = sem("logit"), sem("gexp"), sem("eexp")
        onehot_ready, count_mm, sel_ready, wrow_mm, selT_t = (sem(n) for n in (
            "onehot_ready", "count_mm", "sel_ready", "wrow_mm", "selT_t"))
        gather_act, routed, gather_mm, gather_dve, y_zero = (sem(n) for n in (
            "gather_act", "routed", "gather_mm", "gather_dve", "y_zero"))
        mask_ready, silu_ready, gated, hidT_mm, hid_ready, y_copied, y_copied2, yT_mm, y_added, hs_ready = (sem(n) for n in (
            "mask_ready", "silu_ready", "gated", "hidT_mm", "hid_ready", "y_copied", "y_copied2", "yT_mm", "y_added", "hs_ready"))
        yt_t, yt_act, yt_dve, comb_mm, comb_out, fin_sq, fin_rt, fin_ready, stored = (sem(n) for n in (
            "yt_t", "yt_act", "yt_dve", "comb_mm", "comb_out", "fin_sq", "fin_rt", "fin_ready", "stored"))

        counts = view(keep, [NE])
        base_end = view(keep + 32, [NE])
        xlim = view(keep + 64, [XMAX])
        iota_c = view(keep + 72, [CAP])
        itab = ctx.enter_context(nc.sbuf_tensor("itab", [P, 80], I32))
        base_i, xexp_i, xbase_i, nx_i = itab[:, 0:32], itab[:, 32:40], itab[:, 40:48], itab[:, 48:49]

        rs = lambda o, shape: view(rt + o, shape)
        lg = rs(0, [TB, NG + NE])
        iota_s = view(R2 + 2048, [SLOTS])
        rev_iota = small("rev_iota", [NE])
        iota_e = small("iota_e", [NE])

        gl_exp = rs(72, [TB, NG])
        m_diff = rs(80, [TB, 1])
        g_one = rs(84, [TB, NG])
        g_max = rs(92, [TB, 1])
        e_sel = rs(96, [TB, EG])
        k_one = [rs(112 + 16 * k, [TB, EG]) for k in range(2)]
        m_top = rs(144, [TB, 2])
        t_a, t_b = rs(148, [TB, NG]), rs(160, [TB, EG])
        g_p = rs(176, [TB, 1])
        w_top = rs(180, [TB, 2])
        one32 = [rs(192 + 64 * k, [TB, NE]) for k in range(2)]
        both = rs(320, [TB, NE])
        slot_e = rs(384, [TB, NE])
        slot_t = rs(448, [TB, 2])
        big = rs(512, [XMAX, NE])
        big2 = rs(768, [XMAX, NE])
        nxt, xcum = rs(456, [NE]), small("xcum", [NE])
        prod4 = rs(320, [TB, EG, NG])
        rowf = small("rowf", [3, XMAX])
        y_tmp = view(R2 + 3072, [SLOTS])
        iota_e2 = view(keep + 264, [NE])
        tri = view(keep + 136, [P])

        block = ctx.enter_context(nc.Block())

        def glu_rows(k):
            return a["w_glu"].rearrange("(c p) n -> p c n", p=P)[:, :, 512 * k:512 * (k + 1)]

        W_IN_COLS = [1280 + 256 * k for k in range(4)] + [1024] + [256 * k for k in range(4)]

        def slot3(k, chunks):
            return ring[k].rearrange("p (c n) -> p c n", c=chunks)

        GATE_A, UP_A, GATE_B, UP_B, DOWN_A, DOWN_B = range(6)
        ring_of = lambda k: (PRE + k) % RING
        pre_on = [len([n for n in range(NPRE) if n % PRE == k]) if k < PRE else 0 for k in range(RING)]

        def expert_source(k, e):
            e1 = bass.ds(e, 1)
            if k in (GATE_A, GATE_B):
                return a["w_gate"].rearrange("e (p c) f -> e p c f", p=P)[e1, :, 8 * (k == GATE_B):8 * (k == GATE_B) + 8, :]
            if k in (UP_A, UP_B):
                return a["w_up"].rearrange("e (p c) f -> e p c f", p=P)[e1, :, 8 * (k == UP_B):8 * (k == UP_B) + 8, :]
            return a["w_down"].rearrange("e (p c) d -> e p c d", p=P)[e1, :, 2 * (k == DOWN_B):2 * (k == DOWN_B) + 2, :]

        @block.sync
        def _(sp):
            for b in range(TB):
                sp.dma_start(x1[:, b, :], a["x"][P * b:P * (b + 1), :]).then_inc(x_in, 16)

            def room(n):
                if n >= PRE:
                    sp.wait_ge(consumed, n - PRE + 1)

            n = 0
            for col in W_IN_COLS:
                room(n)
                sp.dma_start(slot3(n % PRE, DC), a["w_in"].rearrange("(p c) n -> p c n", p=P)[:, :, col:col + 256]
                             ).then_inc(landed[n % PRE], 16)
                n += 1
            for k in range(N_GLU):
                room(n)
                sp.dma_start(slot3(n % PRE, 8), glu_rows(k)).then_inc(landed[n % PRE], 16)
                n += 1
            for k in range(N_OUT):
                room(n)
                cols = slice(256 * k, 256 * (k + 1))
                sp.dma_start(slot3(n % PRE, DC)[:, 0:8, :],
                             a["w_out"][0:1024].rearrange("(p c) n -> p c n", p=P)[:, :, cols]).then_inc(landed[n % PRE], 16)
                sp.dma_start(slot3(n % PRE, DC)[:, 8:16, :],
                             a["w_out"][1024:2048].rearrange("(c p) n -> p c n", p=P)[:, :, cols]).then_inc(landed[n % PRE], 16)
                n += 1
                if k == 0:
                    sp.wait_ge(gelu_in, 1)
                    sp.wait_ge(sc_mm, 4)
                    for b in range(TB):
                        sp.dma_start(x1[:, b, :], a["x"][P * b:P * (b + 1), :]).then_inc(x_again, 16)

            def fetch(e, block_no, first=False):
                for k in range(RING):
                    if first and k < PRE:
                        if k == 0:
                            sp.wait_ge(attn_t, 1)
                            sp.wait_ge(toep_mm, 8)
                    elif first:
                        sp.wait_ge(consumed, max(m for m in range(NPRE) if m % PRE == ring_of(k)) + 1)
                    else:
                        sp.wait_ge(consumed, NPRE + RING * (block_no - 1) + k + 1)
                    chunks = 2 if k >= DOWN_A else 8
                    sp.dma_start(slot3(ring_of(k), chunks), expert_source(k, e)).then_inc(landed[ring_of(k)], 16)

            fetch(0, 0, first=True)
            with sp.Fori(1, NE) as e:
                fetch(e, e)
            sp.wait_ge(routed, 1)
            nx = sp.value_load(nx_i[0:1, :], min_val=0, max_val=XMAX - 1)
            with sp.If(nx > 0):
                with sp.Fori(0, nx) as j:
                    e = sp.value_load(xexp_i[0:1, bass.ds(j, 1)], min_val=0, max_val=NE - 1)
                    fetch(e, j + NE)
            for b in range(TB):
                sp.wait_ge(fin_ready, b + 1)
                sp.dma_start(out[P * b:P * (b + 1), :], result[:, b, :]).then_inc(stored, 16)
            sp.wait_ge(stored, 16 * TB)

        @block.gpsimd
        def _(pool):
            me = Count(pool_self)

            def link(ins):
                pool.wait_ge(pool_self, me.inc(ins))

            link(pool.memset(ident[:, :], 0.0))
            pool.affine_select(out=ident[:, :], in_=ident[:, :], compare_op=ALU.not_equal, fill=1.0, base=0,
                               pattern=[[-1, P]], channel_multiplier=1).then_inc(const_ready, 1)
            pool.memset(ones[:, :], 1.0).then_inc(const_ready, 1)
            pool.iota(iota_e[:, :], pattern=[[1, NE]], base=0, channel_multiplier=0,
                      allow_small_or_imprecise_dtypes=True).then_inc(const_ready, 1)
            pool.iota(rev_iota[:, :], pattern=[[-1, NE]], base=NE, channel_multiplier=0,
                      allow_small_or_imprecise_dtypes=True).then_inc(const_ready, 1)
            for m in (bbar_r, bbar_i, cp_r, cp_i, bp_r, bp_i, toep):
                pool.memset(m[:], 0.0).then_inc(const_ready, 1)
            u4v = u4.rearrange("p (c q) t -> p q c t", q=4)
            pool.wait_ge(proj_out, 4)
            pool.wait_ge(const_ready, 11)
            for q in range(4):
                for s in range(Q):
                    if q or s:
                        pool.wait_ge(u4_ready, Q * q + s)
                    pool.tensor_copy(u4v[32 * s:32 * s + 32, q], uT.rearrange("p c (t s) -> p s c t", s=Q)[32 * q:32 * q + 32, s]
                                     ).then_inc(u4_ready, 1)
            pool.wait_ge(u4_ready, 16)
            for h in range(NH):
                pool.wait_ge(row_out, h + 1)
                pool.dma_start(skew[h], bias_row[:, h % 2, :]).then_inc(row_dma[h % 2], 16)
            for k in range(2):
                pool.wait_ge(row_dma[k], 16 * NH // 2)
            for k in range(4):
                pool.dma_start(bias[:, 4 * k:4 * k + 4, :],
                               bass.AP(tensor=skew, offset=4 * k * P * 384 + P - 1,
                                       ap=[[383, P], [P * 384, 4], [1, 2 * W]])).then_inc(bias_in, 16)
            for half in range(2):
                pool.wait_ge(cp_ready, half + 1)
                pool.memset(toep[:], 0.0).then_inc(toep_zero, 1)
                if half == 0:
                    pool.wait_ge(y_mm, 1)
                    pool.memset(bp_r[:], 0.0).then_inc(toep_zero, 1)
                    pool.memset(bp_i[:], 0.0).then_inc(toep_zero, 1)
            pool.wait_ge(consumed, NPRE)
            link(pool.memset(tri[:, :], 1.0))
            pool.affine_select(out=tri[:, :], in_=tri[:, :], compare_op=ALU.is_gt, fill=0.0, base=0,
                               pattern=[[1, P]], channel_multiplier=-1).then_inc(const_ready, 1)
            pool.iota(iota_s[:, :], pattern=[[1, SLOTS]], base=0, channel_multiplier=0,
                      allow_small_or_imprecise_dtypes=True).then_inc(logit, 1)
            pool.iota(iota_c[:, :], pattern=[[1, CAP]], base=0, channel_multiplier=0,
                      allow_small_or_imprecise_dtypes=True).then_inc(logit, 1)
            pool.memset(wrow[:, SLOTS:PADDED], 0.0).then_inc(logit, 1)
            pool.wait_ge(router_mm, 1)
            pool.memset(h_sorted[:, :, SLOTS:PADDED], 0.0).then_inc(y_zero, 1)
            pool.wait_ge(gather_mm, DC)
            pool.wait_ge(routed, 1)
            pool.wait_ge(gather_act, DC // 2)
            pool.wait_ge(gather_dve, DC // 2)
            pool.wait_ge(y_zero, 1)

            def window(base):
                pool.tensor_copy(hs[:, :, :], h_sorted[:, :, bass.ds(base, CAP)]).then_inc(hs_ready, 1)

            pool.memset(gated_h[0:64, :], 0.0).then_inc(y_zero, 1)
            window(pool.value_load(base_i[0:1, 0:1], min_val=0, max_val=SLOTS))
            pool.memset(y_sorted[:], 0.0).then_inc(y_zero, 1)
            with pool.Fori(1, NE) as e:
                base = pool.value_load(base_i[0:1, bass.ds(e, 1)], min_val=0, max_val=SLOTS)
                pool.wait_ge(consumed, RING * e + (NPRE + 4 - RING))
                window(base)
            nx = pool.value_load(nx_i[0:1, :], min_val=0, max_val=XMAX - 1)
            with pool.If(nx > 0):
                with pool.Fori(0, nx) as j:
                    base = pool.value_load(xbase_i[0:1, bass.ds(j, 1)], min_val=0, max_val=SLOTS)
                    pool.wait_ge(consumed, RING * j + (NPRE + 4 + RING * (NE - 1)))
                    window(base)

        @block.scalar
        def _(sc):
            nc_s = nc.scalar
            me = Count(act)

            def link(ins):
                sc.wait_ge(act, me.inc(ins))

            for name, tile in (("g_mix", g_mix), ("g_ffn", g_ffn), ("g_attn", g_attn), ("g_ssm", g_ssm),
                               ("d_skip", d_skip), ("b_glu", b_glu)):
                sc.dma_start(tile[:, :], a[name]).then_inc(small_in, 16)
            sc.dma_start(lam_r[:, :], a["lam_re"]).then_inc(ssm_in, 16)
            sc.dma_start(lam_i[:, :], a["lam_im"]).then_inc(ssm_in, 16)
            for g in range(2):
                sc.dma_start(dt[64 * g:64 * g + 64, :], a["log_dt"][g:g + 1, :].partition_broadcast(64)).then_inc(ssm_in, 16)
            for name, tile in (("b_re", braw_r), ("b_im", braw_i), ("c_re", craw_r), ("c_im", craw_i)):
                sc.dma_start(tile[:, :, :], a[name]).then_inc(ssm_in, 16)
            sc.dma_start(table[0:32, :], a["table"]).then_inc(t5_in, 16)
            sc.dma_start(onehot[0:33, :], a["onehot"]).then_inc(t5_in, 16)
            sc.dma_start(sinks[:, :], a["sinks"].partition_broadcast(P)).then_inc(small_in, 16)
            sc.dma_start(b_rt[:, :], a["b_router"].partition_broadcast(P)).then_inc(small_in, 16)

            for b in range(TB):
                sc.wait_ge(x_in, 32)
                nc_s.activation(hT.rearrange("p c t -> p (c t)")[:, 2048 * b:2048 * b + 2048], x1[:, b, :], ACT.Square,
                                accum_out=stat[:, b:b + 1]).then_inc(x_sq, 1)
            sc.wait_ge(h_ready, 1)
            nc_s.activation(stat[:, 4:6], stat[:, 2:4], ACT.Sqrt).then_inc(x_sq, 1)
            sc.wait_ge(small_in, 16 * 8)
            for c in (c for c in range(DC) if c // 2 % 2 == 0):
                sc.wait_ge(hT_t, c // 2 + 1)
                nc_s.activation(hT[:, c, :], psum[:, c // 2, T * (c % 2):T * (c % 2) + T], ACT.Copy, scale=g_mix[:, c:c + 1]).then_inc(hT_ready, 1)
            sc.wait_ge(ssm_in, 16 * 8)
            nc_s.activation(dt[:, :], dt[:, :], ACT.Exp).then_inc(dt_ready, 1)
            sc.wait_ge(ssm_mag, 1)
            nc_s.activation(mag[:, :], mag[:, :], ACT.Exp).then_inc(ssm_mag, 1)
            sc.wait_ge(ang_ready, 1)
            nc_s.activation(sn[:, :], ang[:, :], ACT.Sin).then_inc(ssm_sin, 1)
            nc_s.activation(cs[:, :], ang[:, :], ACT.Sin, scale=0.5).then_inc(ssm_sin, 1)
            def bias_rows(h0, h1):
                for h in range(h0, h1):
                    sc.wait_ge(row_done, h + 1)
                    if h >= 2:
                        sc.wait_ge(row_dma[h % 2], 16 * (h // 2))
                    nc_s.copy(bias_row[:, h % 2, :], psum[:, 2 + h % 4, 0:384]).then_inc(row_out, 1)

            for n in range(4):
                sc.wait_ge(consumed, n + 1)
                nc_s.copy(uT[:, 2 * n:2 * n + 2, :], psum[:, n % 2, :].rearrange("p (a b) -> p a b", a=2)).then_inc(proj_out, 1)
            sc.wait_ge(consumed, 5)
            for half in range(2):
                for g in range(2):
                    link(nc_s.copy(kk[64 * half:64 * half + 64, g, :], psum[64 * g:64 * g + 64, 0, 0:T]))
            nc_s.copy(vv[:, :, :], psum[:, 0, T:2 * T].rearrange("p (a b) -> p a b", a=2)).then_inc(proj_out, 1)
            bias_rows(0, NH)

            def transposed_b(half):
                for k in range(8):
                    sc.wait_ge(bt_t, 8 * half + k + 1)
                    dst = (bt_r if k % 2 == 0 else bt_i)[:, 4 * (k // 2):4 * (k // 2) + 4, :]
                    nc_s.copy(dst, psum[:, 2 + k % 4, :].rearrange("p (a b) -> p a b", a=4)).then_inc(bt_out, 1)

            def toeplitz(half):
                sc.wait_ge(toep_zero, 1 + 3 * half)
                for k in range(4):
                    sc.wait_ge(toep_mm, 4 * half + k + 1)
                    src = psum[0:32, 6 + k % 2, :].rearrange("p (a t c) -> p a t c", a=4, t=Q)
                    for s in range(Q):
                        nc_s.copy(toep[32 * s:32 * s + 32, 4 * k:4 * k + 4, s:Q, :], src[:, :, 0:Q - s, :]).then_inc(toep_out, 1)

            def q_pieces(n0, n1):
                for n in range(n0, n1):
                    sc.wait_ge(consumed, n + 1)
                    c = 2 * (n - 5)
                    nc_s.mul(qT[:, c:c + 2, :], psum[:, n % 2, :].rearrange("p (a b) -> p a b", a=2), HD ** -0.5).then_inc(proj_out, 1)

            def softmax(b):
                sc.wait_ge(sc_ready, b + 1)
                for h in range(4):
                    nc_s.activation(scores[:, h, 0:W], scores[:, h, 0:W], ACT.Exp, bias=mxs[:, h, 0:1],
                                    accum_out=sums[:, h, 0:1]).then_inc(probs, 1)
                    nc_s.activation(scores[:, h, W:3 * W], scores[:, h, W:3 * W], ACT.Exp, bias=mxs[:, h, 1:2],
                                    accum_out=sums[:, h, 1:2]).then_inc(probs, 1)
                nc_s.activation(esink[:, :, :], esink[:, :, :], ACT.Exp).then_inc(probs, 1)
                for h in range(4):
                    sc.wait_ge(pt_t, 4 * b + h + 1)
                    nc_s.copy(scores[:, h, :], psum[:, 2 + h, 0:3 * W]).then_inc(pt_out, 1)

            def ssm_outputs(half):
                sc.wait_ge(y_mm, half + 1)
                src = psum[:, 6:8, :].rearrange("p b (c q t) -> p q (b c) t", q=4, t=NCH)
                for q in range(4):
                    for t in range(Q):
                        dst = y_store[32 * q:32 * q + 32, 4 * half:4 * half + 4, :].rearrange("p c (t s) -> p s c t", s=Q)[:, t]
                        last = nc_s.copy(dst, src[32 * t:32 * t + 32, q])
                        if not (q == 3 and t == Q - 1):
                            link(last)
                last.then_inc(y_out, 1)

            y_store = view(R2, [8, T])
            transposed_b(0)
            toeplitz(0)
            q_pieces(5, 9)
            softmax(0)
            softmax(1)
            ssm_outputs(0)
            transposed_b(1)
            toeplitz(1)
            softmax(2)
            softmax(3)
            ssm_outputs(1)

            sc.wait_ge(pv_out, 8)
            for b in range(TB):
                nc_s.activation(bias.rearrange("p h w -> p (h w)")[:, 1024 * b:1024 * b + 1024], attn[:, b, :], ACT.Square,
                                accum_out=stat[:, 8 + b:9 + b]).then_inc(attn_sq, 1)
            sc.wait_ge(attn_rs, 1)
            nc_s.activation(stat[:, 12:14], stat[:, 10:12], ACT.Sqrt).then_inc(attn_sq, 1)
            sc.wait_ge(gelu_in, 1)
            nc_s.activation(ssm[:, :, :], ssm[:, :, :], ACT.Gelu_apprx_tanh).then_inc(gelu_out, 1)
            for c in range(8):
                sc.wait_ge(glu_mm, c + 1)
                nc_s.activation(sgate[:, c, :], psum[:, c % 2, 0:T], ACT.Sigmoid, bias=b_glu[:, c:c + 1]).then_inc(glu_sig, 1)
            sc.wait_ge(attn_t, 1)
            for c in range(8):
                nc_s.activation(mixT[:, c, :], psum[:, 2 + c // 2, T * (c % 2):T * (c % 2) + T], ACT.Copy,
                                scale=g_attn[:, c:c + 1]).then_inc(attn_out, 1)
            sc.wait_ge(ssq_mm, 2)
            nc_s.activation(ssm_rs[:, :], ssm_rs[:, :], ACT.Sqrt).then_inc(ssq_rt, 1)
            sc.wait_ge(ssm_out, 8)
            sc.dma_start(wr[:, :, :], a["w_router"]).then_inc(router_in, 16)

            sc.wait_ge(x1_out, N_OUT)
            for b in range(TB):
                nc_s.activation(h2[:, b, :], x1[:, b, :], ACT.Square, accum_out=stat[:, 16 + b:17 + b]).then_inc(x1_sq, 1)
            sc.wait_ge(x1_rt, 1)
            nc_s.activation(stat[:, 20:22], stat[:, 18:20], ACT.Sqrt).then_inc(x1_sq, 1)
            for c in (c for c in range(DC) if c // 2 % 2 == 0):
                sc.wait_ge(h2_t, c // 2 + 1)
                nc_s.activation(h2T[:, c, :], psum[:, c // 2, T * (c % 2):T * (c % 2) + T], ACT.Copy, scale=g_ffn[:, c:c + 1]).then_inc(h2_out, 1)
            sc.wait_ge(eexp, 1)
            nc_s.activation(gl_exp[:, :, :], gl_exp[:, :, :], ACT.Exp).then_inc(gexp, 1)
            nc_s.activation(m_diff[:, :, :], m_diff[:, :, :], ACT.Exp).then_inc(gexp, 1)
            for c in range(0, DC, 2):
                sc.wait_ge(gather_mm, c + 1)
                nc_s.activation(h_sorted[:, c, 0:SLOTS], psum[:, c % 8, :], ACT.Copy, scale=g_ffn[:, c:c + 1]).then_inc(gather_act, 1)

            def expert(block_no):
                sc.wait_ge(consumed, RING * block_no + (NPRE + 4))
                nc_s.activation(gated_h[64:128, :], psum[0:64, 0, :], ACT.Silu).then_inc(silu_ready, 1)
                sc.wait_ge(consumed, RING * block_no + (NPRE + 6))
                nc_s.copy(y_rows[:, 0, :], psum[:, 2, :]).then_inc(y_copied, 1)

            with sc.Fori(0, NE) as e:
                expert(e)
            sc.wait_ge(routed, 1)
            nx = sc.value_load(nx_i[0:1, :], min_val=0, max_val=XMAX - 1)
            with sc.If(nx > 0):
                with sc.Fori(0, nx) as j:
                    expert(j + NE)
            sc.wait_ge(consumed, RING * nx + (NPRE + RING * NE))
            sc.dma_start(g_fin[:, :], a["g_final"].partition_broadcast(P)).then_inc(gfin_in, 16)
            for k in range(0, 16, 2):
                sc.wait_ge(yt_t, k + 1)
                nc_s.copy(y_tok[:, k // 4, 512 * (k % 4):512 * (k % 4) + 512], psum[:, k % 8, :]).then_inc(yt_act, 1)
            for b in range(TB):
                sc.wait_ge(comb_out, 4 * (b + 1))
                nc_s.activation(result[:, b, :], x1[:, b, :], ACT.Square, accum_out=stat[:, 24 + b:25 + b]).then_inc(fin_sq, 1)
                sc.wait_ge(fin_rt, b + 1)
                nc_s.activation(stat[:, 28 + b:29 + b], stat[:, 26 + b:27 + b], ACT.Sqrt).then_inc(fin_sq, 1)

        @block.vector
        def _(v):
            me = Count(dve)
            nv = nc.vector

            def link(ins):
                v.wait_ge(dve, me.inc(ins))

            TT, TS, STT = nv.tensor_tensor, nv.tensor_scalar, nv.scalar_tensor_tensor

            v.wait_ge(x_sq, 2)
            TS(stat[:, 2:4], stat[:, 0:2], 1.0 / D, EPS, ALU.mult, ALU.add).then_inc(h_ready, 1)
            v.wait_ge(x_sq, 3)
            link(nv.reciprocal(stat[:, 6:8], stat[:, 4:6]))
            for b in range(TB):
                TS(x1[:, b, :], x1[:, b, :], stat[:, 6 + b:7 + b], None, ALU.mult).then_inc(h_ready, 1)
            v.wait_ge(small_in, 16 * 8)
            for c in (c for c in range(DC) if c // 2 % 2 == 1):
                v.wait_ge(hT_t, c // 2 + 1)
                TS(hT[:, c, :], psum[:, c // 2, T * (c % 2):T * (c % 2) + T], g_mix[:, c:c + 1], None, ALU.mult).then_inc(hT_ready, 1)

            v.wait_ge(t5_in, 32)
            link(nv.memset(table[32:33, :], NEG))
            nv.tensor_copy(tab_wide[0:33, :, :], bcast(table[0:33, :], 2, P)).then_inc(wide_ready, 1)

            v.wait_ge(dt_ready, 1)
            TT(mag[:, :], lam_r[:, :], dt[:, :], ALU.mult).then_inc(ssm_mag, 1)
            link(TT(ang[:, :], lam_i[:, :], dt[:, :], ALU.mult))
            link(TS(c1[:, :], ang[:, :], 1.0 / (2 * PI), MAGIC, ALU.mult, ALU.add))
            link(TS(c1[:, :], c1[:, :], MAGIC, None, ALU.subtract))
            link(STT(ang[:, :], c1[:, :], -TWO_PI_HI, ang[:, :], ALU.mult, ALU.add))
            link(STT(ang[:, :], c1[:, :], -TWO_PI_LO, ang[:, :], ALU.mult, ALU.add))
            TS(ang[:, :], ang[:, :], 3.1415925, -3.1415925, ALU.min, ALU.max).then_inc(ang_ready, 1)
            v.wait_ge(ssm_sin, 2)
            v.wait_ge(ssm_mag, 2)
            link(TT(cs[:, :], cs[:, :], cs[:, :], ALU.mult))
            link(TS(cs[:, :], cs[:, :], -2.0, 1.0, ALU.mult, ALU.add))
            link(nv.memset(pw_r[:, 0, :], 1.0))
            link(nv.memset(pw_i[:, 0, :], 0.0))
            link(TT(pw_r[:, 1, :], mag[:, :], cs[:, :], ALU.mult))
            link(TT(pw_i[:, 1, :], mag[:, :], sn[:, :], ALU.mult))

            def cmul(or_, oi, ar, ai, br, bi, t1, t2):
                link(TT(t1, ai, bi, ALU.mult))
                link(TT(t2, ar, bi, ALU.mult))
                link(TT(oi, ai, br, ALU.mult))
                link(TT(or_, ar, br, ALU.mult))
                link(TT(or_, or_, t1, ALU.subtract))
                link(TT(oi, oi, t2, ALU.add))

            for k in range(2, Q + 1):
                cmul(pw_r[:, k, :], pw_i[:, k, :], pw_r[:, k - 1, :], pw_i[:, k - 1, :], pw_r[:, 1, :], pw_i[:, 1, :],
                     c1[:, :], c2[:, :])
            for k in range(Q):
                link(nv.tensor_copy(rev_r[:, k, :], pw_r[:, Q - k, :]))
                link(nv.tensor_copy(rev_i[:, k, :], pw_i[:, Q - k, :]))
            cmul(c3[:, :], c4[:, :], cs[:, :], sn[:, :], cs[:, :], sn[:, :], c1[:, :], c2[:, :])
            cmul(e_r[:, 0, :], e_i[:, 0, :], c3[:, :], c4[:, :], c3[:, :], c4[:, :], c1[:, :], c2[:, :])
            for k in range(1, 6):
                cmul(e_r[:, k, :], e_i[:, k, :], e_r[:, k - 1, :], e_i[:, k - 1, :], e_r[:, k - 1, :], e_i[:, k - 1, :],
                     c1[:, :], c2[:, :])
            link(TT(c1[:, :], lam_r[:, :], lam_r[:, :], ALU.mult))
            link(TT(c2[:, :], lam_i[:, :], lam_i[:, :], ALU.mult))
            link(TT(c1[:, :], c1[:, :], c2[:, :], ALU.add))
            link(nv.reciprocal(c1[:, :], c1[:, :]))
            link(TS(c2[:, :], pw_r[:, 1, :], -1.0, None, ALU.add))
            link(TT(rot[:, :], c2[:, :], lam_r[:, :], ALU.mult))
            link(TT(c3[:, :], pw_i[:, 1, :], lam_i[:, :], ALU.mult))
            link(TT(rot[:, :], rot[:, :], c3[:, :], ALU.add))
            link(TT(rot[:, :], rot[:, :], c1[:, :], ALU.mult))
            link(TT(sn[:, :], pw_i[:, 1, :], lam_r[:, :], ALU.mult))
            link(TT(c3[:, :], c2[:, :], lam_i[:, :], ALU.mult))
            link(TT(sn[:, :], sn[:, :], c3[:, :], ALU.subtract))
            link(TT(sn[:, :], sn[:, :], c1[:, :], ALU.mult))
            link(TT(mag[:, :], mag[:, :], mag[:, :], ALU.mult))
            link(TT(mag[:, :], mag[:, :], mag[:, :], ALU.mult))

            v.wait_ge(const_ready, 11)
            for g in range(2):
                ps, cols = slice(64 * g, 64 * g + 64), slice(SC * g, SC * g + SC)
                fr, fi = bcast(rot[ps, :], 2, SC), bcast(sn[ps, :], 2, SC)
                tmp = full_tmp[ps]
                link(TT(tmp, braw_i[ps], fi, ALU.mult))
                link(TT(bbar_r[ps, :, cols], braw_r[ps], fr, ALU.mult))
                link(TT(bbar_r[ps, :, cols], bbar_r[ps, :, cols], tmp, ALU.subtract))
                link(TT(tmp, braw_r[ps], fi, ALU.mult))
                link(TT(bbar_i[ps, :, cols], braw_i[ps], fr, ALU.mult))
                link(TT(bbar_i[ps, :, cols], bbar_i[ps, :, cols], tmp, ALU.add))
            link(nv.memset(cp_r[:], 0.0))

            def matrices(half):
                js = slice(HP * half, HP * half + HP)
                for g in range(2):
                    ps, cols = slice(64 * g, 64 * g + 64), slice(SC * g, SC * g + SC)

                    def steps(m):
                        return bcast(m, 2, Q)

                    def chans(m):
                        return bcast(m[ps, :, js].rearrange("p k j -> p j k"), 3, SC)

                    br, bi = steps(bbar_r[ps, js, cols]), steps(bbar_i[ps, js, cols])
                    tmp, o_r, o_i = cp_i[ps, :, :, cols], bp_r[ps, :, :, cols], bp_i[ps, :, :, cols]
                    link(TT(tmp, bi, chans(rev_i), ALU.mult))
                    link(TT(o_r, br, chans(rev_r), ALU.mult))
                    link(TT(o_r, o_r, tmp, ALU.subtract))
                    link(TT(tmp, br, chans(rev_i), ALU.mult))
                    link(TT(o_i, bi, chans(rev_r), ALU.mult))
                    last = TT(o_i, o_i, tmp, ALU.add)
                    last.then_inc(bp_ready, 1)
                for g in range(2):
                    ps, cols = slice(64 * g, 64 * g + 64), slice(SC * g, SC * g + SC)
                    cr, ci = bcast(craw_r[ps, js], 2, Q), bcast(craw_i[ps, js], 2, Q)
                    pr = bcast(pw_r[ps, 0:Q, js].rearrange("p k j -> p j k"), 3, SC)
                    pi = bcast(pw_i[ps, 0:Q, js].rearrange("p k j -> p j k"), 3, SC)
                    tmp, o_r, o_i = toep[ps, :, :, cols], cp_r[ps, :, :, cols], cp_i[ps, :, :, cols]
                    link(TT(tmp, ci, pi, ALU.mult))
                    link(TT(o_r, cr, pr, ALU.mult))
                    link(TT(o_r, o_r, tmp, ALU.subtract))
                    link(TT(tmp, ci, pr, ALU.mult))
                    link(TT(o_i, cr, pi, ALU.mult))
                    if g == 0:
                        link(STT(o_i, o_i, -1.0, tmp, ALU.mult, ALU.subtract))
                    else:
                        STT(o_i, o_i, -1.0, tmp, ALU.mult, ALU.subtract).then_inc(cp_ready, 1)

            def turn_tables(half):
                js = slice(HP * half, HP * half + HP)
                v.wait_ge(bt_t, 8 * (half + 1))
                link(nv.memset(cos_t[:, :, 0:1], 1.0))
                link(nv.memset(sin_t[:, :, 0:1], 0.0))
                for k in range(6):
                    n = 1 << k
                    er, ei = bcast(e_r[:, k, js], 2, n), bcast(e_i[:, k, js], 2, n)
                    c0, s0 = cos_t[:, :, 0:n], sin_t[:, :, 0:n]
                    c1_, s1_ = cos_t[:, :, n:2 * n], sin_t[:, :, n:2 * n]
                    link(TT(tmp_a[:, :, 0:n], s0, ei, ALU.mult))
                    link(TT(tmp_b[:, :, 0:n], c0, ei, ALU.mult))
                    link(TT(c1_, c0, er, ALU.mult))
                    link(TT(s1_, s0, er, ALU.mult))
                    link(TT(c1_, c1_, tmp_a[:, :, 0:n], ALU.subtract))
                    link(TT(s1_, s1_, tmp_b[:, :, 0:n], ALU.add))

            def scan(half):
                js = slice(HP * half, HP * half + HP)
                link(nv.memset(z_r[:, :, 0:1], 0.0))
                link(nv.memset(z_i[:, :, 0:1], 0.0))
                v.wait_ge(v_mm, half + 1)
                vr = psum[:, 2:4, :].rearrange("p b (j c) -> p (b j) c", c=NCH)[:, :, 0:NCH - 1]
                vi = psum[:, 4:6, :].rearrange("p b (j c) -> p (b j) c", c=NCH)[:, :, 0:NCH - 1]
                co, si = cos_t[:, :, 1:NCH], sin_t[:, :, 1:NCH]
                zr, zi, ta, tb = (m[:, :, 1:NCH] for m in (z_r, z_i, tmp_a, tmp_b))
                link(TT(zr, vr, co, ALU.mult))
                link(TT(ta, vi, si, ALU.mult))
                link(TT(zi, vi, co, ALU.mult))
                TT(tb, vr, si, ALU.mult).then_inc(v_read, 1)
                v.wait_ge(v_read, half + 1)
                link(TT(zr, zr, ta, ALU.add))
                link(TT(zi, zi, tb, ALU.subtract))
                link(nv.memset(decay[:, :, 0:1], 0.0))
                link(nv.tensor_copy(decay[:, :, 1:NCH], bcast(mag[:, js], 2, NCH - 1)))
                flat = lambda m: m.rearrange("p j c -> p (j c)")
                link(nv.tensor_tensor_scan(flat(tmp_a), flat(decay), flat(z_r), 0.0, ALU.mult, ALU.add))
                link(nv.tensor_tensor_scan(flat(tmp_b), flat(decay), flat(z_i), 0.0, ALU.mult, ALU.add))
                link(TT(z_r, tmp_a, cos_t, ALU.mult))
                link(TT(decay, tmp_b, sin_t, ALU.mult))
                link(TT(z_r, z_r, decay, ALU.subtract))
                link(TT(z_i, tmp_a, sin_t, ALU.mult))
                link(TT(decay, tmp_b, cos_t, ALU.mult))
                TT(z_i, z_i, decay, ALU.add).then_inc(w_ready, 1)

            def softmax(b):
                v.wait_ge(sc_mm, b + 1)
                hs = slice(4 * b, 4 * b + 4)
                if b == 0:
                    v.wait_ge(bias_in, 64)
                if b > 0:
                    v.wait_ge(pv_mm, b)
                sp_ = psum[:, 2:6, :]
                link(TT(scores[:, :, 0:W], sp_[:, :, 0:W], bias[:, hs, W:2 * W], ALU.add))
                link(TT(scores[:, :, W:2 * W], sp_[:, :, W:2 * W], bias[:, hs, W:2 * W], ALU.add))
                link(TT(scores[:, :, 2 * W:3 * W], sp_[:, :, 2 * W:3 * W], bias[:, hs, 0:W], ALU.add))
                link(nv.tensor_reduce(mxs[:, :, 0], scores[:, :, 0:W], AX, ALU.max))
                link(nv.tensor_reduce(mxs[:, :, 1], scores[:, :, W:3 * W], AX, ALU.max))
                sk = bcast(sinks[:, hs], 2, 2)
                link(TT(mxs[:, :, :], mxs[:, :, :], sk, ALU.max))
                link(TT(esink[:, :, :], sk, mxs[:, :, :], ALU.subtract))
                TS(mxs[:, :, :], mxs[:, :, :], -1.0, None, ALU.mult).then_inc(sc_ready, 1)
                v.wait_ge(probs, 9 * (b + 1))
                link(TT(sums[:, :, :], sums[:, :, :], esink[:, :, :], ALU.add))
                link(nv.reciprocal(recs[:, :, :], sums[:, :, :]))
                v.wait_ge(pv_mm, b + 1)
                o = psum[:, 6, :].rearrange("p (h k d) -> p h k d", h=4, k=2)
                for k in range(2):
                    dst = attn[:, k, :].rearrange("p (h d) -> p h d", d=HD)[:, hs, :]
                    TT(dst, o[:, :, k, :], bcast(recs[:, :, k], 2, HD), ALU.mult).then_inc(pv_out, 1)

            matrices(0)
            turn_tables(0)
            scan(0)
            softmax(0)
            softmax(1)
            v.wait_ge(toep_zero, 3)
            v.wait_ge(y_mm, 1)
            matrices(1)
            turn_tables(1)
            scan(1)
            softmax(2)
            softmax(3)

            v.wait_ge(attn_sq, 2)
            TS(stat[:, 10:12], stat[:, 8:10], 1.0 / (NH * HD), EPS, ALU.mult, ALU.add).then_inc(attn_rs, 1)
            v.wait_ge(attn_sq, 3)
            link(nv.reciprocal(stat[:, 14:16], stat[:, 12:14]))
            v.wait_ge(pv_out, 8)
            for b in range(TB):
                TS(attn[:, b, :], attn[:, b, :], stat[:, 14 + b:15 + b], None, ALU.mult).then_inc(attn_ready, 1)

            y_store = view(R2, [8, T])
            v.wait_ge(y_out, 2)
            for c in range(8):
                ins = STT(ssm[:, c, :], uT[:, c, :], d_skip[:, c:c + 1], y_store[:, c, :], ALU.mult, ALU.add)
                if c < 7:
                    link(ins)
                else:
                    ins.then_inc(gelu_in, 1)
            v.wait_ge(gelu_in, 1)
            v.wait_ge(glu_mm, 8)
            for c in range(8):
                v.wait_ge(glu_sig, c + 1)
                link(TT(ssm[:, c, :], ssm[:, c, :], sgate[:, c, :], ALU.mult))
                TT(ysq[:, c, :], ssm[:, c, :], ssm[:, c, :], ALU.mult).then_inc(ssq_ready, 1)
            v.wait_ge(ssq_mm, 1)
            TS(ssm_rs[:, :], psum[:, 6, 0:T], 1.0 / (G * SC), EPS, ALU.mult, ALU.add).then_inc(ssq_mm, 1)
            v.wait_ge(ssq_rt, 1)
            link(nv.reciprocal(ssm_rs[:, :], ssm_rs[:, :]))
            for c in range(8):
                STT(mixT[:, 8 + c, :], ssm[:, c, :], g_ssm[:, c:c + 1], ssm_rs[:, :], ALU.mult, ALU.mult).then_inc(ssm_out, 1)

            v.wait_ge(x_again, 32)
            for k in range(N_OUT):
                v.wait_ge(consumed, N_WIN + N_GLU + k + 1)
                xs = x1[:, :, 256 * k:256 * (k + 1)]
                TT(xs, psum[:, k % 2, :].rearrange("p (b n) -> p b n", b=TB), xs, ALU.add).then_inc(x1_out, 1)
            v.wait_ge(x1_sq, 2)
            TS(stat[:, 18:20], stat[:, 16:18], 1.0 / D, EPS, ALU.mult, ALU.add).then_inc(x1_rt, 1)
            v.wait_ge(x1_sq, 3)
            link(nv.reciprocal(stat[:, 22:24], stat[:, 20:22]))
            for b in range(TB):
                TS(h2[:, b, :], x1[:, b, :], stat[:, 22 + b:23 + b], None, ALU.mult).then_inc(h2_ready, 1)
            for c in (c for c in range(DC) if c // 2 % 2 == 1):
                v.wait_ge(h2_t, c // 2 + 1)
                TS(h2T[:, c, :], psum[:, c // 2, T * (c % 2):T * (c % 2) + T], g_ffn[:, c:c + 1], None, ALU.mult).then_inc(h2_out, 1)

            v.wait_ge(router_mm, 1)
            link(TT(lg[:, :, :], psum[:, 0, 0:TB * 36].rearrange("p (b n) -> p b n", b=TB), bcast(b_rt[:, :], 1, TB), ALU.add))

            def first_max(dst, src, m, tmp, n):
                link(nv.tensor_reduce(m, src, AX, ALU.max))
                link(TT(tmp, src, bcast(m, 2, n), ALU.is_equal))
                r = bcast(rev_iota[:, 0:n], 1, TB)
                link(TT(tmp, tmp, r, ALU.mult))
                link(nv.tensor_reduce(slot_t[:, :, 0], tmp, AX, ALU.max))
                link(TT(dst, r, bcast(slot_t[:, :, 0], 2, n), ALU.is_equal))

            first_max(g_one[:, :, :], lg[:, :, 0:NG], g_max[:, :, 0], t_a[:, :, :], NG)
            link(TT(gl_exp[:, :, :], lg[:, :, 0:NG], bcast(g_max[:, :, 0], 2, NG), ALU.subtract))
            link(TT(prod4.rearrange("p b e g -> p b g e"), lg[:, :, NG:].rearrange("p b (g e) -> p b g e", g=NG),
                    bcast(g_one[:, :, :], 3, EG), ALU.mult))
            link(nv.tensor_reduce(e_sel[:, :, :], prod4[:, :, :, :], AX, ALU.add))
            first_max(k_one[0][:, :, :], e_sel[:, :, :], m_top[:, :, 0], t_b[:, :, :], EG)
            link(STT(e_sel[:, :, :], k_one[0][:, :, :], NEG, e_sel[:, :, :], ALU.mult, ALU.add))
            first_max(k_one[1][:, :, :], e_sel[:, :, :], m_top[:, :, 1], t_b[:, :, :], EG)
            TT(m_diff[:, :, 0], m_top[:, :, 1], m_top[:, :, 0], ALU.subtract).then_inc(eexp, 1)
            for k in range(2):
                link(TT(one32[k].rearrange("p b (g e) -> p b g e", g=NG), bcast(g_one[:, :, :], 3, EG),
                        bcast(k_one[k][:, :, :], 2, NG), ALU.mult))
            TT(both[:, :, :], one32[0][:, :, :], one32[1][:, :, :], ALU.add).then_inc(onehot_ready, 1)
            v.wait_ge(gexp, 2)
            link(nv.tensor_reduce(g_p[:, :, 0], gl_exp[:, :, :], AX, ALU.add))
            link(nv.reciprocal(g_p[:, :, :], g_p[:, :, :]))
            link(TS(w_top[:, :, 0], m_diff[:, :, 0], 1.0, None, ALU.add))
            link(nv.reciprocal(w_top[:, :, 0], w_top[:, :, 0]))
            link(TT(w_top[:, :, 0], w_top[:, :, 0], g_p[:, :, 0], ALU.mult))
            link(TT(w_top[:, :, 1], w_top[:, :, 0], m_diff[:, :, 0], ALU.mult))
            v.wait_ge(count_mm, 1)
            v.wait_ge(logit, 3)
            link(nv.tensor_copy(counts[:, :], psum[:, 1, 0:NE]))
            link(nv.tensor_tensor_scan(base_end[:, :], ones[:, 0:NE], counts[:, :], 0.0, ALU.mult, ALU.add))
            link(TT(nxt[:, :], base_end[:, :], counts[:, :], ALU.subtract))
            link(nv.tensor_copy(base_i[:, :], nxt[:, :]))
            link(TT(slot_e[:, :, :], psum[:, 1, 64:64 + TB * NE].rearrange("p (b e) -> p b e", b=TB), bcast(nxt[:, :], 1, TB), ALU.add))
            for k in range(2):
                link(TT(one32[k][:, :, :], one32[k][:, :, :], slot_e[:, :, :], ALU.mult))
                link(nv.tensor_reduce(slot_t[:, :, k], one32[k][:, :, :], AX, ALU.add))
            for b in range(TB):
                link(TS(sel[:, b, :], iota_s[:, :], slot_t[:, b, 0:1], None, ALU.is_equal))
                link(TS(selw[:, b, :], iota_s[:, :], slot_t[:, b, 1:2], None, ALU.is_equal))
                sw = y_tmp[:, :]
                link(TS(sw, sel[:, b, :], w_top[:, b, 0:1], None, ALU.mult))
                link(TT(sel[:, b, :], sel[:, b, :], selw[:, b, :], ALU.add))
                STT(selw[:, b, :], selw[:, b, :], w_top[:, b, 1:2], sw, ALU.mult, ALU.add).then_inc(sel_ready, 1)
            b0 = big[:, 0, :]
            link(TS(xcum[:, :], counts[:, :], float(CAP), None, ALU.is_gt))
            for m in (2, 3):
                link(TS(b0, counts[:, :], float(m * CAP), None, ALU.is_gt))
                link(TT(xcum[:, :], xcum[:, :], b0, ALU.add))
            ends = big[:, 1, :]
            link(nv.tensor_tensor_scan(ends, ones[:, 0:NE], xcum[:, :], 0.0, ALU.mult, ALU.add))
            link(nv.tensor_copy(nx_i[:, :], ends[:, NE - 1:NE]))
            
            link(nv.tensor_copy(iota_e2[:, :], ends))
            link(TT(xcum[:, :], ends, xcum[:, :], ALU.subtract))
            jrow = bcast(iota_e[:, 0:XMAX], 2, NE)
            link(TT(big[:, :, :], bcast(xcum[:, :], 1, XMAX), jrow, ALU.is_le))
            link(TT(big2[:, :, :], bcast(iota_e2[:, :], 1, XMAX), jrow, ALU.is_gt))
            link(TT(big[:, :, :], big[:, :, :], big2[:, :, :], ALU.mult))
            link(TT(big2[:, :, :], big[:, :, :], bcast(iota_e[:, :], 1, XMAX), ALU.mult))
            link(nv.tensor_reduce(rowf[:, 0, :], big2[:, :, :], AX, ALU.add))
            link(nv.tensor_copy(xexp_i[:, :], rowf[:, 0, :]))
            link(TT(big2[:, :, :], jrow, bcast(xcum[:, :], 1, XMAX), ALU.subtract))
            link(TS(big2[:, :, :], big2[:, :, :], float(CAP), float(CAP), ALU.mult, ALU.add))
            link(TT(big2[:, :, :], big2[:, :, :], big[:, :, :], ALU.mult))
            link(nv.tensor_reduce(rowf[:, 1, :], big2[:, :, :], AX, ALU.add))
            link(TT(big2[:, :, :], big[:, :, :], bcast(counts[:, :], 1, XMAX), ALU.mult))
            link(nv.tensor_reduce(rowf[:, 2, :], big2[:, :, :], AX, ALU.add))
            link(TT(xlim[:, :], rowf[:, 2, :], rowf[:, 1, :], ALU.subtract))
            link(TT(big2[:, :, :], big[:, :, :], bcast(nxt[:, :], 1, XMAX), ALU.mult))
            link(nv.tensor_reduce(rowf[:, 2, :], big2[:, :, :], AX, ALU.add))
            link(TT(rowf[:, 2, :], rowf[:, 2, :], rowf[:, 1, :], ALU.add))
            link(nv.tensor_copy(xbase_i[:, :], rowf[:, 2, :]))
            v.wait_ge(wrow_mm, 1)
            link(nv.tensor_copy(wrow[:, 0:SLOTS], psum[:, 2, :]))
            v.wait_ge(selT_t, 1)
            nv.tensor_copy(selT[:, :, :], psum[:, 3:5, :].rearrange("p b (s t) -> p (b s) t", s=2)).then_inc(routed, 1)
            for c in range(1, DC, 2):
                v.wait_ge(gather_mm, c + 1)
                TS(h_sorted[:, c, 0:SLOTS], psum[:, c % 8, :], g_ffn[:, c:c + 1], None, ALU.mult).then_inc(gather_dve, 1)
            v.wait_ge(gather_mm, DC)
            v.wait_ge(y_zero, 3)
            v.wait_ge(routed, 1)

            def expert(block_no, base, limit):
                STT(wmask[:, :], iota_c[:, :], limit, wrow[:, bass.ds(base, CAP)], ALU.is_lt, ALU.mult).then_inc(mask_ready, 1)
                v.wait_ge(silu_ready, block_no + 1)
                TT(gated_h[64:128, :], psum[64:128, 0, :], gated_h[64:128, :], ALU.mult).then_inc(gated, 1)
                v.wait_ge(hidT_mm, block_no + 1)
                v.wait_ge(mask_ready, block_no + 1)
                TT(hid[:, :, :], psum[:, 1, :].rearrange("p (m t) -> p m t", m=4)[:, :, P - CAP:P], bcast(wmask[:, :], 1, 4),
                   ALU.mult).then_inc(hid_ready, 1)
                v.wait_ge(consumed, RING * block_no + (NPRE + 6))
                nv.tensor_copy(y_rows[:, 1, :], psum[:, 3, :]).then_inc(y_copied2, 1)
                for k in range(2):
                    v.wait_ge(yT_mm, 2 * block_no + (k + 1))
                    ys = y_sorted[:, 8 * k:8 * k + 8, bass.ds(base, CAP)].rearrange("p (h i) t -> p i h t", h=2)
                    TT(ys, psum[:, 4 + k, :].rearrange("p (i h t) -> p i h t", i=4, h=2), ys, ALU.add).then_inc(y_added, 1)

            with v.Fori(0, NE) as e:
                base = v.value_load(base_i[0:1, bass.ds(e, 1)], min_val=0, max_val=SLOTS)
                expert(e, base, counts[:, bass.ds(e, 1)])
            nx = v.value_load(nx_i[0:1, :], min_val=0, max_val=XMAX - 1)
            with v.If(nx > 0):
                with v.Fori(0, nx) as j:
                    base = v.value_load(xbase_i[0:1, bass.ds(j, 1)], min_val=0, max_val=SLOTS)
                    expert(j + NE, base, xlim[:, bass.ds(j, 1)])

            for k in range(1, 16, 2):
                v.wait_ge(yt_t, k + 1)
                nv.tensor_copy(y_tok[:, k // 4, 512 * (k % 4):512 * (k % 4) + 512], psum[:, k % 8, :]).then_inc(yt_dve, 1)
            for b in range(TB):
                for n in range(4):
                    v.wait_ge(comb_mm, 4 * b + n + 1)
                    xs = x1[:, b, 512 * n:512 * n + 512]
                    TT(xs, psum[:, 4 * b + n, :], xs, ALU.add).then_inc(comb_out, 1)
            for b in range(TB):
                v.wait_ge(fin_sq, 2 * b + 1)
                TS(stat[:, 26 + b:27 + b], stat[:, 24 + b:25 + b], 1.0 / D, EPS, ALU.mult, ALU.add).then_inc(fin_rt, 1)
                v.wait_ge(fin_sq, 2 * b + 2)
                link(nv.reciprocal(stat[:, 30 + b:31 + b], stat[:, 28 + b:29 + b]))
                if b == 0:
                    v.wait_ge(gfin_in, 16)
                STT(result[:, b, :], x1[:, b, :], stat[:, 30 + b:31 + b], g_fin[:, :], ALU.mult, ALU.mult).then_inc(fin_ready, 1)

        @block.tensor
        def _(pe):
            mm, tr = nc.tensor.matmul, nc.tensor.transpose

            pe.wait_ge(const_ready, 2)
            pe.wait_ge(h_ready, 3)
            hv = x1.rearrange("p b (q c) -> p b c q", c=DC)
            for c in range(DC):
                for b in range(TB):
                    last = tr(psum[:, c // 2, T * (c % 2) + P * b:T * (c % 2) + P * b + P], hv[:, b, c, :], ident[:, :])
                if c % 2:
                    last.then_inc(hT_t, 1)

            piece = [0]

            def take():
                n = piece[0]
                piece[0] += 1
                two = 2 if n >= N_WIN + N_GLU else 1
                k = n % PRE
                before = sum(2 if m >= N_WIN + N_GLU else 1 for m in range(n) if m % PRE == k)
                pe.wait_ge(landed[k], 16 * (before + two))
                return ring[k]

            def project(n):
                w = take().rearrange("p (c n) -> p c n", c=DC)
                if n >= 2:
                    pe.wait_ge(proj_out, n - 1)
                for m in range(2):
                    if n == 4 and m == 1:
                        break
                    for k in range(DC):
                        last = mm(psum[:, n % 2, T * m:T * m + T], w[:, k, P * m:P * m + P], hT[:, k, :],
                                  start=(k == 0), stop=(k == DC - 1))
                if n == 4:
                    for b in range(TB):
                        for k in range(DC):
                            last = mm(psum[:, 0, T + P * b:T + P * b + P], hT[:, k, P * b:P * b + P], w[:, k, P:2 * P],
                                      start=(k == 0), stop=(k == DC - 1))
                last.then_inc(consumed, 1)

            pe.wait_ge(hT_ready, DC)
            for n in range(5):
                project(n)
            pe.wait_ge(wide_ready, 1)
            for h in range(NH):
                if h >= 4:
                    pe.wait_ge(row_out, h - 3)
                mm(psum[:, 2 + h % 4, 0:384], tab_wide[0:33, h, :], onehot[0:33, :], start=True, stop=True).then_inc(row_done, 1)

            def ssm_prepare(half):
                pe.wait_ge(bp_ready, 2 * half + 2)
                for k in range(8):
                    if k >= 4:
                        pe.wait_ge(bt_out, 8 * half + k - 3)
                    elif half == 0:
                        pe.wait_ge(row_out, 13 + k)
                    elif k == 0:
                        pe.wait_ge(pt_out, 8)
                    src = bp_r if k % 2 == 0 else bp_i
                    for i in range(4):
                        last = tr(psum[:, 2 + k % 4, P * i:P * i + P],
                                  src[:, 4 * (k // 2) + i, :, :].rearrange("p s c -> p (s c)"), ident[:, :])
                    last.then_inc(bt_t, 1)
                pe.wait_ge(cp_ready, half + 1)
                for k in range(4):
                    if k >= 2:
                        pe.wait_ge(toep_out, 16 * half + 4 * (k - 1))
                    elif half == 1 and k == 0:
                        pe.wait_ge(y_out, 1)
                    for i in range(4):
                        j = 4 * k + i
                        o = psum[0:32, 6 + k % 2, P * i:P * i + P]
                        mm(o, bbar_r[:, HP * half + j, :], cp_r[:, j].rearrange("p s c -> p (s c)"), start=True, stop=False)
                        last = mm(o, bbar_i[:, HP * half + j, :], cp_i[:, j].rearrange("p s c -> p (s c)"), start=False, stop=True)
                    last.then_inc(toep_mm, 1)

            def ssm_inject(half):
                pe.wait_ge(u4_ready, 16)
                pe.wait_ge(bt_out, 8 * half + 8)
                for part, bt in enumerate((bt_r, bt_i)):
                    for j in range(HP):
                        last = mm(psum[:, 2 + 2 * part + j // 8, NCH * (j % 8):NCH * (j % 8) + NCH], bt[:, j, :],
                                  u4[:, HP * half + j, :], start=True, stop=True)
                last.then_inc(v_mm, 1)

            def ssm_output(half):
                pe.wait_ge(w_ready, half + 1)
                pe.wait_ge(toep_out, 16 * (half + 1))
                if half == 0:
                    pe.wait_ge(pv_out, 4)
                else:
                    pe.wait_ge(pv_out, 8)
                for j in range(HP):
                    o = psum[:, 6 + j // 8, NCH * (j % 8):NCH * (j % 8) + NCH]
                    mm(o, cp_r[:, j].rearrange("p s c -> p (s c)"), z_r[:, j, :], start=True, stop=False)
                    mm(o, cp_i[:, j].rearrange("p s c -> p (s c)"), z_i[:, j, :], start=False, stop=False)
                    last = mm(o, toep[:, j].rearrange("p s c -> p (s c)"), u4[:, HP * half + j, :], start=False, stop=True)
                last.then_inc(y_mm, 1)

            def attention(b):
                if b == 0:
                    pe.wait_ge(v_read, 1)
                if b == 2:
                    pe.wait_ge(v_read, 2)
                if b:
                    pe.wait_ge(pt_out, 4 * b)
                for h in range(4):
                    hh = 4 * b + h
                    ps = slice(64 * (hh % 2), 64 * (hh % 2) + 64)
                    kv = hh // 8
                    for i, (q0, k0) in enumerate(((0, 0), (W, W), (W, 0))):
                        last = mm(psum[:, 2 + h, W * i:W * i + W], qT[ps, hh // 2, q0:q0 + W], kk[ps, kv, k0:k0 + W],
                                  start=True, stop=True)
                last.then_inc(sc_mm, 1)
                for h in range(4):
                    pe.wait_ge(probs, 9 * b + 2 * h + 2)
                    for i in range(3):
                        last = tr(psum[:, 2 + h, W * i:W * i + W], scores[:, h, W * i:W * i + W], ident[:, :])
                    last.then_inc(pt_t, 1)
                if b == 0:
                    pe.wait_ge(toep_out, 16)
                elif b == 2:
                    pe.wait_ge(toep_out, 32)
                    pe.wait_ge(y_out, 1)
                if b:
                    pe.wait_ge(pv_out, 2 * b)
                for h in range(4):
                    hh = 4 * b + h
                    kv = slice(HD * (hh // 8), HD * (hh // 8) + HD)
                    pe.wait_ge(pt_out, 4 * b + h + 1)
                    o = P * h
                    mm(psum[:, 6, o:o + HD], scores[:, h, 0:W], vv[:, 0, kv], start=True, stop=True)
                    mm(psum[:, 6, o + HD:o + 2 * HD], scores[:, h, 2 * W:3 * W], vv[:, 0, kv], start=True, stop=False)
                    last = mm(psum[:, 6, o + HD:o + 2 * HD], scores[:, h, W:2 * W], vv[:, 1, kv], start=False, stop=True)
                last.then_inc(pv_mm, 1)

            ssm_prepare(0)
            project(5)
            project(6)
            ssm_inject(0)
            project(7)
            project(8)
            pe.wait_ge(proj_out, 9)
            attention(0)
            attention(1)
            ssm_output(0)
            ssm_prepare(1)
            ssm_inject(1)
            attention(2)
            attention(3)
            ssm_output(1)
            pe.wait_ge(attn_ready, 2)
            pe.wait_ge(pt_out, 16)
            av = attn.rearrange("p b (q c) -> p b c q", c=8)
            for c in range(8):
                for b in range(TB):
                    last = tr(psum[:, 2 + c // 2, T * (c % 2) + P * b:T * (c % 2) + P * b + P], av[:, b, c, :], ident[:, :])
            last.then_inc(attn_t, 1)
            pe.wait_ge(gelu_out, 1)
            for n in range(N_GLU):
                w = take().rearrange("p (c n) -> p c n", c=8)
                for m in range(4):
                    c = 4 * n + m
                    if c >= 2:
                        pe.wait_ge(glu_sig, c - 1)
                    for k in range(8):
                        last = mm(psum[:, c % 2, 0:T], w[:, k, P * m:P * m + P], ssm[:, k, :], start=(k == 0), stop=(k == 7))
                    last.then_inc(glu_mm, 1)
                pe.wait_ge(glu_mm, 4 * n + 4)
                pe.nop().then_inc(consumed, 1)
            pe.wait_ge(y_out, 2)
            for c in range(8):
                pe.wait_ge(ssq_ready, c + 1)
                last = mm(psum[:, 6, 0:T], ones[:, :], ysq[:, c, :], start=(c == 0), stop=(c == 7))
            last.then_inc(ssq_mm, 1)
            pe.wait_ge(attn_out, 8)
            pe.wait_ge(ssm_out, 8)
            pe.wait_ge(glu_sig, 8)
            for n in range(N_OUT):
                w = take().rearrange("p (c n) -> p c n", c=DC)
                if n >= 2:
                    pe.wait_ge(x1_out, n - 1)
                for b in range(TB):
                    for k in range(DC):
                        last = mm(psum[:, n % 2, 256 * b:256 * b + 256], mixT[:, k, P * b:P * b + P], w[:, k, :],
                                  start=(k == 0), stop=(k == DC - 1))
                last.then_inc(consumed, 1)

            pe.wait_ge(h2_ready, 2)
            hv2 = h2.rearrange("p b (q c) -> p b c q", c=DC)
            for c in range(DC):
                for b in range(TB):
                    last = tr(psum[:, c // 2, T * (c % 2) + P * b:T * (c % 2) + P * b + P], hv2[:, b, c, :], ident[:, :])
                if c % 2:
                    last.then_inc(h2_t, 1)
            pe.wait_ge(h2_out, DC)
            pe.wait_ge(router_in, 16)
            for b in range(TB):
                for k in range(DC):
                    last = mm(psum[:, 0, 36 * b:36 * b + 36], h2T[:, k, P * b:P * b + P], wr[:, k, :],
                              start=(k == 0), stop=(k == DC - 1))
            last.then_inc(router_mm, 1)
            pe.wait_ge(onehot_ready, 1)
            pe.wait_ge(const_ready, 12)
            mm(psum[:, 1, 0:NE], ones[:, :], both[:, 0, :], start=True, stop=False)
            mm(psum[:, 1, 0:NE], ones[:, :], both[:, 1, :], start=False, stop=True)
            mm(psum[:, 1, 64:64 + NE], tri[:, :], both[:, 0, :], start=True, stop=True)
            mm(psum[:, 1, 96:96 + NE], tri[:, :], both[:, 1, :], start=True, stop=False)
            mm(psum[:, 1, 96:96 + NE], ones[:, :], both[:, 0, :], start=False, stop=True).then_inc(count_mm, 1)
            pe.wait_ge(sel_ready, 2)
            mm(psum[:, 2, :], ones[:, :], selw[:, 0, :], start=True, stop=False)
            mm(psum[:, 2, :], ones[:, :], selw[:, 1, :], start=False, stop=True).then_inc(wrow_mm, 1)
            for s in range(4):
                for b in range(TB):
                    last = tr(psum[:, 3 + s // 2, T * (s % 2) + P * b:T * (s % 2) + P * b + P], sel[:, b, P * s:P * s + P], ident[:, :])
            last.then_inc(selT_t, 1)
            pe.wait_ge(routed, 1)
            for c in range(DC):
                if c >= 8:
                    pe.wait_ge(gather_act if c % 2 == 0 else gather_dve, (c - 8) // 2 + 1)
                for b in range(TB):
                    last = mm(psum[:, c % 8, :], hv2[:, b, c, :], sel[:, b, :], start=(b == 0), stop=(b == TB - 1))
                last.then_inc(gather_mm, 1)
            pe.wait_ge(gather_act, DC // 2)
            pe.wait_ge(gather_dve, DC // 2)
            pe.wait_ge(y_zero, 1)

            def expert(block_no, base):
                def weights(k):
                    pre = 16 * sum(2 if m >= N_WIN + N_GLU else 1 for m in range(NPRE) if m % PRE == ring_of(k)) if ring_of(k) < PRE else 0
                    pe.wait_ge(landed[ring_of(k)], 16 * block_no + (pre + 16))
                    return ring[ring_of(k)]

                pe.wait_ge(hs_ready, block_no + 1)
                for half, (kg, ku) in enumerate(((GATE_A, UP_A), (GATE_B, UP_B))):
                    wg = weights(kg).rearrange("p (c n) -> p c n", c=8)
                    wu = weights(ku).rearrange("p (c n) -> p c n", c=8)
                    for c in range(8):
                        st, sp_ = half == 0 and c == 0, half == 1 and c == 7
                        g = mm(psum[0:64, 0, :], hs[:, 8 * half + c, :], wg[:, c, :], start=st, stop=sp_)
                        u = mm(psum[64:128, 0, :], hs[:, 8 * half + c, :], wu[:, c, :], start=st, stop=sp_)
                    g.then_inc(consumed, 1)
                    u.then_inc(consumed, 1)
                pe.wait_ge(gated, block_no + 1)
                gv = gated_h[:, :].rearrange("p (q c) -> p c q", c=4)
                for c in range(4):
                    last = tr(psum[:, 1, P * c:P * c + P], gv[:, c, :], ident[:, :])
                last.then_inc(hidT_mm, 1)
                pe.wait_ge(hid_ready, block_no + 1)
                for half, k in enumerate((DOWN_A, DOWN_B)):
                    w = weights(k).rearrange("p (c n) -> p c n", c=2)
                    for c in range(2):
                        for n in range(4):
                            last = mm(psum[64 * (n % 2):64 * (n % 2) + 64, 2 + n // 2, :], hid[:, 2 * half + c, :],
                                      w[:, c, 512 * n:512 * n + 512], start=(half == 0 and c == 0), stop=(half == 1 and c == 1))
                    last.then_inc(consumed, 1)
                pe.wait_ge(y_copied, block_no + 1)
                pe.wait_ge(y_copied2, block_no + 1)
                for k in range(2):
                    for i in range(4):
                        last = tr(psum[:, 4 + k, P * i:P * i + P], y_rows[:, k, P * i:P * i + P], ident[:, :])
                    last.then_inc(yT_mm, 1)

            with pe.Fori(0, NE) as e:
                base = pe.value_load(base_i[0:1, bass.ds(e, 1)], min_val=0, max_val=SLOTS)
                expert(e, base)
            nx = pe.value_load(nx_i[0:1, :], min_val=0, max_val=XMAX - 1)
            with pe.If(nx > 0):
                with pe.Fori(0, nx) as j:
                    base = pe.value_load(xbase_i[0:1, bass.ds(j, 1)], min_val=0, max_val=SLOTS)
                    expert(j + NE, base)

            pe.wait_ge(y_added, 2 * (nx + NE))
            for k in range(16):
                s, n = k // 4, k % 4
                if k >= 8:
                    pe.wait_ge(yt_act if k % 2 == 0 else yt_dve, (k - 8) // 2 + 1)
                for i in range(4):
                    last = tr(psum[:, k % 8, P * i:P * i + P], y_sorted[:, 4 * n + i, P * s:P * s + P], ident[:, :])
                last.then_inc(yt_t, 1)
            pe.wait_ge(yt_act, 8)
            pe.wait_ge(yt_dve, 8)
            for b in range(TB):
                for n in range(4):
                    for s in range(4):
                        last = mm(psum[:, 4 * b + n, :], selT[:, s, P * b:P * b + P], y_tok[:, s, 512 * n:512 * n + 512],
                                  start=(s == 0), stop=(s == 3))
                    last.then_inc(comb_mm, 1)


def t5_onehot():
    import math
    import numpy as np

    buckets, half = 32, 16
    oh = np.zeros((buckets + 1, 3 * W), np.float32)
    for m in range(3 * W):
        n = 2 * W - 1 - m
        if not 0 <= n < W:
            oh[buckets, m] = 1.0
        elif n < half:
            oh[n, m] = 1.0
        else:
            oh[min(buckets - 1, half + int(math.log(n / half) / math.log(W / half) * half)), m] = 1.0
    return oh


def kernel(**inputs):
    import numpy as np
    import concourse.bacc as bacc
    from concourse.bass_utils import run_bass_kernel_spmd

    x = {k: np.asarray(v) for k, v in inputs.items()}
    col = lambda v: v.reshape(P, -1)
    chan = lambda v: v.reshape(-1, P).T
    state = lambda v: v.reshape(NPAIR, P).T
    arrays = {
        "x": x["x"].reshape(T, D), "table": x["rel_bias_table"], "onehot": t5_onehot(),
        "g_mix": col(x["g_norm_mix"]), "g_ffn": col(x["g_norm_ffn"]), "g_attn": col(x["g_attn_out"]),
        "g_ssm": chan(x["g_ssm_out"]), "d_skip": chan(x["ssm_d"]), "b_glu": chan(x["b_glu"]),
        "lam_re": state(x["lam_re"]), "lam_im": state(x["lam_im"]), "log_dt": x["log_dt"].reshape(NPAIR, 2).T,
        "b_re": x["ssm_b_re"].reshape(NPAIR, P, SC).transpose(1, 0, 2),
        "b_im": x["ssm_b_im"].reshape(NPAIR, P, SC).transpose(1, 0, 2),
        "c_re": x["ssm_c_re"].reshape(NPAIR, 2, SC, NS).transpose(1, 3, 0, 2).reshape(P, NPAIR, SC),
        "c_im": x["ssm_c_im"].reshape(NPAIR, 2, SC, NS).transpose(1, 3, 0, 2).reshape(P, NPAIR, SC),
        "sinks": x["attn_sinks"].reshape(NH),
        "w_router": np.concatenate([x["w_router_group"][0], x["w_router_expert"][0].transpose(1, 0, 2).reshape(D, NE)],
                                   axis=1).reshape(P, DC, NG + NE),
        "b_router": np.concatenate([x["b_router_group"].reshape(-1), x["b_router_expert"].reshape(-1)]),
        "w_in": x["w_in"][0], "w_glu": x["w_glu"][0], "w_out": x["w_out"][0],
        "w_gate": x["w_gate"].reshape(NE, D, FF), "w_up": x["w_up"].reshape(NE, D, FF),
        "w_down": x["w_down"].reshape(NE, FF, D), "g_final": x["g_final"],
    }
    nc = bacc.Bacc("TRN2", target_bir_lowering=False, num_devices=1)
    feed, aps = {}, {}
    for name, v in arrays.items():
        v = np.ascontiguousarray(v)
        feed[f"in_{name}"] = v
        aps[name] = nc.dram_tensor(f"in_{name}", v.shape, mybir.dt.from_np(v.dtype), kind="ExternalInput").ap()
    out = nc.dram_tensor("out_block", (T, D), F32, kind="ExternalOutput").ap()
    hymba_block(nc, aps, out)
    r = run_bass_kernel_spmd(nc, [feed], core_ids=[0])
    return r.results[0]["out_block"].reshape(1, T, D)
```

```python
from contextlib import ExitStack

import concourse.bass as bass
from concourse import mybir

F32 = mybir.dt.float32
I32 = mybir.dt.int32
ALU = mybir.AluOpType
ACT = mybir.ActivationFunctionType
AX = mybir.AxisListType.X

P = 128
D, T, TB = 2048, 256, 2
DC = D // P
NH, HD = 16, 64
W = 128
G, SC, NS = 64, 16, 64
NPAIR = G // 2
Q = 4
NCH = T // Q
HP = NPAIR // 2
NE, NG, EG, FF = 32, 4, 8, 512
SLOTS = 2 * T
CAP = 64
XMAX = SLOTS // CAP
PADDED = SLOTS + CAP
RING, SLOT = 6, 4096
PRE = 2
N_WIN, N_GLU, N_OUT = 9, 2, 8
NPRE = N_WIN + N_GLU + N_OUT
EPS = 1e-6
NEG = -1e30
PI = 3.14159265358979
MAGIC = 12582912.0
TWO_PI_HI = 6.28125
TWO_PI_LO = 2 * PI - TWO_PI_HI


def bcast(ap, axis, n):
    v = ap.unsqueeze(axis)
    shape = list(v.shape)
    shape[axis] = n
    return v.broadcast_to(shape)


class Count:

    def __init__(self, sem):
        self.sem, self.n = sem, 0

    def inc(self, ins, by=1):
        self.n += by
        ins.then_inc(self.sem, by)
        return self.n


def hymba_block(nc, a, out):
    with ExitStack() as ctx:
        def sem(name):
            return ctx.enter_context(nc.semaphore(name))

        arena = ctx.enter_context(nc.sbuf_tensor("arena", [P, RING * SLOT + 2 * 9216 + 2 * 4096], F32))
        psum = ctx.enter_context(nc.psum_tensor("psum", [P, 8, 512], F32))
        skew = nc.dram_tensor("bias_skew", [NH, P, 384], F32, kind="Internal")

        def view(start, shape):
            n = 1
            for s in shape:
                n *= s
            v = arena[:, start:start + n]
            if len(shape) > 1:
                names = ["a", "b", "c", "d"][:len(shape)]
                v = v.rearrange(f"p ({' '.join(names)}) -> p {' '.join(names)}",
                                **dict(zip(names[1:], shape[1:])))
            return v

        def small(name, shape, dt=F32):
            return ctx.enter_context(nc.sbuf_tensor(name, [P] + shape, dt))

        ssm_params = ctx.enter_context(nc.sbuf_tensor("ssm_params", [P, 42 * NPAIR], F32))
        at = [0]

        def param(*shape):
            n = 1
            for k in shape:
                n *= k
            v = ssm_params[:, at[0]:at[0] + n]
            at[0] += n
            return v.rearrange("p (k j) -> p k j", k=shape[0]) if len(shape) > 1 else v

        ring = [view(SLOT * k, [SLOT]) for k in range(RING)]
        C0 = PRE * SLOT
        bias = view(C0, [NH, 2 * W])
        scores = [view(C0 + 4096 + 768 * k, [2, 3 * W]) for k in range(3)]
        attnT = view(C0 + 6400, [8, T])
        kk = view(C0 + 8448, [2, T])
        vv = view(C0 + 8960, [TB, 2 * HD])
        bbar_r = view(C0 + 9216, [NPAIR, 2 * SC])
        bbar_i = view(C0 + 10240, [NPAIR, 2 * SC])
        craw_r = view(C0 + 11264, [NPAIR, SC])
        craw_i = view(C0 + 11776, [NPAIR, SC])
        BP1 = C0 + 12288
        braw_r = view(C0 + 6400, [NPAIR, SC])
        braw_i = view(C0 + 6912, [NPAIR, SC])
        onehot = view(C0 + 5120, [384])
        table = view(C0 + 5504, [NH])
        bias_row = view(C0 + 5632, [384])
        turn_a = view(C0 + 4096, [HP, NCH // 2])
        turn_b = view(C0 + 4608, [HP, NCH // 2])
        attn_rs = view(C0 + 4096, [T])

        M0 = RING * SLOT
        u4 = view(M0, [NPAIR, NCH])
        BP = (M0 + 2048, BP1)
        bp_r = [view(b, [HP, Q, 2 * SC]) for b in BP]
        bp_i = [view(b + 2048, [HP, Q, 2 * SC]) for b in BP]
        z_r, z_i, tmp_a, tmp_b = ([view(b + 1024 * k, [HP, NCH]) for b in BP] for k in range(4))
        bt_r = view(M0 + 6144, [HP, P])
        bt_i = view(M0 + 8192, [HP, P])
        decay = view(M0 + 6144, [HP, NCH])
        cp_r = view(M0 + 10240, [HP, Q, 2 * SC])
        cp_i = view(M0 + 12288, [HP, Q, 2 * SC])
        toep = view(M0 + 14336, [HP, Q, 2 * SC])
        cos_t = view(M0 + 16384, [HP, NCH])
        sin_t = view(M0 + 17408, [HP, NCH])
        full_tmp = view(M0 + 10240, [NPAIR, SC])

        h_sorted = view(M0, [DC, PADDED])
        y_sorted = view(M0 + 9216, [DC, PADDED])
        h2 = view(M0 + 9216, [TB, D])
        h2T = view(M0 + 9216 + 4096, [DC, T])
        rt = M0 + 9216 + 8192
        wr = view(M0, [DC, NG + NE])

        R1 = M0 + 18432
        x1 = view(R1, [TB, D])
        uT = view(R1, [8, T])
        qT = view(R1 + 2048, [8, T])
        R2 = R1 + 4096
        hT = view(R2, [DC, T])
        mixT = view(R2, [DC, T])
        sel = view(R2, [TB, SLOTS])
        selw = view(R2 + 1024, [TB, SLOTS])
        selT = view(R2 + 2048, [4, T])
        wrow = view(R2 + 3072, [PADDED])
        keep = R2 + 3072 + PADDED
        hs = view(R2, [DC, CAP])
        gated_h = view(R2 + 1024, [FF])
        hid = view(R2 + 1536, [4, CAP])
        wmask = view(R2 + 1792, [CAP])
        y_tok = view(0, [4, D])
        g_fin = view(M0, [D])
        result = view(M0 + 2048, [TB, D])
        sgate = view(M0 + 4096, [8, T])
        ysq = view(M0 + 6144, [8, T])
        attn_sq = view(M0 + 8192, [8, T])
        ssm = view(R2 + 2048, [8, T])
        ssm_rs = view(M0 + 10240, [T])
        y_first = view(M0 + 7168, [4, T])

        ident, ones = small("ident", [P]), small("ones", [P])
        g_mix, g_ffn = small("g_mix", [DC]), small("g_ffn", [DC])
        g_attn, g_ssm = small("g_attn", [8]), small("g_ssm", [8])
        d_skip, b_glu = small("d_skip", [8]), small("b_glu", [8])
        sinks, b_rt = small("sinks", [NH]), small("b_rt", [NG + NE])
        lam_r, lam_i, dt = param(NPAIR), param(NPAIR), param(NPAIR)
        pw_r, pw_i = param(Q + 1, NPAIR), param(Q + 1, NPAIR)
        rev_r, rev_i = param(Q, NPAIR), param(Q, NPAIR)
        e_r, e_i = param(6, NPAIR), param(6, NPAIR)
        mag, ang, rot, sn, cs, c1, c2, c3, c4 = (param(NPAIR) for _ in range(9))
        y_rows = ssm_params[:, 0:2 * 512].rearrange("p (b n) -> p b n", b=2)
        stat = small("stat", [32])
        mxs, sums, recs, esink = ([small(f"{n}{k}", [2, 2]) for k in range(2)] for n in ("mxs", "sums", "recs", "esink"))
        tok_sq = small("tok_sq", [TB, N_OUT])

        landed = [sem(f"ring{k}_landed") for k in range(RING)]
        consumed = sem("ring_consumed")
        x_in, x_again = [sem("x_in0"), sem("x_in1")], sem("x_again")
        small_in, ssm_in, t5_in = sem("small_in"), sem("ssm_in"), sem("t5_in")
        router_in, gfin_in = sem("router_in"), sem("gfin_in")
        const_ready = sem("const_ready")
        pool_self = sem("pool_self")
        dve, act = sem("dve_self"), sem("act_self")
        x_sq = sem("x_sq")
        h_ready = sem("h_ready")
        hT_t, hT_ready = sem("hT_t"), sem("hT_ready")
        proj_out = sem("proj_out")
        table_ready, row_done, row_out, row_dma = sem("table_ready"), sem("row_done"), sem("row_out"), sem("row_dma")
        bias_in = sem("bias_in")
        ssm_mag, ssm_sin = sem("ssm_mag"), sem("ssm_sin")
        dt_ready, ang_ready = sem("dt_ready"), sem("ang_ready")
        u4_ready, u4_act = sem("u4_ready"), sem("u4_act")
        bp_ready, cp_ready = sem("bp_ready"), sem("cp_ready")
        bt_t, bt_out = sem("bt_t"), sem("bt_out")
        toep_zero, toep_mm, toep_out = sem("toep_zero"), sem("toep_mm"), sem("toep_out")
        v_mm, v_read = sem("v_mm"), sem("v_read")
        w_ready, y_mm, y_out = sem("w_ready"), sem("y_mm"), sem("y_out")
        sc_mm, sc_read, sc_ready = sem("sc_mm"), sem("sc_read"), sem("sc_ready")
        probs = sem("probs")
        normed, pt_t, pt_out, pv_mm, pv_out = (sem(n) for n in ("normed", "pt_t", "pt_out", "pv_mm", "pv_out"))
        asq_ready, asq_mm, asq_rt, attn_out = (sem(n) for n in ("asq_ready", "asq_mm", "asq_rt", "attn_out"))
        gelu_in, gelu_out = sem("gelu_in"), sem("gelu_out")
        glu_mm, glu_sig, ssq_ready, ssq_mm, ssq_rt, ssm_out = (sem(n) for n in (
            "glu_mm", "glu_sig", "ssq_ready", "ssq_mm", "ssq_rt", "ssm_out"))
        x1_out, x1_sq, x1_rt, h2_ready = (sem(n) for n in (
            "x1_out", "x1_sq", "x1_rt", "h2_ready"))
        h2_t, h2_out, router_mm = sem("h2_t"), sem("h2_out"), sem("router_mm")
        logit, gexp, eexp = sem("logit"), sem("gexp"), sem("eexp")
        onehot_ready, count_mm, sel_ready, wrow_mm, selT_t = (sem(n) for n in (
            "onehot_ready", "count_mm", "sel_ready", "wrow_mm", "selT_t"))
        gather_act, routed, gather_mm, gather_dve, y_zero = (sem(n) for n in (
            "gather_act", "routed", "gather_mm", "gather_dve", "y_zero"))
        mask_ready, silu_ready, gated, hidT_mm, hid_ready, y_copied, y_copied2, yT_mm, y_added, hs_ready = (sem(n) for n in (
            "mask_ready", "silu_ready", "gated", "hidT_mm", "hid_ready", "y_copied", "y_copied2", "yT_mm", "y_added", "hs_ready"))
        yt_t, yt_act, yt_dve, comb_mm, comb_out, fin_sq, fin_rt, fin_ready, stored = (sem(n) for n in (
            "yt_t", "yt_act", "yt_dve", "comb_mm", "comb_out", "fin_sq", "fin_rt", "fin_ready", "stored"))

        counts = view(keep, [NE])
        base_end = view(keep + 32, [NE])
        xlim = view(keep + 64, [XMAX])
        iota_c = view(keep + 72, [CAP])
        itab = ctx.enter_context(nc.sbuf_tensor("itab", [P, 80], I32))
        base_i, xexp_i, xbase_i, nx_i = itab[:, 0:32], itab[:, 32:40], itab[:, 40:48], itab[:, 48:49]

        rs = lambda o, shape: view(rt + o, shape)
        lg = rs(0, [TB, NG + NE])
        iota_s = view(R2 + 2048, [SLOTS])
        rev_iota = small("rev_iota", [NE])
        iota_e = small("iota_e", [NE])

        gl_exp = rs(72, [TB, NG])
        m_diff = rs(80, [TB, 1])
        g_one = rs(84, [TB, NG])
        g_max = rs(92, [TB, 1])
        e_sel = rs(96, [TB, EG])
        k_one = [rs(112 + 16 * k, [TB, EG]) for k in range(2)]
        m_top = rs(144, [TB, 2])
        t_a, t_b = rs(148, [TB, NG]), rs(160, [TB, EG])
        g_p = rs(176, [TB, 1])
        w_top = rs(180, [TB, 2])
        one32 = [rs(192 + 64 * k, [TB, NE]) for k in range(2)]
        both = rs(320, [TB, NE])
        slot_e = rs(384, [TB, NE])
        slot_t = rs(448, [TB, 2])
        big = rs(512, [XMAX, NE])
        big2 = rs(768, [XMAX, NE])
        nxt, xcum = rs(456, [NE]), view(keep + 320, [NE])
        prod4 = rs(320, [TB, EG, NG])
        rowf = view(keep + 296, [3, XMAX])
        y_tmp = view(R2 + 3072, [SLOTS])
        iota_e2 = view(keep + 264, [NE])
        tri = view(keep + 136, [P])

        u4v = u4.rearrange("p (c q) t -> p q c t", q=4)
        uTs = uT.rearrange("p c (t s) -> p s c t", s=Q)

        block = ctx.enter_context(nc.Block())

        def glu_rows(k):
            return a["w_glu"].rearrange("(c p) n -> p c n", p=P)[:, :, 512 * k:512 * (k + 1)]

        proj_bank = lambda n: n % 2 if n < 6 else 0
        GLU_BANKS = (0, 1, 4, 5)

        W_IN_COLS = [1280 + 256 * k for k in range(4)] + [1024] + [256 * k for k in range(4)]

        def slot3(k, chunks):
            return ring[k].rearrange("p (c n) -> p c n", c=chunks)

        GATE_A, UP_A, GATE_B, UP_B, DOWN_A, DOWN_B = range(6)
        ring_of = lambda k: (PRE + k) % RING

        def expert_source(k, e):
            e1 = bass.ds(e, 1)
            if k in (GATE_A, GATE_B):
                return a["w_gate"].rearrange("e (p c) f -> e p c f", p=P)[e1, :, 8 * (k == GATE_B):8 * (k == GATE_B) + 8, :]
            if k in (UP_A, UP_B):
                return a["w_up"].rearrange("e (p c) f -> e p c f", p=P)[e1, :, 8 * (k == UP_B):8 * (k == UP_B) + 8, :]
            return a["w_down"].rearrange("e (p c) d -> e p c d", p=P)[e1, :, 2 * (k == DOWN_B):2 * (k == DOWN_B) + 2, :]

        @block.sync
        def _(sp):
            for b in range(TB):
                sp.dma_start(x1[:, b, :], a["x"][P * b:P * (b + 1), :]).then_inc(x_in[b], 16)

            def room(n):
                if n >= PRE:
                    sp.wait_ge(consumed, n - PRE + 1)

            n = 0
            for col in W_IN_COLS:
                room(n)
                sp.dma_start(slot3(n % PRE, DC), a["w_in"].rearrange("(p c) n -> p c n", p=P)[:, :, col:col + 256]
                             ).then_inc(landed[n % PRE], 16)
                n += 1
            for k in range(N_GLU):
                room(n)
                sp.dma_start(slot3(n % PRE, 8), glu_rows(k)).then_inc(landed[n % PRE], 16)
                n += 1
            for k in range(N_OUT):
                room(n)
                cols = slice(256 * k, 256 * (k + 1))
                sp.dma_start(slot3(n % PRE, DC), a["w_out"].rearrange("(c p) n -> p c n", p=P)[:, :, cols]).then_inc(landed[n % PRE], 16)
                n += 1
                if k == 0:
                    sp.wait_ge(gelu_in, 2)
                    sp.wait_ge(sc_mm, 8)
                    for b in range(TB):
                        sp.dma_start(x1[:, b, :], a["x"][P * b:P * (b + 1), :]).then_inc(x_again, 16)

            def fetch(e, block_no, first=False):
                for k in range(RING):
                    if first and ring_of(k) >= PRE:
                        if k == 0:
                            sp.wait_ge(attn_out, 8)
                            sp.wait_ge(y_mm, 2)
                    elif first:
                        sp.wait_ge(consumed, max(m for m in range(NPRE) if m % PRE == ring_of(k)) + 1)
                    else:
                        sp.wait_ge(consumed, NPRE + RING * (block_no - 1) + k + 1)
                    chunks = 2 if k >= DOWN_A else 8
                    sp.dma_start(slot3(ring_of(k), chunks), expert_source(k, e)).then_inc(landed[ring_of(k)], 16)

            fetch(0, 0, first=True)
            with sp.Fori(1, NE) as e:
                fetch(e, e)
            sp.wait_ge(routed, 1)
            nx = sp.value_load(nx_i[0:1, :], min_val=0, max_val=XMAX - 1)
            with sp.If(nx > 0):
                with sp.Fori(0, nx) as j:
                    e = sp.value_load(xexp_i[0:1, bass.ds(j, 1)], min_val=0, max_val=NE - 1)
                    fetch(e, j + NE)
            for b in range(TB):
                sp.wait_ge(fin_ready, b + 1)
                sp.dma_start(out[P * b:P * (b + 1), :], result[:, b, :]).then_inc(stored, 16)
            sp.wait_ge(stored, 16 * TB)

        @block.gpsimd
        def _(pool):
            me = Count(pool_self)

            def link(ins):
                pool.wait_ge(pool_self, me.inc(ins))

            link(pool.memset(ident[:, :], 0.0))
            pool.affine_select(out=ident[:, :], in_=ident[:, :], compare_op=ALU.not_equal, fill=1.0, base=0,
                               pattern=[[-1, P]], channel_multiplier=1).then_inc(const_ready, 1)
            pool.memset(ones[:, :], 1.0).then_inc(const_ready, 1)
            pool.iota(iota_e[:, :], pattern=[[1, NE]], base=0, channel_multiplier=0,
                      allow_small_or_imprecise_dtypes=True).then_inc(const_ready, 1)
            pool.iota(rev_iota[:, :], pattern=[[-1, NE]], base=NE, channel_multiplier=0,
                      allow_small_or_imprecise_dtypes=True).then_inc(const_ready, 1)
            for m in (bbar_r, bbar_i, cp_r, cp_i, bp_r[0], bp_i[0], toep, bp_r[1], bp_i[1]):
                pool.memset(m[:], 0.0).then_inc(const_ready, 1)
            pool.wait_ge(row_out, 1)
            pool.dma_start(skew.ap(), bcast(bias_row[0:NH, :], 1, P)).then_inc(row_dma, 16)
            pool.wait_ge(row_dma, 16)
            for k in range(4):
                pool.dma_start(bias[:, 4 * k:4 * k + 4, :],
                               bass.AP(tensor=skew, offset=4 * k * P * 384 + P - 1,
                                       ap=[[383, P], [P * 384, 4], [1, 2 * W]])).then_inc(bias_in, 16)
            pool.wait_ge(proj_out, 4)
            pool.wait_ge(const_ready, 13)
            for q in range(2):
                for s in range(Q):
                    if q or s:
                        pool.wait_ge(u4_ready, Q * q + s)
                    pool.tensor_copy(u4v[32 * s:32 * s + 32, q], uTs[32 * q:32 * q + 32, s]).then_inc(u4_ready, 1)
            pool.wait_ge(u4_ready, 8)
            for half in range(2):
                pool.wait_ge(cp_ready, 2 * half + 2)
                pool.memset(toep[:], 0.0).then_inc(toep_zero, 1)
            pool.wait_ge(consumed, NPRE)
            link(pool.memset(tri[:, :], 1.0))
            pool.affine_select(out=tri[:, :], in_=tri[:, :], compare_op=ALU.is_gt, fill=0.0, base=0,
                               pattern=[[1, P]], channel_multiplier=-1).then_inc(const_ready, 1)
            pool.iota(iota_s[:, :], pattern=[[1, SLOTS]], base=0, channel_multiplier=0,
                      allow_small_or_imprecise_dtypes=True).then_inc(logit, 1)
            pool.iota(iota_c[:, :], pattern=[[1, CAP]], base=0, channel_multiplier=0,
                      allow_small_or_imprecise_dtypes=True).then_inc(logit, 1)
            pool.memset(wrow[:, SLOTS:PADDED], 0.0).then_inc(logit, 1)
            pool.wait_ge(router_mm, 1)
            pool.memset(h_sorted[:, :, SLOTS:PADDED], 0.0).then_inc(y_zero, 1)
            pool.wait_ge(gather_mm, DC)
            pool.wait_ge(routed, 1)
            pool.wait_ge(gather_act, DC)
            pool.wait_ge(y_zero, 1)

            def window(base):
                pool.tensor_copy(hs[:, :, :], h_sorted[:, :, bass.ds(base, CAP)]).then_inc(hs_ready, 1)

            pool.memset(gated_h[0:64, :], 0.0).then_inc(y_zero, 1)
            window(pool.value_load(base_i[0:1, 0:1], min_val=0, max_val=SLOTS))
            pool.memset(y_sorted[:], 0.0).then_inc(y_zero, 1)
            with pool.Fori(1, NE) as e:
                base = pool.value_load(base_i[0:1, bass.ds(e, 1)], min_val=0, max_val=SLOTS)
                pool.wait_ge(consumed, RING * e + (NPRE + 4 - RING))
                window(base)
            nx = pool.value_load(nx_i[0:1, :], min_val=0, max_val=XMAX - 1)
            with pool.If(nx > 0):
                with pool.Fori(0, nx) as j:
                    base = pool.value_load(xbase_i[0:1, bass.ds(j, 1)], min_val=0, max_val=SLOTS)
                    pool.wait_ge(consumed, RING * j + (NPRE + 4 + RING * (NE - 1)))
                    window(base)

        @block.scalar
        def _(sc):
            nc_s = nc.scalar
            me = Count(act)

            def link(ins):
                sc.wait_ge(act, me.inc(ins))

            sc.dma_start(table[0:32, :], a["table"]).then_inc(t5_in, 16)
            sc.dma_start(onehot[0:33, :], a["onehot"]).then_inc(t5_in, 16)
            for name, tile in (("g_mix", g_mix), ("g_ffn", g_ffn), ("g_attn", g_attn), ("g_ssm", g_ssm),
                               ("d_skip", d_skip), ("b_glu", b_glu)):
                sc.dma_start(tile[:, :], a[name]).then_inc(small_in, 16)
            sc.dma_start(lam_r[:, :], a["lam_re"]).then_inc(ssm_in, 16)
            sc.dma_start(lam_i[:, :], a["lam_im"]).then_inc(ssm_in, 16)
            for g in range(2):
                sc.dma_start(dt[64 * g:64 * g + 64, :], a["log_dt"][g:g + 1, :].partition_broadcast(64)).then_inc(ssm_in, 16)
            for name, tile in (("b_re", braw_r), ("b_im", braw_i), ("c_re", craw_r), ("c_im", craw_i)):
                sc.dma_start(tile[:, :, :], a[name]).then_inc(ssm_in, 16)
            sc.dma_start(sinks[:, :], a["sinks"].partition_broadcast(P)).then_inc(small_in, 16)
            sc.dma_start(b_rt[:, :], a["b_router"].partition_broadcast(P)).then_inc(small_in, 16)

            for b in range(TB):
                sc.wait_ge(x_in[b], 16)
                nc_s.activation(hT.rearrange("p c t -> p (c t)")[:, 2048 * b:2048 * b + 2048], x1[:, b, :], ACT.Square,
                                accum_out=stat[:, b:b + 1]).then_inc(x_sq, 1)
            sc.wait_ge(h_ready, 1)
            nc_s.activation(stat[:, 4:6], stat[:, 2:4], ACT.Sqrt).then_inc(x_sq, 1)
            sc.wait_ge(small_in, 16 * 8)
            for c in (c for c in range(DC) if c // 2 % 2 == 0):
                sc.wait_ge(hT_t, c // 2 + 1)
                nc_s.activation(hT[:, c, :], psum[:, c // 2, T * (c % 2):T * (c % 2) + T], ACT.Copy, scale=g_mix[:, c:c + 1]).then_inc(hT_ready, 1)
            sc.wait_ge(row_done, 1)
            nc_s.copy(bias_row[0:NH, :], psum[0:NH, 7, 0:384]).then_inc(row_out, 1)
            sc.wait_ge(ssm_in, 16 * 8)
            nc_s.activation(dt[:, :], dt[:, :], ACT.Exp).then_inc(dt_ready, 1)
            sc.wait_ge(ssm_mag, 1)
            nc_s.activation(mag[:, :], mag[:, :], ACT.Exp).then_inc(ssm_mag, 1)
            sc.wait_ge(ang_ready, 1)
            nc_s.activation(sn[:, :], ang[:, :], ACT.Sin).then_inc(ssm_sin, 1)
            nc_s.activation(cs[:, :], ang[:, :], ACT.Sin, scale=0.5).then_inc(ssm_sin, 1)
            for n in range(4):
                sc.wait_ge(consumed, n + 1)
                nc_s.copy(uT[:, 2 * n:2 * n + 2, :], psum[:, n % 2, :].rearrange("p (a b) -> p a b", a=2)).then_inc(proj_out, 1)
            sc.wait_ge(proj_out, 4)
            for q in range(2, 4):
                for s in range(Q):
                    nc_s.copy(u4v[32 * s:32 * s + 32, q], uTs[32 * q:32 * q + 32, s]).then_inc(u4_act, 1)

            def kv_piece():
                sc.wait_ge(consumed, 5)
                for half in range(2):
                    for g in range(2):
                        link(nc_s.copy(kk[64 * half:64 * half + 64, g, :], psum[64 * g:64 * g + 64, 0, 0:T]))
                nc_s.copy(vv[:, :, :], psum[:, 0, T:2 * T].rearrange("p (a b) -> p a b", a=2)).then_inc(proj_out, 1)

            def transposed_b(half):
                if half == 1:
                    sc.wait_ge(w_ready, 1)
                for k in range(8):
                    sc.wait_ge(bt_t, 8 * half + k + 1)
                    dst = (bt_r if k % 2 == 0 else bt_i)[:, 4 * (k // 2):4 * (k // 2) + 4, :]
                    nc_s.copy(dst, psum[:, 2 + k % 4, :].rearrange("p (a b) -> p a b", a=4)).then_inc(bt_out, 1)

            def toeplitz(half):
                sc.wait_ge(toep_zero, half + 1)
                sc.wait_ge(toep_mm, half + 1)
                tv = toep.rearrange("p (k i) t c -> p i k t c", i=4)
                for i in range(4):
                    src = psum[32 * i:32 * i + 32, 6 if half == 0 else 0, :].rearrange("p (k t c) -> p k t c", k=4, t=Q)
                    for s in range(Q):
                        nc_s.copy(tv[32 * s:32 * s + 32, i, :, s:Q, :].rearrange("p k t c -> p k (t c)"),
                                  src[:, :, 0:Q - s, :].rearrange("p k t c -> p k (t c)")).then_inc(toep_out, 1)

            def q_pieces(n0, n1):
                for n in range(n0, n1):
                    sc.wait_ge(consumed, n + 1)
                    c = 2 * (n - 5)
                    nc_s.mul(qT[:, c:c + 2, :], psum[:, proj_bank(n), :].rearrange("p (a b) -> p a b", a=2), HD ** -0.5).then_inc(proj_out, 1)

            def ssm_outputs(half):
                sc.wait_ge(y_mm, half + 1)
                bank = 6 if half == 0 else 2
                src = psum[:, bank:bank + 2, :].rearrange("p b (c q t) -> p q (b c) t", q=4, t=NCH)
                y = y_first if half == 0 else ssm[:, 4:8, :]
                for q in range(4):
                    for t in range(Q):
                        dst = y[32 * q:32 * q + 32, :, :].rearrange("p c (t s) -> p s c t", s=Q)[:, t]
                        nc_s.copy(dst, src[32 * t:32 * t + 32, q]).then_inc(y_out, 1)

            def exps(b):
                sc.wait_ge(sc_ready, b + 1)
                s2, m2, a2, e2 = scores[b % 3], mxs[b % 2], sums[b % 2], esink[b % 2]
                for h in range(2):
                    nc_s.activation(s2[:, h, 0:W], s2[:, h, 0:W], ACT.Exp, bias=m2[:, h, 0:1], accum_out=a2[:, h, 0:1]).then_inc(probs, 1)
                    nc_s.activation(s2[:, h, W:3 * W], s2[:, h, W:3 * W], ACT.Exp, bias=m2[:, h, 1:2], accum_out=a2[:, h, 1:2]).then_inc(probs, 1)
                nc_s.activation(e2[:, :, :], e2[:, :, :], ACT.Exp).then_inc(probs, 1)

            def probs_back(b):
                for h in range(2):
                    sc.wait_ge(pt_t, 2 * b + h + 1)
                    nc_s.copy(scores[b % 3][:, h, :], psum[:, 6 + h, 0:3 * W]).then_inc(pt_out, 1)

            def attn_rows(b):
                sc.wait_ge(pv_mm, b + 1)
                nc_s.copy(attnT[:, b, :], psum[:, 1, 0:T]).then_inc(pv_out, 1)

            def gelu(half):
                sc.wait_ge(gelu_in, half + 1)
                ys = ssm[:, 4 * half:4 * half + 4, :]
                nc_s.activation(ys, ys, ACT.Gelu_apprx_tanh).then_inc(gelu_out, 1)

            kv_piece()
            transposed_b(0)
            toeplitz(0)
            q_pieces(5, 7)
            transposed_b(1)
            ssm_outputs(0)
            for b in range(10):
                if b < 8:
                    exps(b)
                if b in (2, 4):
                    q_pieces(6 + b // 2, 7 + b // 2)
                if b == 7:
                    toeplitz(1)
                if b == 8:
                    gelu(0)
                if 1 <= b < 9:
                    probs_back(b - 1)
                if b >= 2:
                    attn_rows(b - 2)
            ssm_outputs(1)
            gelu(1)
            sc.wait_ge(asq_mm, 2)
            nc_s.activation(attn_rs[:, :], attn_rs[:, :], ACT.Sqrt).then_inc(asq_rt, 1)
            for c in range(8):
                sc.wait_ge(glu_mm, c + 1)
                nc_s.activation(sgate[:, c, :], psum[:, GLU_BANKS[c % 4], 0:T], ACT.Sigmoid, bias=b_glu[:, c:c + 1]).then_inc(glu_sig, 1)
            sc.wait_ge(ssq_mm, 2)
            nc_s.activation(ssm_rs[:, :], ssm_rs[:, :], ACT.Sqrt).then_inc(ssq_rt, 1)
            sc.wait_ge(ssm_out, 8)
            sc.dma_start(wr[:, :, :], a["w_router"]).then_inc(router_in, 16)

            for k in range(N_OUT):
                sc.wait_ge(x1_out, k + 1)
                for b in range(TB):
                    cols = slice(256 * k, 256 * (k + 1))
                    nc_s.activation(h2[:, b, cols], x1[:, b, cols], ACT.Square, accum_out=tok_sq[:, b, k:k + 1]).then_inc(x1_sq, 1)
            sc.wait_ge(x1_rt, 1)
            nc_s.activation(stat[:, 20:22], stat[:, 18:20], ACT.Sqrt).then_inc(x1_sq, 1)
            for c in (c for c in range(DC) if c // 2 % 2 == 0):
                sc.wait_ge(h2_t, c // 2 + 1)
                nc_s.activation(h2T[:, c, :], psum[:, c // 2, T * (c % 2):T * (c % 2) + T], ACT.Copy, scale=g_ffn[:, c:c + 1]).then_inc(h2_out, 1)
            sc.wait_ge(eexp, 1)
            nc_s.activation(gl_exp[:, :, :], gl_exp[:, :, :], ACT.Exp).then_inc(gexp, 1)
            nc_s.activation(m_diff[:, :, :], m_diff[:, :, :], ACT.Exp).then_inc(gexp, 1)
            for c in range(DC):
                sc.wait_ge(gather_mm, c + 1)
                nc_s.activation(h_sorted[:, c, 0:SLOTS], psum[:, (c + 5) % 8, :], ACT.Copy, scale=g_ffn[:, c:c + 1]).then_inc(gather_act, 1)

            def expert(block_no):
                sc.wait_ge(consumed, RING * block_no + (NPRE + 4))
                nc_s.activation(gated_h[64:128, :], psum[0:64, 0, :], ACT.Silu).then_inc(silu_ready, 1)
                sc.wait_ge(consumed, RING * block_no + (NPRE + 6))
                nc_s.copy(y_rows[:, 0, :], psum[:, 2, :]).then_inc(y_copied, 1)

            with sc.Fori(0, NE) as e:
                expert(e)
            sc.wait_ge(routed, 1)
            nx = sc.value_load(nx_i[0:1, :], min_val=0, max_val=XMAX - 1)
            with sc.If(nx > 0):
                with sc.Fori(0, nx) as j:
                    expert(j + NE)
            sc.wait_ge(consumed, RING * nx + (NPRE + RING * NE))
            sc.dma_start(g_fin[:, :], a["g_final"].partition_broadcast(P)).then_inc(gfin_in, 16)
            for k in range(0, 16, 2):
                sc.wait_ge(yt_t, k + 1)
                nc_s.copy(y_tok[:, k // 4, 512 * (k % 4):512 * (k % 4) + 512], psum[:, k % 8, :]).then_inc(yt_act, 1)
            for b in range(TB):
                sc.wait_ge(comb_out, 4 * (b + 1))
                nc_s.activation(result[:, b, :], x1[:, b, :], ACT.Square, accum_out=stat[:, 24 + b:25 + b]).then_inc(fin_sq, 1)
                sc.wait_ge(fin_rt, b + 1)
                nc_s.activation(stat[:, 28 + b:29 + b], stat[:, 26 + b:27 + b], ACT.Sqrt).then_inc(fin_sq, 1)

        @block.vector
        def _(v):
            me = Count(dve)
            nv = nc.vector

            def link(ins):
                v.wait_ge(dve, me.inc(ins))

            TT, TS, STT = nv.tensor_tensor, nv.tensor_scalar, nv.scalar_tensor_tensor

            v.wait_ge(t5_in, 32)
            nv.memset(table[32:33, :], NEG).then_inc(table_ready, 1)
            v.wait_ge(x_sq, 2)
            TS(stat[:, 2:4], stat[:, 0:2], 1.0 / D, EPS, ALU.mult, ALU.add).then_inc(h_ready, 1)
            v.wait_ge(x_sq, 3)
            link(nv.reciprocal(stat[:, 6:8], stat[:, 4:6]))
            for b in range(TB):
                TS(x1[:, b, :], x1[:, b, :], stat[:, 6 + b:7 + b], None, ALU.mult).then_inc(h_ready, 1)
            v.wait_ge(small_in, 16 * 8)
            for c in (c for c in range(DC) if c // 2 % 2 == 1):
                v.wait_ge(hT_t, c // 2 + 1)
                TS(hT[:, c, :], psum[:, c // 2, T * (c % 2):T * (c % 2) + T], g_mix[:, c:c + 1], None, ALU.mult).then_inc(hT_ready, 1)

            v.wait_ge(dt_ready, 1)
            TT(mag[:, :], lam_r[:, :], dt[:, :], ALU.mult).then_inc(ssm_mag, 1)
            link(TT(ang[:, :], lam_i[:, :], dt[:, :], ALU.mult))
            link(TS(c1[:, :], ang[:, :], 1.0 / (2 * PI), MAGIC, ALU.mult, ALU.add))
            link(TS(c1[:, :], c1[:, :], MAGIC, None, ALU.subtract))
            link(STT(ang[:, :], c1[:, :], -TWO_PI_HI, ang[:, :], ALU.mult, ALU.add))
            link(STT(ang[:, :], c1[:, :], -TWO_PI_LO, ang[:, :], ALU.mult, ALU.add))
            TS(ang[:, :], ang[:, :], 3.1415925, -3.1415925, ALU.min, ALU.max).then_inc(ang_ready, 1)
            v.wait_ge(ssm_sin, 2)
            v.wait_ge(ssm_mag, 2)
            link(TT(cs[:, :], cs[:, :], cs[:, :], ALU.mult))
            link(TS(cs[:, :], cs[:, :], -2.0, 1.0, ALU.mult, ALU.add))
            link(nv.memset(pw_r[:, 0, :], 1.0))
            link(nv.memset(pw_i[:, 0, :], 0.0))
            link(TT(pw_r[:, 1, :], mag[:, :], cs[:, :], ALU.mult))
            link(TT(pw_i[:, 1, :], mag[:, :], sn[:, :], ALU.mult))

            def cmul(or_, oi, ar, ai, br, bi, t1, t2):
                link(TT(t1, ai, bi, ALU.mult))
                link(TT(t2, ar, bi, ALU.mult))
                link(TT(oi, ai, br, ALU.mult))
                link(TT(or_, ar, br, ALU.mult))
                link(TT(or_, or_, t1, ALU.subtract))
                link(TT(oi, oi, t2, ALU.add))

            for k in range(2, Q + 1):
                cmul(pw_r[:, k, :], pw_i[:, k, :], pw_r[:, k - 1, :], pw_i[:, k - 1, :], pw_r[:, 1, :], pw_i[:, 1, :],
                     c1[:, :], c2[:, :])
            for k in range(Q):
                link(nv.tensor_copy(rev_r[:, k, :], pw_r[:, Q - k, :]))
                link(nv.tensor_copy(rev_i[:, k, :], pw_i[:, Q - k, :]))
            cmul(c3[:, :], c4[:, :], cs[:, :], sn[:, :], cs[:, :], sn[:, :], c1[:, :], c2[:, :])
            cmul(e_r[:, 0, :], e_i[:, 0, :], c3[:, :], c4[:, :], c3[:, :], c4[:, :], c1[:, :], c2[:, :])
            for k in range(1, 6):
                cmul(e_r[:, k, :], e_i[:, k, :], e_r[:, k - 1, :], e_i[:, k - 1, :], e_r[:, k - 1, :], e_i[:, k - 1, :],
                     c1[:, :], c2[:, :])
            link(TT(c1[:, :], lam_r[:, :], lam_r[:, :], ALU.mult))
            link(TT(c2[:, :], lam_i[:, :], lam_i[:, :], ALU.mult))
            link(TT(c1[:, :], c1[:, :], c2[:, :], ALU.add))
            link(nv.reciprocal(c1[:, :], c1[:, :]))
            link(TS(c2[:, :], pw_r[:, 1, :], -1.0, None, ALU.add))
            link(TT(rot[:, :], c2[:, :], lam_r[:, :], ALU.mult))
            link(TT(c3[:, :], pw_i[:, 1, :], lam_i[:, :], ALU.mult))
            link(TT(rot[:, :], rot[:, :], c3[:, :], ALU.add))
            link(TT(rot[:, :], rot[:, :], c1[:, :], ALU.mult))
            link(TT(sn[:, :], pw_i[:, 1, :], lam_r[:, :], ALU.mult))
            link(TT(c3[:, :], c2[:, :], lam_i[:, :], ALU.mult))
            link(TT(sn[:, :], sn[:, :], c3[:, :], ALU.subtract))
            link(TT(sn[:, :], sn[:, :], c1[:, :], ALU.mult))
            link(TT(mag[:, :], mag[:, :], mag[:, :], ALU.mult))
            link(TT(mag[:, :], mag[:, :], mag[:, :], ALU.mult))

            v.wait_ge(const_ready, 13)
            for g in range(2):
                ps, cols = slice(64 * g, 64 * g + 64), slice(SC * g, SC * g + SC)
                fr, fi = bcast(rot[ps, :], 2, SC), bcast(sn[ps, :], 2, SC)
                tmp = full_tmp[ps]
                link(TT(tmp, braw_i[ps], fi, ALU.mult))
                link(TT(bbar_r[ps, :, cols], braw_r[ps], fr, ALU.mult))
                link(TT(bbar_r[ps, :, cols], bbar_r[ps, :, cols], tmp, ALU.subtract))
                link(TT(tmp, braw_r[ps], fi, ALU.mult))
                link(TT(bbar_i[ps, :, cols], braw_i[ps], fr, ALU.mult))
                link(TT(bbar_i[ps, :, cols], bbar_i[ps, :, cols], tmp, ALU.add))
            link(nv.memset(cp_r[:], 0.0))

            def input_matrix(half):
                js = slice(HP * half, HP * half + HP)
                for g in range(2):
                    ps, cols = slice(64 * g, 64 * g + 64), slice(SC * g, SC * g + SC)

                    def steps(m):
                        return bcast(m, 2, Q)

                    def chans(m):
                        return bcast(m[ps, :, js].rearrange("p k j -> p j k"), 3, SC)

                    br, bi = steps(bbar_r[ps, js, cols]), steps(bbar_i[ps, js, cols])
                    tmp = (cp_i[ps, :, :, cols] if half == 0 else spare[ps])
                    o_r, o_i = bp_r[half][ps, :, :, cols], bp_i[half][ps, :, :, cols]
                    link(TT(tmp, bi, chans(rev_i), ALU.mult))
                    link(TT(o_r, br, chans(rev_r), ALU.mult))
                    link(TT(o_r, o_r, tmp, ALU.subtract))
                    link(TT(tmp, br, chans(rev_i), ALU.mult))
                    link(TT(o_i, bi, chans(rev_r), ALU.mult))
                    last = TT(o_i, o_i, tmp, ALU.add)
                    last.then_inc(bp_ready, 1)

            def output_matrix(half, g):
                js = slice(HP * half, HP * half + HP)
                if half == 1:
                    v.wait_ge(y_mm, 1)
                ps, cols = slice(64 * g, 64 * g + 64), slice(SC * g, SC * g + SC)
                cr, ci = bcast(craw_r[ps, js], 2, Q), bcast(craw_i[ps, js], 2, Q)
                pr = bcast(pw_r[ps, 0:Q, js].rearrange("p k j -> p j k"), 3, SC)
                pi = bcast(pw_i[ps, 0:Q, js].rearrange("p k j -> p j k"), 3, SC)
                tmp, o_r, o_i = toep[ps, :, :, cols], cp_r[ps, :, :, cols], cp_i[ps, :, :, cols]
                link(TT(tmp, ci, pi, ALU.mult))
                link(TT(o_r, cr, pr, ALU.mult))
                link(TT(o_r, o_r, tmp, ALU.subtract))
                link(TT(tmp, ci, pr, ALU.mult))
                link(TT(o_i, cr, pi, ALU.mult))
                STT(o_i, o_i, -1.0, tmp, ALU.mult, ALU.subtract).then_inc(cp_ready, 1)

            def turn_tables(half):
                js = slice(HP * half, HP * half + HP)
                if half == 0:
                    v.wait_ge(bp_ready, 4)
                else:
                    v.wait_ge(w_ready, 1)
                link(nv.memset(cos_t[:, :, 0:1], 1.0))
                link(nv.memset(sin_t[:, :, 0:1], 0.0))
                for k in range(6):
                    n = 1 << k
                    er, ei = bcast(e_r[:, k, js], 2, n), bcast(e_i[:, k, js], 2, n)
                    c0, s0 = cos_t[:, :, 0:n], sin_t[:, :, 0:n]
                    c1_, s1_ = cos_t[:, :, n:2 * n], sin_t[:, :, n:2 * n]
                    link(TT(turn_a[:, :, 0:n], s0, ei, ALU.mult))
                    link(TT(turn_b[:, :, 0:n], c0, ei, ALU.mult))
                    link(TT(c1_, c0, er, ALU.mult))
                    link(TT(s1_, s0, er, ALU.mult))
                    link(TT(c1_, c1_, turn_a[:, :, 0:n], ALU.subtract))
                    link(TT(s1_, s1_, turn_b[:, :, 0:n], ALU.add))

            def scan(half):
                js = slice(HP * half, HP * half + HP)
                zr0, zi0, ta0, tb0 = z_r[half], z_i[half], tmp_a[half], tmp_b[half]
                v.wait_ge(v_mm, half + 1)
                link(nv.memset(zr0[:, :, 0:1], 0.0))
                link(nv.memset(zi0[:, :, 0:1], 0.0))
                vr = psum[:, 2:4, :].rearrange("p b (j c) -> p (b j) c", c=NCH)[:, :, 0:NCH - 1]
                vi = psum[:, 4:6, :].rearrange("p b (j c) -> p (b j) c", c=NCH)[:, :, 0:NCH - 1]
                co, si = cos_t[:, :, 1:NCH], sin_t[:, :, 1:NCH]
                zr, zi, ta, tb = (m[:, :, 1:NCH] for m in (zr0, zi0, ta0, tb0))
                link(TT(zr, vr, co, ALU.mult))
                link(TT(ta, vi, si, ALU.mult))
                link(TT(zi, vi, co, ALU.mult))
                TT(tb, vr, si, ALU.mult).then_inc(v_read, 1)
                v.wait_ge(v_read, half + 1)
                link(TT(zr, zr, ta, ALU.add))
                link(TT(zi, zi, tb, ALU.subtract))
                link(nv.memset(decay[:, :, 0:1], 0.0))
                link(nv.tensor_copy(decay[:, :, 1:NCH], bcast(mag[:, js], 2, NCH - 1)))
                flat = lambda m: m.rearrange("p j c -> p (j c)")
                link(nv.tensor_tensor_scan(flat(ta0), flat(decay), flat(zr0), 0.0, ALU.mult, ALU.add))
                link(nv.tensor_tensor_scan(flat(tb0), flat(decay), flat(zi0), 0.0, ALU.mult, ALU.add))
                link(TT(zr0, ta0, cos_t, ALU.mult))
                link(TT(decay, tb0, sin_t, ALU.mult))
                link(TT(zr0, zr0, decay, ALU.subtract))
                link(TT(zi0, ta0, sin_t, ALU.mult))
                link(TT(decay, tb0, cos_t, ALU.mult))
                TT(zi0, zi0, decay, ALU.add).then_inc(w_ready, 1)

            def maxima(b):
                v.wait_ge(sc_mm, b + 1)
                if b == 0:
                    v.wait_ge(bias_in, 64)
                if b >= 3:
                    v.wait_ge(pv_mm, b - 2)
                hs2 = slice(2 * b, 2 * b + 2)
                bank, s2, m2 = psum[:, 2 + 2 * (b % 2):4 + 2 * (b % 2), :], scores[b % 3], mxs[b % 2]
                link(TT(s2[:, :, 0:W], bank[:, :, 0:W], bias[:, hs2, W:2 * W], ALU.add))
                TT(s2[:, :, W:3 * W], bank[:, :, W:3 * W], bias[:, hs2, :], ALU.add).then_inc(sc_read, 1)
                v.wait_ge(sc_read, b + 1)
                link(nv.tensor_reduce(m2[:, :, 0], s2[:, :, 0:W], AX, ALU.max))
                link(nv.tensor_reduce(m2[:, :, 1], s2[:, :, W:3 * W], AX, ALU.max))
                sk = bcast(sinks[:, hs2], 2, 2)
                link(TT(m2[:, :, :], m2[:, :, :], sk, ALU.max))
                link(TT(esink[b % 2][:, :, :], sk, m2[:, :, :], ALU.subtract))
                TS(m2[:, :, :], m2[:, :, :], -1.0, None, ALU.mult).then_inc(sc_ready, 1)

            def normalise(b):
                s2, a2, r2 = scores[b % 3], sums[b % 2], recs[b % 2]
                v.wait_ge(probs, 5 * (b + 1))
                link(TT(a2[:, :, :], a2[:, :, :], esink[b % 2][:, :, :], ALU.add))
                link(nv.reciprocal(r2[:, :, :], a2[:, :, :]))
                for h in range(2):
                    TS(s2[:, h, 0:W], s2[:, h, 0:W], r2[:, h, 0:1], None, ALU.mult).then_inc(normed, 1)
                    TS(s2[:, h, W:3 * W], s2[:, h, W:3 * W], r2[:, h, 1:2], None, ALU.mult).then_inc(normed, 1)

            def skip(half):
                v.wait_ge(y_out, 16 * (half + 1))
                if half == 0:
                    v.wait_ge(consumed, N_WIN)
                for c in range(4 * half, 4 * half + 4):
                    y = y_first[:, c, :] if half == 0 else ssm[:, c, :]
                    ins = STT(ssm[:, c, :], uT[:, c, :], d_skip[:, c:c + 1], y, ALU.mult, ALU.add)
                    if c % 4 < 3:
                        link(ins)
                    else:
                        ins.then_inc(gelu_in, 1)

            spare = view(M0 + 16384, [HP, Q, SC])
            def square(c):
                v.wait_ge(pv_out, c + 1)
                TT(attn_sq[:, c, :], attnT[:, c, :], attnT[:, c, :], ALU.mult).then_inc(asq_ready, 1)

            input_matrix(0)
            output_matrix(0, 0)
            output_matrix(0, 1)
            input_matrix(1)
            turn_tables(0)
            scan(0)
            turn_tables(1)
            scan(1)
            for b in range(9):
                if b < 8:
                    maxima(b)
                if b >= 1:
                    normalise(b - 1)
                if b in (1, 3):
                    output_matrix(1, b // 2)
                if b == 6:
                    skip(0)
                if b >= 3:
                    square(b - 3)
            square(6)
            square(7)
            skip(1)

            v.wait_ge(asq_mm, 1)
            TS(attn_rs[:, :], psum[:, 6, 0:T], 1.0 / (NH * HD), EPS, ALU.mult, ALU.add).then_inc(asq_mm, 1)
            v.wait_ge(asq_rt, 1)
            link(nv.reciprocal(attn_rs[:, :], attn_rs[:, :]))
            for c in range(8):
                STT(mixT[:, c, :], attnT[:, c, :], g_attn[:, c:c + 1], attn_rs[:, :], ALU.mult, ALU.mult).then_inc(attn_out, 1)
            for c in range(8):
                v.wait_ge(glu_sig, c + 1)
                link(TT(sgate[:, c, :], ssm[:, c, :], sgate[:, c, :], ALU.mult))
                TT(ysq[:, c, :], sgate[:, c, :], sgate[:, c, :], ALU.mult).then_inc(ssq_ready, 1)
            v.wait_ge(ssq_mm, 1)
            TS(ssm_rs[:, :], psum[:, 7, 0:T], 1.0 / (G * SC), EPS, ALU.mult, ALU.add).then_inc(ssq_mm, 1)
            v.wait_ge(glu_mm, 8)
            v.wait_ge(ssq_rt, 1)
            link(nv.reciprocal(ssm_rs[:, :], ssm_rs[:, :]))
            for c in range(8):
                STT(mixT[:, 8 + c, :], sgate[:, c, :], g_ssm[:, c:c + 1], ssm_rs[:, :], ALU.mult, ALU.mult).then_inc(ssm_out, 1)

            v.wait_ge(x_again, 32)
            for k in range(N_OUT):
                v.wait_ge(consumed, N_WIN + N_GLU + k + 1)
                xs = x1[:, :, 256 * k:256 * (k + 1)]
                TT(xs, psum[:, 2 * (k % 2):2 * (k % 2) + TB, 0:256], xs, ALU.add).then_inc(x1_out, 1)
            v.wait_ge(x1_sq, TB * N_OUT)
            link(nv.tensor_reduce(stat[:, 16:18], tok_sq[:, :, :], AX, ALU.add))
            TS(stat[:, 18:20], stat[:, 16:18], 1.0 / D, EPS, ALU.mult, ALU.add).then_inc(x1_rt, 1)
            v.wait_ge(x1_sq, TB * N_OUT + 1)
            link(nv.reciprocal(stat[:, 22:24], stat[:, 20:22]))
            for b in range(TB):
                TS(h2[:, b, :], x1[:, b, :], stat[:, 22 + b:23 + b], None, ALU.mult).then_inc(h2_ready, 1)
            for c in (c for c in range(DC) if c // 2 % 2 == 1):
                v.wait_ge(h2_t, c // 2 + 1)
                TS(h2T[:, c, :], psum[:, c // 2, T * (c % 2):T * (c % 2) + T], g_ffn[:, c:c + 1], None, ALU.mult).then_inc(h2_out, 1)

            v.wait_ge(router_mm, 1)
            link(TT(lg[:, :, :], psum[:, 0, 0:TB * 36].rearrange("p (b n) -> p b n", b=TB), bcast(b_rt[:, :], 1, TB), ALU.add))

            def first_max(dst, src, m, tmp, n):
                link(nv.tensor_reduce(m, src, AX, ALU.max))
                link(TT(tmp, src, bcast(m, 2, n), ALU.is_equal))
                r = bcast(rev_iota[:, 0:n], 1, TB)
                link(TT(tmp, tmp, r, ALU.mult))
                link(nv.tensor_reduce(slot_t[:, :, 0], tmp, AX, ALU.max))
                link(TT(dst, r, bcast(slot_t[:, :, 0], 2, n), ALU.is_equal))

            first_max(g_one[:, :, :], lg[:, :, 0:NG], g_max[:, :, 0], t_a[:, :, :], NG)
            link(TT(gl_exp[:, :, :], lg[:, :, 0:NG], bcast(g_max[:, :, 0], 2, NG), ALU.subtract))
            link(TT(prod4.rearrange("p b e g -> p b g e"), lg[:, :, NG:].rearrange("p b (g e) -> p b g e", g=NG),
                    bcast(g_one[:, :, :], 3, EG), ALU.mult))
            link(nv.tensor_reduce(e_sel[:, :, :], prod4[:, :, :, :], AX, ALU.add))
            first_max(k_one[0][:, :, :], e_sel[:, :, :], m_top[:, :, 0], t_b[:, :, :], EG)
            link(STT(e_sel[:, :, :], k_one[0][:, :, :], NEG, e_sel[:, :, :], ALU.mult, ALU.add))
            first_max(k_one[1][:, :, :], e_sel[:, :, :], m_top[:, :, 1], t_b[:, :, :], EG)
            TT(m_diff[:, :, 0], m_top[:, :, 1], m_top[:, :, 0], ALU.subtract).then_inc(eexp, 1)
            for k in range(2):
                link(TT(one32[k].rearrange("p b (g e) -> p b g e", g=NG), bcast(g_one[:, :, :], 3, EG),
                        bcast(k_one[k][:, :, :], 2, NG), ALU.mult))
            TT(both[:, :, :], one32[0][:, :, :], one32[1][:, :, :], ALU.add).then_inc(onehot_ready, 1)
            v.wait_ge(gexp, 2)
            link(nv.tensor_reduce(g_p[:, :, 0], gl_exp[:, :, :], AX, ALU.add))
            link(nv.reciprocal(g_p[:, :, :], g_p[:, :, :]))
            link(TS(w_top[:, :, 0], m_diff[:, :, 0], 1.0, None, ALU.add))
            link(nv.reciprocal(w_top[:, :, 0], w_top[:, :, 0]))
            link(TT(w_top[:, :, 0], w_top[:, :, 0], g_p[:, :, 0], ALU.mult))
            link(TT(w_top[:, :, 1], w_top[:, :, 0], m_diff[:, :, 0], ALU.mult))
            v.wait_ge(count_mm, 1)
            v.wait_ge(logit, 3)
            link(nv.tensor_copy(counts[:, :], psum[:, 1, 0:NE]))
            link(nv.tensor_tensor_scan(base_end[:, :], ones[:, 0:NE], counts[:, :], 0.0, ALU.mult, ALU.add))
            link(TT(nxt[:, :], base_end[:, :], counts[:, :], ALU.subtract))
            link(nv.tensor_copy(base_i[:, :], nxt[:, :]))
            link(TT(slot_e[:, :, :], psum[:, 1, 64:64 + TB * NE].rearrange("p (b e) -> p b e", b=TB), bcast(nxt[:, :], 1, TB), ALU.add))
            for k in range(2):
                link(TT(one32[k][:, :, :], one32[k][:, :, :], slot_e[:, :, :], ALU.mult))
                link(nv.tensor_reduce(slot_t[:, :, k], one32[k][:, :, :], AX, ALU.add))
            for b in range(TB):
                link(TS(sel[:, b, :], iota_s[:, :], slot_t[:, b, 0:1], None, ALU.is_equal))
                link(TS(selw[:, b, :], iota_s[:, :], slot_t[:, b, 1:2], None, ALU.is_equal))
                sw = y_tmp[:, :]
                link(TS(sw, sel[:, b, :], w_top[:, b, 0:1], None, ALU.mult))
                link(TT(sel[:, b, :], sel[:, b, :], selw[:, b, :], ALU.add))
                STT(selw[:, b, :], selw[:, b, :], w_top[:, b, 1:2], sw, ALU.mult, ALU.add).then_inc(sel_ready, 1)
            b0 = big[:, 0, :]
            link(TS(xcum[:, :], counts[:, :], float(CAP), None, ALU.is_gt))
            for m in (2, 3):
                link(TS(b0, counts[:, :], float(m * CAP), None, ALU.is_gt))
                link(TT(xcum[:, :], xcum[:, :], b0, ALU.add))
            ends = big[:, 1, :]
            link(nv.tensor_tensor_scan(ends, ones[:, 0:NE], xcum[:, :], 0.0, ALU.mult, ALU.add))
            link(nv.tensor_copy(nx_i[:, :], ends[:, NE - 1:NE]))
            
            link(nv.tensor_copy(iota_e2[:, :], ends))
            link(TT(xcum[:, :], ends, xcum[:, :], ALU.subtract))
            jrow = bcast(iota_e[:, 0:XMAX], 2, NE)
            link(TT(big[:, :, :], bcast(xcum[:, :], 1, XMAX), jrow, ALU.is_le))
            link(TT(big2[:, :, :], bcast(iota_e2[:, :], 1, XMAX), jrow, ALU.is_gt))
            link(TT(big[:, :, :], big[:, :, :], big2[:, :, :], ALU.mult))
            link(TT(big2[:, :, :], big[:, :, :], bcast(iota_e[:, :], 1, XMAX), ALU.mult))
            link(nv.tensor_reduce(rowf[:, 0, :], big2[:, :, :], AX, ALU.add))
            link(nv.tensor_copy(xexp_i[:, :], rowf[:, 0, :]))
            link(TT(big2[:, :, :], jrow, bcast(xcum[:, :], 1, XMAX), ALU.subtract))
            link(TS(big2[:, :, :], big2[:, :, :], float(CAP), float(CAP), ALU.mult, ALU.add))
            link(TT(big2[:, :, :], big2[:, :, :], big[:, :, :], ALU.mult))
            link(nv.tensor_reduce(rowf[:, 1, :], big2[:, :, :], AX, ALU.add))
            link(TT(big2[:, :, :], big[:, :, :], bcast(counts[:, :], 1, XMAX), ALU.mult))
            link(nv.tensor_reduce(rowf[:, 2, :], big2[:, :, :], AX, ALU.add))
            link(TT(xlim[:, :], rowf[:, 2, :], rowf[:, 1, :], ALU.subtract))
            link(TT(big2[:, :, :], big[:, :, :], bcast(nxt[:, :], 1, XMAX), ALU.mult))
            link(nv.tensor_reduce(rowf[:, 2, :], big2[:, :, :], AX, ALU.add))
            link(TT(rowf[:, 2, :], rowf[:, 2, :], rowf[:, 1, :], ALU.add))
            link(nv.tensor_copy(xbase_i[:, :], rowf[:, 2, :]))
            v.wait_ge(wrow_mm, 1)
            link(nv.tensor_copy(wrow[:, 0:SLOTS], psum[:, 2, :]))
            v.wait_ge(selT_t, 1)
            nv.tensor_copy(selT[:, :, :], psum[:, 3:5, :].rearrange("p b (s t) -> p (b s) t", s=2)).then_inc(routed, 1)
            v.wait_ge(gather_mm, DC)
            v.wait_ge(y_zero, 3)
            v.wait_ge(routed, 1)

            def expert(block_no, base, limit):
                STT(wmask[:, :], iota_c[:, :], limit, wrow[:, bass.ds(base, CAP)], ALU.is_lt, ALU.mult).then_inc(mask_ready, 1)
                v.wait_ge(silu_ready, block_no + 1)
                TT(gated_h[64:128, :], psum[64:128, 0, :], gated_h[64:128, :], ALU.mult).then_inc(gated, 1)
                v.wait_ge(hidT_mm, block_no + 1)
                v.wait_ge(mask_ready, block_no + 1)
                TT(hid[:, :, :], psum[:, 1, :].rearrange("p (m t) -> p m t", m=4)[:, :, P - CAP:P], bcast(wmask[:, :], 1, 4),
                   ALU.mult).then_inc(hid_ready, 1)
                v.wait_ge(consumed, RING * block_no + (NPRE + 6))
                nv.tensor_copy(y_rows[:, 1, :], psum[:, 3, :]).then_inc(y_copied2, 1)
                for k in range(2):
                    v.wait_ge(yT_mm, 2 * block_no + (k + 1))
                    ys = y_sorted[:, 8 * k:8 * k + 8, bass.ds(base, CAP)].rearrange("p (h i) t -> p i h t", h=2)
                    TT(ys, psum[:, 4 + k, :].rearrange("p (i h t) -> p i h t", i=4, h=2), ys, ALU.add).then_inc(y_added, 1)

            with v.Fori(0, NE) as e:
                base = v.value_load(base_i[0:1, bass.ds(e, 1)], min_val=0, max_val=SLOTS)
                expert(e, base, counts[:, bass.ds(e, 1)])
            nx = v.value_load(nx_i[0:1, :], min_val=0, max_val=XMAX - 1)
            with v.If(nx > 0):
                with v.Fori(0, nx) as j:
                    base = v.value_load(xbase_i[0:1, bass.ds(j, 1)], min_val=0, max_val=SLOTS)
                    expert(j + NE, base, xlim[:, bass.ds(j, 1)])

            for k in range(1, 16, 2):
                v.wait_ge(yt_t, k + 1)
                nv.tensor_copy(y_tok[:, k // 4, 512 * (k % 4):512 * (k % 4) + 512], psum[:, k % 8, :]).then_inc(yt_dve, 1)
            for b in range(TB):
                for n in range(4):
                    v.wait_ge(comb_mm, 4 * b + n + 1)
                    xs = x1[:, b, 512 * n:512 * n + 512]
                    TT(xs, psum[:, 4 * b + n, :], xs, ALU.add).then_inc(comb_out, 1)
            for b in range(TB):
                v.wait_ge(fin_sq, 2 * b + 1)
                TS(stat[:, 26 + b:27 + b], stat[:, 24 + b:25 + b], 1.0 / D, EPS, ALU.mult, ALU.add).then_inc(fin_rt, 1)
                v.wait_ge(fin_sq, 2 * b + 2)
                link(nv.reciprocal(stat[:, 30 + b:31 + b], stat[:, 28 + b:29 + b]))
                if b == 0:
                    v.wait_ge(gfin_in, 16)
                STT(result[:, b, :], x1[:, b, :], stat[:, 30 + b:31 + b], g_fin[:, :], ALU.mult, ALU.mult).then_inc(fin_ready, 1)

        @block.tensor
        def _(pe):
            mm, tr = nc.tensor.matmul, nc.tensor.transpose

            pe.wait_ge(table_ready, 1)
            mm(psum[0:NH, 7, 0:384], table[0:33, :], onehot[0:33, :], start=True, stop=True).then_inc(row_done, 1)
            pe.wait_ge(const_ready, 2)
            pe.wait_ge(h_ready, 3)
            hv = x1.rearrange("p b (q c) -> p b c q", c=DC)
            for c in range(DC):
                if c == 14:
                    pe.wait_ge(row_out, 1)
                for b in range(TB):
                    last = tr(psum[:, c // 2, T * (c % 2) + P * b:T * (c % 2) + P * b + P], hv[:, b, c, :], ident[:, :])
                if c % 2:
                    last.then_inc(hT_t, 1)

            piece = [0]

            def take():
                n = piece[0]
                piece[0] += 1
                k = n % PRE
                pe.wait_ge(landed[k], 16 * (n // PRE + 1))
                return ring[k]

            def project(n):
                w = take().rearrange("p (c n) -> p c n", c=DC)
                if n >= 2:
                    pe.wait_ge(proj_out, n if n > 6 else n - 1)
                for m in range(2):
                    if n == 4 and m == 1:
                        break
                    for k in range(DC):
                        last = mm(psum[:, proj_bank(n), T * m:T * m + T], w[:, k, P * m:P * m + P], hT[:, k, :],
                                  start=(k == 0), stop=(k == DC - 1))
                if n == 4:
                    for b in range(TB):
                        for k in range(DC):
                            last = mm(psum[:, 0, T + P * b:T + P * b + P], hT[:, k, P * b:P * b + P], w[:, k, P:2 * P],
                                      start=(k == 0), stop=(k == DC - 1))
                last.then_inc(consumed, 1)

            pe.wait_ge(hT_ready, DC)
            for n in range(4):
                project(n)

            def ssm_transposes(half):
                pe.wait_ge(bp_ready, 2 * half + 2)
                for k in range(8):
                    if k >= 4:
                        pe.wait_ge(bt_out, 8 * half + k - 3)
                    elif half == 1:
                        pe.wait_ge(v_read, 1)
                    src = (bp_r if k % 2 == 0 else bp_i)[half]
                    for i in range(4):
                        last = tr(psum[:, 2 + k % 4, P * i:P * i + P],
                                  src[:, 4 * (k // 2) + i, :, :].rearrange("p s c -> p (s c)"), ident[:, :])
                    last.then_inc(bt_t, 1)

            def ssm_toeplitz(half):
                pe.wait_ge(cp_ready, 2 * half + 2)
                if half == 1:
                    pe.wait_ge(proj_out, 9)
                for k in range(4):
                    for part, (bb, cc) in enumerate(((bbar_r, cp_r), (bbar_i, cp_i))):
                        for i in range(4):
                            j = 4 * k + i
                            last = mm(psum[32 * i:32 * i + 32, 6 if half == 0 else 0, P * k:P * k + P], bb[:, HP * half + j, :],
                                      cc[:, j].rearrange("p s c -> p (s c)"), start=(part == 0), stop=(part == 1))
                last.then_inc(toep_mm, 1)

            def ssm_inject(half):
                pe.wait_ge(u4_ready, 8)
                pe.wait_ge(u4_act, 8)
                pe.wait_ge(bt_out, 8 * half + 8)
                for part, bt in enumerate((bt_r, bt_i)):
                    for j in range(HP):
                        last = mm(psum[:, 2 + 2 * part + j // 8, NCH * (j % 8):NCH * (j % 8) + NCH], bt[:, j, :],
                                  u4[:, HP * half + j, :], start=True, stop=True)
                last.then_inc(v_mm, 1)

            def ssm_output(half):
                pe.wait_ge(w_ready, half + 1)
                pe.wait_ge(toep_out, 16 * (half + 1))
                if half == 1:
                    pe.wait_ge(sc_read, 7)
                for j in range(HP):
                    o = psum[:, (6 if half == 0 else 2) + j // 8, NCH * (j % 8):NCH * (j % 8) + NCH]
                    mm(o, cp_r[:, j].rearrange("p s c -> p (s c)"), z_r[half][:, j, :], start=True, stop=False)
                    mm(o, cp_i[:, j].rearrange("p s c -> p (s c)"), z_i[half][:, j, :], start=False, stop=False)
                    last = mm(o, toep[:, j].rearrange("p s c -> p (s c)"), u4[:, HP * half + j, :], start=False, stop=True)
                last.then_inc(y_mm, 1)

            def attn_scores(b):
                pe.wait_ge(proj_out, 6 + b // 2)
                if b < 2:
                    pe.wait_ge(v_read, 2)
                else:
                    pe.wait_ge(sc_read, b - 1)
                for q0, n0, k0, n in ((0, 0, 0, W), (W, W, 0, 2 * W)):
                    for h in range(2):
                        ps = slice(64 * h, 64 * h + 64)
                        last = mm(psum[:, 2 + 2 * (b % 2) + h, n0:n0 + n], qT[ps, b, q0:q0 + W], kk[ps, b // 4, k0:k0 + n],
                                  start=True, stop=True)
                last.then_inc(sc_mm, 1)

            def attn_transposes(b):
                if b == 0:
                    pe.wait_ge(y_out, 16)
                for h in range(2):
                    pe.wait_ge(normed, 4 * b + 2 * h + 2)
                    for i in range(3):
                        last = tr(psum[:, 6 + h, W * i:W * i + W], scores[b % 3][:, h, W * i:W * i + W], ident[:, :])
                    last.then_inc(pt_t, 1)

            def attn_values(b):
                pe.wait_ge(pt_out, 2 * b + 2)
                if b >= 1:
                    pe.wait_ge(pv_out, b)
                kv = slice(HD * (b // 4), HD * (b // 4) + HD)
                for h in range(2):
                    mm(psum[64 * h:64 * h + 64, 1, 0:T], vv[:, 0, kv], scores[b % 3][:, h, 0:T], start=True, stop=False)
                for h in range(2):
                    last = mm(psum[64 * h:64 * h + 64, 1, W:T], vv[:, 1, kv], scores[b % 3][:, h, T:T + W],
                              start=False, stop=True)
                last.then_inc(pv_mm, 1)

            project(4)
            ssm_transposes(0)
            ssm_toeplitz(0)
            ssm_inject(0)
            project(5)
            project(6)
            ssm_transposes(1)
            ssm_inject(1)
            ssm_output(0)
            attn_scores(0)
            attn_scores(1)
            for b in range(8):
                if b + 2 < 8:
                    attn_scores(b + 2)
                attn_transposes(b)
                if b == 7:
                    ssm_output(1)
                attn_values(b)
                if b in (0, 2):
                    project(7 + b // 2)
                if b == 5:
                    ssm_toeplitz(1)
            for c in range(8):
                pe.wait_ge(asq_ready, c + 1)
                last = mm(psum[:, 6, 0:T], ones[:, :], attn_sq[:, c, :], start=(c == 0), stop=(c == 7))
            last.then_inc(asq_mm, 1)

            def glu(w, c, k0, k1):
                for k in range(k0, k1):
                    last = mm(psum[:, GLU_BANKS[c % 4], 0:T], w[:, k, P * (c % 4):P * (c % 4) + P], ssm[:, k, :],
                              start=(k == 0), stop=(k == 7))
                return last

            w = take().rearrange("p (c n) -> p c n", c=8)
            pe.wait_ge(toep_out, 32)
            pe.wait_ge(pv_out, 8)
            pe.wait_ge(sc_read, 8)
            for k0, half in ((0, 0), (4, 1)):
                pe.wait_ge(gelu_out, half + 1)
                for c in range(4):
                    last = glu(w, c, k0, k0 + 4)
                    if half == 1:
                        last.then_inc(glu_mm, 1)
            pe.wait_ge(glu_mm, 4)
            pe.nop().then_inc(consumed, 1)
            w = take().rearrange("p (c n) -> p c n", c=8)
            for c in range(4, 8):
                pe.wait_ge(glu_sig, c - 3)
                glu(w, c, 0, 8).then_inc(glu_mm, 1)
            pe.wait_ge(glu_mm, 8)
            pe.nop().then_inc(consumed, 1)
            for c in range(8):
                pe.wait_ge(ssq_ready, c + 1)
                last = mm(psum[:, 7, 0:T], ones[:, :], ysq[:, c, :], start=(c == 0), stop=(c == 7))
            last.then_inc(ssq_mm, 1)
            pe.wait_ge(attn_out, 8)
            pe.wait_ge(y_out, 32)
            pe.wait_ge(glu_sig, 8)

            def w_out(n, w, b, k0, k1):
                for k in range(k0, k1):
                    last = mm(psum[:, 2 * (n % 2) + b, 0:256], mixT[:, k, P * b:P * b + P], w[:, k, :],
                              start=(k == 0), stop=(k == DC - 1))
                return last

            for n in range(N_OUT):
                w = take().rearrange("p (c n) -> p c n", c=DC)
                if n >= 2:
                    pe.wait_ge(x1_out, n - 1)
                if n == 0:
                    for b in range(TB):
                        w_out(n, w, b, 0, 8)
                    pe.wait_ge(ssm_out, 8)
                for b in range(TB):
                    last = w_out(n, w, b, 8 if n == 0 else 0, DC)
                last.then_inc(consumed, 1)

            pe.wait_ge(h2_ready, 2)
            hv2 = h2.rearrange("p b (q c) -> p b c q", c=DC)
            for c in range(DC):
                for b in range(TB):
                    last = tr(psum[:, c // 2, T * (c % 2) + P * b:T * (c % 2) + P * b + P], hv2[:, b, c, :], ident[:, :])
                if c % 2:
                    last.then_inc(h2_t, 1)
            pe.wait_ge(h2_out, DC)
            pe.wait_ge(router_in, 16)
            for b in range(TB):
                for k in range(DC):
                    last = mm(psum[:, 0, 36 * b:36 * b + 36], h2T[:, k, P * b:P * b + P], wr[:, k, :],
                              start=(k == 0), stop=(k == DC - 1))
            last.then_inc(router_mm, 1)
            pe.wait_ge(onehot_ready, 1)
            pe.wait_ge(const_ready, 14)
            mm(psum[:, 1, 0:NE], ones[:, :], both[:, 0, :], start=True, stop=False)
            mm(psum[:, 1, 0:NE], ones[:, :], both[:, 1, :], start=False, stop=True)
            mm(psum[:, 1, 64:64 + NE], tri[:, :], both[:, 0, :], start=True, stop=True)
            mm(psum[:, 1, 96:96 + NE], tri[:, :], both[:, 1, :], start=True, stop=False)
            mm(psum[:, 1, 96:96 + NE], ones[:, :], both[:, 0, :], start=False, stop=True).then_inc(count_mm, 1)
            pe.wait_ge(sel_ready, 2)
            mm(psum[:, 2, :], ones[:, :], selw[:, 0, :], start=True, stop=False)
            mm(psum[:, 2, :], ones[:, :], selw[:, 1, :], start=False, stop=True).then_inc(wrow_mm, 1)
            for s in range(4):
                for b in range(TB):
                    last = tr(psum[:, 3 + s // 2, T * (s % 2) + P * b:T * (s % 2) + P * b + P], sel[:, b, P * s:P * s + P], ident[:, :])
            last.then_inc(selT_t, 1)
            for c in range(DC):
                if c >= 8:
                    pe.wait_ge(gather_act, c - 7)
                elif c == 4:
                    pe.wait_ge(routed, 1)
                for b in range(TB):
                    last = mm(psum[:, (c + 5) % 8, :], hv2[:, b, c, :], sel[:, b, :], start=(b == 0), stop=(b == TB - 1))
                last.then_inc(gather_mm, 1)
            pe.wait_ge(gather_act, DC)
            pe.wait_ge(routed, 1)
            pe.wait_ge(y_zero, 1)

            def expert(block_no, base):
                def weights(k):
                    pre = 16 * len([m for m in range(NPRE) if m % PRE == ring_of(k)]) if ring_of(k) < PRE else 0
                    pe.wait_ge(landed[ring_of(k)], 16 * block_no + (pre + 16))
                    return ring[ring_of(k)]

                pe.wait_ge(hs_ready, block_no + 1)
                for half, (kg, ku) in enumerate(((GATE_A, UP_A), (GATE_B, UP_B))):
                    wg = weights(kg).rearrange("p (c n) -> p c n", c=8)
                    wu = weights(ku).rearrange("p (c n) -> p c n", c=8)
                    for c in range(8):
                        st, sp_ = half == 0 and c == 0, half == 1 and c == 7
                        g = mm(psum[0:64, 0, :], hs[:, 8 * half + c, :], wg[:, c, :], start=st, stop=sp_)
                        u = mm(psum[64:128, 0, :], hs[:, 8 * half + c, :], wu[:, c, :], start=st, stop=sp_)
                    g.then_inc(consumed, 1)
                    u.then_inc(consumed, 1)
                pe.wait_ge(gated, block_no + 1)
                gv = gated_h[:, :].rearrange("p (q c) -> p c q", c=4)
                for c in range(4):
                    last = tr(psum[:, 1, P * c:P * c + P], gv[:, c, :], ident[:, :])
                last.then_inc(hidT_mm, 1)
                pe.wait_ge(hid_ready, block_no + 1)
                for half, k in enumerate((DOWN_A, DOWN_B)):
                    w = weights(k).rearrange("p (c n) -> p c n", c=2)
                    for c in range(2):
                        for n in range(4):
                            last = mm(psum[64 * (n % 2):64 * (n % 2) + 64, 2 + n // 2, :], hid[:, 2 * half + c, :],
                                      w[:, c, 512 * n:512 * n + 512], start=(half == 0 and c == 0), stop=(half == 1 and c == 1))
                    last.then_inc(consumed, 1)
                pe.wait_ge(y_copied, block_no + 1)
                pe.wait_ge(y_copied2, block_no + 1)
                for k in range(2):
                    for i in range(4):
                        last = tr(psum[:, 4 + k, P * i:P * i + P], y_rows[:, k, P * i:P * i + P], ident[:, :])
                    last.then_inc(yT_mm, 1)

            with pe.Fori(0, NE) as e:
                base = pe.value_load(base_i[0:1, bass.ds(e, 1)], min_val=0, max_val=SLOTS)
                expert(e, base)
            nx = pe.value_load(nx_i[0:1, :], min_val=0, max_val=XMAX - 1)
            with pe.If(nx > 0):
                with pe.Fori(0, nx) as j:
                    base = pe.value_load(xbase_i[0:1, bass.ds(j, 1)], min_val=0, max_val=SLOTS)
                    expert(j + NE, base)

            pe.wait_ge(y_added, 2 * (nx + NE))
            for k in range(16):
                s, n = k // 4, k % 4
                if k >= 8:
                    pe.wait_ge(yt_act if k % 2 == 0 else yt_dve, (k - 8) // 2 + 1)
                for i in range(4):
                    last = tr(psum[:, k % 8, P * i:P * i + P], y_sorted[:, 4 * n + i, P * s:P * s + P], ident[:, :])
                last.then_inc(yt_t, 1)
            pe.wait_ge(yt_act, 8)
            pe.wait_ge(yt_dve, 8)
            for b in range(TB):
                for n in range(4):
                    for s in range(4):
                        last = mm(psum[:, 4 * b + n, :], selT[:, s, P * b:P * b + P], y_tok[:, s, 512 * n:512 * n + 512],
                                  start=(s == 0), stop=(s == 3))
                    last.then_inc(comb_mm, 1)


def t5_onehot():
    import math
    import numpy as np

    buckets, half = 32, 16
    oh = np.zeros((buckets + 1, 3 * W), np.float32)
    for m in range(3 * W):
        n = 2 * W - 1 - m
        if not 0 <= n < W:
            oh[buckets, m] = 1.0
        elif n < half:
            oh[n, m] = 1.0
        else:
            oh[min(buckets - 1, half + int(math.log(n / half) / math.log(W / half) * half)), m] = 1.0
    return oh


def kernel(**inputs):
    import numpy as np
    import concourse.bacc as bacc
    from concourse.bass_utils import run_bass_kernel_spmd

    x = {k: np.asarray(v) for k, v in inputs.items()}
    col = lambda v: v.reshape(P, -1)
    chan = lambda v: v.reshape(-1, P).T
    state = lambda v: v.reshape(NPAIR, P).T
    arrays = {
        "x": x["x"].reshape(T, D), "table": x["rel_bias_table"], "onehot": t5_onehot(),
        "g_mix": col(x["g_norm_mix"]), "g_ffn": col(x["g_norm_ffn"]), "g_attn": chan(x["g_attn_out"]),
        "g_ssm": chan(x["g_ssm_out"]), "d_skip": chan(x["ssm_d"]), "b_glu": chan(x["b_glu"]),
        "lam_re": state(x["lam_re"]), "lam_im": state(x["lam_im"]), "log_dt": x["log_dt"].reshape(NPAIR, 2).T,
        "b_re": x["ssm_b_re"].reshape(NPAIR, P, SC).transpose(1, 0, 2),
        "b_im": x["ssm_b_im"].reshape(NPAIR, P, SC).transpose(1, 0, 2),
        "c_re": x["ssm_c_re"].reshape(NPAIR, 2, SC, NS).transpose(1, 3, 0, 2).reshape(P, NPAIR, SC),
        "c_im": x["ssm_c_im"].reshape(NPAIR, 2, SC, NS).transpose(1, 3, 0, 2).reshape(P, NPAIR, SC),
        "sinks": x["attn_sinks"].reshape(NH),
        "w_router": np.concatenate([x["w_router_group"][0], x["w_router_expert"][0].transpose(1, 0, 2).reshape(D, NE)],
                                   axis=1).reshape(P, DC, NG + NE),
        "b_router": np.concatenate([x["b_router_group"].reshape(-1), x["b_router_expert"].reshape(-1)]),
        "w_in": x["w_in"][0], "w_glu": x["w_glu"][0], "w_out": x["w_out"][0],
        "w_gate": x["w_gate"].reshape(NE, D, FF), "w_up": x["w_up"].reshape(NE, D, FF),
        "w_down": x["w_down"].reshape(NE, FF, D), "g_final": x["g_final"],
    }
    nc = bacc.Bacc("TRN2", target_bir_lowering=False, num_devices=1)
    feed, aps = {}, {}
    for name, v in arrays.items():
        v = np.ascontiguousarray(v)
        feed[f"in_{name}"] = v
        aps[name] = nc.dram_tensor(f"in_{name}", v.shape, mybir.dt.from_np(v.dtype), kind="ExternalInput").ap()
    out = nc.dram_tensor("out_block", (T, D), F32, kind="ExternalOutput").ap()
    hymba_block(nc, aps, out)
    r = run_bass_kernel_spmd(nc, [feed], core_ids=[0])
    return r.results[0]["out_block"].reshape(1, T, D)
```

```python
from contextlib import ExitStack

import concourse.bass as bass
from concourse import mybir

F32 = mybir.dt.float32
F32R = mybir.dt.float32r
I32 = mybir.dt.int32
ALU = mybir.AluOpType
ACT = mybir.ActivationFunctionType
AX = mybir.AxisListType.X

P = 128
D, T, TB = 2048, 256, 2
DC = D // P
NH, HD = 16, 64
W = 128
G, SC, NS = 64, 16, 64
NPAIR = G // 2
Q = 4
NCH = T // Q
HP = NPAIR // 2
NE, NG, EG, FF = 32, 4, 8, 512
SLOTS = 2 * T
CAP = 64
XMAX = SLOTS // CAP
PADDED = SLOTS + CAP
RING, SLOT = 6, 4096
PRE = 2
N_WIN, N_GLU, N_OUT = 9, 2, 8
NPRE = N_WIN + N_GLU + N_OUT
EPS = 1e-6
NEG = -1e30
PI = 3.14159265358979
MAGIC = 12582912.0
TWO_PI_HI = 6.28125
TWO_PI_LO = 2 * PI - TWO_PI_HI


def bcast(ap, axis, n):
    v = ap.unsqueeze(axis)
    shape = list(v.shape)
    shape[axis] = n
    return v.broadcast_to(shape)


class Count:

    def __init__(self, sem):
        self.sem, self.n = sem, 0

    def inc(self, ins, by=1):
        self.n += by
        ins.then_inc(self.sem, by)
        return self.n


def hymba_block(nc, a, out):
    with ExitStack() as ctx:
        def sem(name):
            return ctx.enter_context(nc.semaphore(name))

        with nc.sbuf_tensor("ring_mem", [P, RING * SLOT], F32) as ring_mem, \
                nc.sbuf_tensor("arena", [P, 2 * 9216 + 2 * 4096], F32) as arena:
            pass

        def over(name, floats, dt=F32):
            return ctx.enter_context(nc.sbuf_tensor(name, [P, floats], dt))

        over("ring_first", PRE * SLOT)
        w_parts = over("w_parts", (RING - PRE) * SLOT, F32R)
        over("before_parts", 9216)
        parts = over("parts", 2 * 4096, F32R)
        over("between", 1024 + 4096)
        sel_part = over("sel_part", 1024, F32R)
        over("after_sel", 3072)
        psum = ctx.enter_context(nc.psum_tensor("psum", [P, 8, 512], F32))
        skew = nc.dram_tensor("bias_skew", [NH, P, 384], F32, kind="Internal")

        def view(start, shape):
            n = 1
            for s in shape:
                n *= s
            v = ring_mem[:, start:start + n] if start < RING * SLOT else arena[:, start - RING * SLOT:start - RING * SLOT + n]
            if len(shape) > 1:
                names = ["a", "b", "c", "d"][:len(shape)]
                v = v.rearrange(f"p ({' '.join(names)}) -> p {' '.join(names)}",
                                **dict(zip(names[1:], shape[1:])))
            return v

        def small(name, shape, dt=F32):
            return ctx.enter_context(nc.sbuf_tensor(name, [P] + shape, dt))

        ssm_params = ctx.enter_context(nc.sbuf_tensor("ssm_params", [P, 42 * NPAIR], F32))
        at = [0]

        def param(*shape):
            n = 1
            for k in shape:
                n *= k
            v = ssm_params[:, at[0]:at[0] + n]
            at[0] += n
            return v.rearrange("p (k j) -> p k j", k=shape[0]) if len(shape) > 1 else v

        ring = [view(SLOT * k, [SLOT]) for k in range(RING)]
        C0 = PRE * SLOT
        bias = view(C0, [NH, 2 * W])
        scores = [view(C0 + 4096 + 768 * k, [2, 3 * W]) for k in range(3)]
        attnT = view(C0 + 6400, [8, T])
        kk = view(C0 + 8448, [2, T])
        vv = view(C0 + 8960, [TB, 2 * HD])
        bbar_r = view(C0 + 9216, [NPAIR, 2 * SC])
        bbar_i = view(C0 + 10240, [NPAIR, 2 * SC])
        craw_r = view(C0 + 11264, [NPAIR, SC])
        craw_i = view(C0 + 11776, [NPAIR, SC])
        BP1 = C0 + 12288
        braw_r = view(C0 + 6400, [NPAIR, SC])
        braw_i = view(C0 + 6912, [NPAIR, SC])
        onehot = view(C0 + 5120, [384])
        table = view(C0 + 5504, [NH])
        bias_row = view(C0 + 5632, [384])
        turn_a = view(C0 + 4096, [HP, NCH // 2])
        turn_b = view(C0 + 4608, [HP, NCH // 2])
        rstd_diag = view(C0 + 4096, [TB, P])
        attn_rs = view(C0 + 4096, [T])

        M0 = RING * SLOT
        u4 = view(M0, [NPAIR, NCH])
        BP = (M0 + 2048, BP1)
        bp_r = [view(b, [HP, Q, 2 * SC]) for b in BP]
        bp_i = [view(b + 2048, [HP, Q, 2 * SC]) for b in BP]
        z_r, z_i, tmp_a, tmp_b = ([view(b + 1024 * k, [HP, NCH]) for b in BP] for k in range(4))
        bt_r = view(M0 + 6144, [HP, P])
        bt_i = view(M0 + 8192, [HP, P])
        decay = view(M0 + 6144, [HP, NCH])
        cp_r = view(M0 + 10240, [HP, Q, 2 * SC])
        cp_i = view(M0 + 12288, [HP, Q, 2 * SC])
        toep = view(M0 + 14336, [HP, Q, 2 * SC])
        cos_sin = view(M0 + 16384, [D])
        cos_t = view(M0 + 16384, [HP, NCH])
        sin_t = view(M0 + 17408, [HP, NCH])
        full_tmp = view(M0 + 10240, [NPAIR, SC])

        x_squares = (view(M0, [D]), cos_sin)
        h_sorted = view(M0, [DC, PADDED])
        h2 = view(M0 + 9216, [TB, D])
        x1T = view(M0 + 9216 + 4096, [DC, T])
        h2_lo, h2_hi = (parts[:, 4096 * k:4096 * k + 4096].rearrange("p (b n) -> p b n", b=TB) for k in range(2))
        rt = M0 + 9216 + 8192
        wr = view(M0, [DC, NG + NE])

        R1 = M0 + 18432
        x1 = view(R1, [TB, D])
        uT = view(R1, [8, T])
        qT = view(R1 + 2048, [8, T])
        R2 = R1 + 4096
        hT = view(R2, [DC, T])
        mixT = view(R2, [DC, T])
        w_hi, w_lo = ([w_parts[:, SLOT * (2 * k + i):SLOT * (2 * k + i) + SLOT].rearrange("p (c n) -> p c n", c=DC)
                       for k in range(2)] for i in range(2))
        mix_hi, mix_lo = (parts[:, 4096 * i:4096 * i + 4096].rearrange("p (c t) -> p c t", c=DC) for i in range(2))
        x1_squares = view(M0 + 2048, [TB, D])
        sel = view(R2, [TB, SLOTS])
        sel_r = sel_part[:, :].rearrange("p (b n) -> p b n", b=TB)
        selw = view(R2 + 1024, [TB, SLOTS])
        wrow = view(R2 + 3072, [PADDED])
        keep = R2 + 3072 + PADDED
        hs = view(rt, [DC, CAP])
        gated_h = view(R2 + 1024, [FF])
        hid = view(R2 + 1536, [4, CAP])
        wmask = view(R2 + 1792, [CAP])
        g_fin = view(M0 + 9216, [D])
        result = view(M0 + 9216 + 2048, [TB, D])
        slot_row = view(R2 + 2560, [2, T])
        place = view(M0 + 9216 + 6144, [T])
        sgate = view(M0 + 4096, [8, T])
        ysq = view(M0 + 6144, [8, T])
        attn_sq = view(M0 + 8192, [8, T])
        ssm = view(R2 + 2048, [8, T])
        ssm_rs = view(M0 + 1024, [T])
        y_first = view(M0 + 7168, [4, T])

        ident, ones = small("ident", [P]), small("ones", [P])
        g_mix, g_ffn = small("g_mix", [DC]), small("g_ffn", [DC])
        g_attn, g_ssm = small("g_attn", [8]), small("g_ssm", [8])
        d_skip, b_glu = small("d_skip", [8]), small("b_glu", [8])
        sinks, b_rt = small("sinks", [NH]), small("b_rt", [NG + NE])
        lam_r, lam_i, dt = param(NPAIR), param(NPAIR), param(NPAIR)
        pw_r, pw_i = param(Q + 1, NPAIR), param(Q + 1, NPAIR)
        rev_r, rev_i = param(Q, NPAIR), param(Q, NPAIR)
        e_r, e_i = param(6, NPAIR), param(6, NPAIR)
        mag, ang, rot, sn, cs, c1, c2, c3, c4 = (param(NPAIR) for _ in range(9))
        y_rows = ssm_params[:, 0:2 * 512].rearrange("p (b n) -> p b n", b=2)
        slot_diag = ssm_params[:, 0:512].rearrange("p (k b n) -> p k b n", k=2, b=TB)
        stat = small("stat", [32])
        mxs, sums, recs, esink = ([small(f"{n}{k}", [2, 2]) for k in range(2)] for n in ("mxs", "sums", "recs", "esink"))
        tok_sq = small("tok_sq", [TB, N_OUT])

        landed = [sem(f"ring{k}_landed") for k in range(RING)]
        consumed = sem("ring_consumed")
        x_in, x_again = [sem("x_in0"), sem("x_in1")], sem("x_again")
        g_mix_in, small_in, ssm_in, t5_in = sem("g_mix_in"), sem("small_in"), sem("ssm_in"), sem("t5_in")
        router_in, gfin_in = sem("router_in"), sem("gfin_in")
        const_ready = sem("const_ready")
        pool_self = sem("pool_self")
        dve, act = sem("dve_self"), sem("act_self")
        x_sq = sem("x_sq")
        h_ready = sem("h_ready")
        xT_t, xT_out, rstd_mm, hT_ready = sem("xT_t"), sem("xT_out"), sem("rstd_mm"), sem("hT_ready")
        proj_out = sem("proj_out")
        table_ready, row_done, row_out, row_dma = sem("table_ready"), sem("row_done"), sem("row_out"), sem("row_dma")
        bias_in = sem("bias_in")
        ssm_mag, ssm_sin = sem("ssm_mag"), sem("ssm_sin")
        dt_ready, ang_ready = sem("dt_ready"), sem("ang_ready")
        u4_ready, u4_act = sem("u4_ready"), sem("u4_act")
        bp_ready, cp_ready = sem("bp_ready"), sem("cp_ready")
        bt_t, bt_out = sem("bt_t"), sem("bt_out")
        toep_zero, toep_mm, toep_out = sem("toep_zero"), sem("toep_mm"), sem("toep_out")
        v_mm, v_read = sem("v_mm"), sem("v_read")
        w_ready, y_mm, y_out = sem("w_ready"), sem("y_mm"), sem("y_out")
        sc_mm, sc_read, sc_ready = sem("sc_mm"), sem("sc_read"), sem("sc_ready")
        probs = sem("probs")
        normed, pt_t, pt_out, pv_mm, pv_out = (sem(n) for n in ("normed", "pt_t", "pt_out", "pv_mm", "pv_out"))
        asq_ready, asq_mm, asq_rt, attn_out = (sem(n) for n in ("asq_ready", "asq_mm", "asq_rt", "attn_out"))
        gelu_in, gelu_out = sem("gelu_in"), sem("gelu_out")
        glu_mm, glu_sig, ssq_ready, ssq_mm, ssq_rt, ssm_out = (sem(n) for n in (
            "glu_mm", "glu_sig", "ssq_ready", "ssq_mm", "ssq_rt", "ssm_out"))
        mix_hi_ready, mix_lo_ready, w_hi_ready, w_lo_ready = (sem(n) for n in (
            "mix_hi_ready", "mix_lo_ready", "w_hi_ready", "w_lo_ready"))
        x1_out, x1_sq, x1_rt, h2_ready = (sem(n) for n in (
            "x1_out", "x1_sq", "x1_rt", "h2_ready"))
        x1_t, x1T_out, router_mm = sem("x1_t"), sem("x1T_out"), sem("router_mm")
        logit, gexp, eexp = sem("logit"), sem("gexp"), sem("eexp")
        onehot_ready, count_mm, sel_ready, selw_ready, wrow_mm, diag_ready, slots_mm = (sem(n) for n in (
            "onehot_ready", "count_mm", "sel_ready", "selw_ready", "wrow_mm", "diag_ready", "slots_mm"))
        gather_act, routed, gather_mm, zeroed = (sem(n) for n in ("gather_act", "routed", "gather_mm", "zeroed"))
        hi_ready, lo_ready = sem("hi_ready"), sem("lo_ready")
        hs_ready, place_ready, mask_ready, silu_ready, gated, hidT_mm, hid_ready = (sem(n) for n in (
            "hs_ready", "place_ready", "mask_ready", "silu_ready", "gated", "hidT_mm", "hid_ready"))
        y_copied, y_copied2, comb_mm, summed = (sem(n) for n in ("y_copied", "y_copied2", "comb_mm", "summed"))
        fin_sq, fin_rt, fin_ready, stored = (sem(n) for n in ("fin_sq", "fin_rt", "fin_ready", "stored"))

        counts = view(keep, [NE])
        base_end = view(keep + 32, [NE])
        xlim = view(keep + 64, [XMAX])
        iota_c = view(keep + 72, [CAP])
        row_of = view(keep + 352, [NE])
        row_of_x = view(keep + 384, [XMAX])
        row_in = view(keep + 392, [1])
        itab = ctx.enter_context(nc.sbuf_tensor("itab", [P, 80], I32))
        base_i, xexp_i, xbase_i, nx_i = itab[:, 0:32], itab[:, 32:40], itab[:, 40:48], itab[:, 48:49]

        rs = lambda o, shape: view(rt + o, shape)
        lg = rs(0, [TB, NG + NE])
        iota_s = view(R2 + 2048, [SLOTS])
        rev_iota = small("rev_iota", [NE])
        iota_e = small("iota_e", [NE])

        gl_exp = rs(72, [TB, NG])
        m_diff = rs(80, [TB, 1])
        g_one = rs(84, [TB, NG])
        g_max = rs(92, [TB, 1])
        e_sel = rs(96, [TB, EG])
        k_one = [rs(112 + 16 * k, [TB, EG]) for k in range(2)]
        m_top = rs(144, [TB, 2])
        t_a, t_b = rs(148, [TB, NG]), rs(160, [TB, EG])
        g_p = rs(176, [TB, 1])
        w_top = rs(180, [TB, 2])
        one32 = [rs(192 + 64 * k, [TB, NE]) for k in range(2)]
        both = rs(320, [TB, NE])
        slot_e = rs(384, [TB, NE])
        slot_t = rs(448, [TB, 2])
        big = rs(512, [XMAX, NE])
        big2 = rs(768, [XMAX, NE])
        nxt, xcum = rs(456, [NE]), view(keep + 320, [NE])
        prod4 = rs(320, [TB, EG, NG])
        rowf = view(keep + 296, [3, XMAX])
        y_tmp = view(R2 + 3072, [SLOTS])
        iota_e2 = view(keep + 264, [NE])
        tri = view(keep + 136, [P])

        u4v = u4.rearrange("p (c q) t -> p q c t", q=4)
        uTs = uT.rearrange("p c (t s) -> p s c t", s=Q)

        block = ctx.enter_context(nc.Block())

        def glu_rows(k):
            return a["w_glu"].rearrange("(c p) n -> p c n", p=P)[:, :, 512 * k:512 * (k + 1)]

        proj_bank = lambda n: n % 2 if n < 6 else 0
        GLU_BANKS = (0, 1, 4, 5)
        GATHER_BANKS = (4, 5, 6, 7, 0, 1)

        W_IN_COLS = [1280 + 256 * k for k in range(4)] + [1024] + [256 * k for k in range(4)]

        def slot3(k, chunks):
            return ring[k].rearrange("p (c n) -> p c n", c=chunks)

        GATE_A, UP_A, GATE_B, UP_B, DOWN_A, DOWN_B = range(6)
        ring_of = lambda k: (PRE + k) % RING

        def expert_source(k, e):
            e1 = bass.ds(e, 1)
            if k in (GATE_A, GATE_B):
                return a["w_gate"].rearrange("e (p c) f -> e p c f", p=P)[e1, :, 8 * (k == GATE_B):8 * (k == GATE_B) + 8, :]
            if k in (UP_A, UP_B):
                return a["w_up"].rearrange("e (p c) f -> e p c f", p=P)[e1, :, 8 * (k == UP_B):8 * (k == UP_B) + 8, :]
            return a["w_down"].rearrange("e (p c) d -> e p c d", p=P)[e1, :, 2 * (k == DOWN_B):2 * (k == DOWN_B) + 2, :]

        @block.sync
        def _(sp):
            for b in range(TB):
                sp.dma_start(x1[:, b, :], a["x"][P * b:P * (b + 1), :]).then_inc(x_in[b], 16)

            def room(n):
                if n - PRE >= N_WIN + N_GLU:
                    sp.wait_ge(w_lo_ready, 2 * (n - PRE - N_WIN - N_GLU) + 2)
                elif n >= PRE:
                    sp.wait_ge(consumed, n - PRE + 1)

            n = 0
            for col in W_IN_COLS:
                room(n)
                sp.dma_start(slot3(n % PRE, DC), a["w_in"].rearrange("(p c) n -> p c n", p=P)[:, :, col:col + 256]
                             ).then_inc(landed[n % PRE], 16)
                n += 1
            for k in range(N_GLU):
                room(n)
                sp.dma_start(slot3(n % PRE, 8), glu_rows(k)).then_inc(landed[n % PRE], 16)
                n += 1
            for k in range(N_OUT):
                room(n)
                cols = slice(256 * k, 256 * (k + 1))
                sp.dma_start(slot3(n % PRE, DC), a["w_out"].rearrange("(c p) n -> p c n", p=P)[:, :, cols]).then_inc(landed[n % PRE], 16)
                n += 1
                if k == 0:
                    sp.wait_ge(gelu_in, 2)
                    sp.wait_ge(sc_mm, 8)
                    for b in range(TB):
                        sp.dma_start(x1[:, b, :], a["x"][P * b:P * (b + 1), :]).then_inc(x_again, 16)

            def fetch(e, block_no, first=False):
                for k in range(RING):
                    if first:
                        if k == 0:
                            sp.wait_ge(consumed, NPRE)
                    else:
                        sp.wait_ge(consumed, NPRE + RING * (block_no - 1) + k + 1)
                    chunks = 2 if k >= DOWN_A else 8
                    sp.dma_start(slot3(ring_of(k), chunks), expert_source(k, e)).then_inc(landed[ring_of(k)], 16)

            fetch(0, 0, first=True)
            with sp.Fori(1, NE) as e:
                fetch(e, e)
            sp.wait_ge(routed, 1)
            nx = sp.value_load(nx_i[0:1, :], min_val=0, max_val=XMAX - 1)
            with sp.If(nx > 0):
                with sp.Fori(0, nx) as j:
                    e = sp.value_load(xexp_i[0:1, bass.ds(j, 1)], min_val=0, max_val=NE - 1)
                    fetch(e, j + NE)
            for b in range(TB):
                sp.wait_ge(fin_ready, b + 1)
                sp.dma_start(out[P * b:P * (b + 1), :], result[:, b, :]).then_inc(stored, 16)
            sp.wait_ge(stored, 16 * TB)

        @block.gpsimd
        def _(pool):
            me = Count(pool_self)

            def link(ins):
                pool.wait_ge(pool_self, me.inc(ins))

            link(pool.memset(ident[:, :], 0.0))
            pool.affine_select(out=ident[:, :], in_=ident[:, :], compare_op=ALU.not_equal, fill=1.0, base=0,
                               pattern=[[-1, P]], channel_multiplier=1).then_inc(const_ready, 1)
            pool.memset(ones[:, :], 1.0).then_inc(const_ready, 1)
            pool.iota(iota_e[:, :], pattern=[[1, NE]], base=0, channel_multiplier=0,
                      allow_small_or_imprecise_dtypes=True).then_inc(const_ready, 1)
            pool.iota(rev_iota[:, :], pattern=[[-1, NE]], base=NE, channel_multiplier=0,
                      allow_small_or_imprecise_dtypes=True).then_inc(const_ready, 1)
            for m in (bbar_r, bbar_i, cp_r, cp_i, bp_r[0], bp_i[0], toep, bp_r[1], bp_i[1]):
                pool.memset(m[:], 0.0).then_inc(const_ready, 1)
            pool.wait_ge(row_out, 1)
            pool.dma_start(skew.ap(), bcast(bias_row[0:NH, :], 1, P)).then_inc(row_dma, 16)
            pool.wait_ge(row_dma, 16)
            for k in range(4):
                pool.dma_start(bias[:, 4 * k:4 * k + 4, :],
                               bass.AP(tensor=skew, offset=4 * k * P * 384 + P - 1,
                                       ap=[[383, P], [P * 384, 4], [1, 2 * W]])).then_inc(bias_in, 16)
            pool.wait_ge(proj_out, 4)
            pool.wait_ge(const_ready, 13)
            for q in range(2):
                for s in range(Q):
                    if q or s:
                        pool.wait_ge(u4_ready, Q * q + s)
                    pool.tensor_copy(u4v[32 * s:32 * s + 32, q], uTs[32 * q:32 * q + 32, s]).then_inc(u4_ready, 1)
            pool.wait_ge(u4_ready, 8)
            for half in range(2):
                pool.wait_ge(cp_ready, 2 * half + 2)
                pool.memset(toep[:], 0.0).then_inc(toep_zero, 1)
            pool.wait_ge(consumed, NPRE)
            link(pool.memset(tri[:, :], 1.0))
            pool.affine_select(out=tri[:, :], in_=tri[:, :], compare_op=ALU.is_gt, fill=0.0, base=0,
                               pattern=[[1, P]], channel_multiplier=-1).then_inc(const_ready, 1)
            pool.iota(iota_s[:, :], pattern=[[1, SLOTS]], base=0, channel_multiplier=0,
                      allow_small_or_imprecise_dtypes=True).then_inc(logit, 1)
            pool.iota(iota_c[:, :], pattern=[[1, CAP]], base=0, channel_multiplier=0,
                      allow_small_or_imprecise_dtypes=True).then_inc(logit, 1)
            pool.memset(wrow[:, SLOTS:PADDED], 0.0).then_inc(logit, 1)
            pool.wait_ge(router_mm, 1)
            for half in range(2):
                pool.wait_ge(logit, 3 + half)
                pool.iota(row_in[64 * half:64 * half + 64, :], pattern=[[0, 1]], base=0, channel_multiplier=1,
                          allow_small_or_imprecise_dtypes=True).then_inc(logit, 1)
            pool.wait_ge(logit, 5)
            for k in range(4):
                q4 = lambda m: m.rearrange("p b (q c) -> p b q c", c=DC)[:, :, :, 4 * k:4 * k + 4]
                pool.wait_ge(hi_ready, TB)
                pool.tensor_tensor(q4(h2_lo), q4(h2), q4(h2_hi), ALU.subtract).then_inc(lo_ready, 1)
            pool.memset(h_sorted[:, :, SLOTS:PADDED], 0.0).then_inc(zeroed, 1)
            pool.wait_ge(routed, 1)
            pool.memset(gated_h[0:64, :], 0.0).then_inc(zeroed, 1)
            pool.wait_ge(zeroed, 1)

            def window(base):
                pool.tensor_copy(hs[:, :, :], h_sorted[:, :, bass.ds(base, CAP)]).then_inc(hs_ready, 1)

            base = pool.value_load(base_i[0:1, 0:1], min_val=0, max_val=SLOTS)
            for k in range(4):
                cs4 = slice(4 * k, 4 * k + 4)
                pool.wait_ge(gather_act, 4 * k + 4)
                last = pool.tensor_copy(hs[:, cs4, :], h_sorted[:, cs4, bass.ds(base, CAP)])
            last.then_inc(hs_ready, 1)
            with pool.Fori(1, NE) as e:
                base = pool.value_load(base_i[0:1, bass.ds(e, 1)], min_val=0, max_val=SLOTS)
                pool.wait_ge(consumed, RING * e + (NPRE + 4 - RING))
                window(base)
            nx = pool.value_load(nx_i[0:1, :], min_val=0, max_val=XMAX - 1)
            with pool.If(nx > 0):
                with pool.Fori(0, nx) as j:
                    base = pool.value_load(xbase_i[0:1, bass.ds(j, 1)], min_val=0, max_val=SLOTS)
                    pool.wait_ge(consumed, RING * j + (NPRE + 4 + RING * (NE - 1)))
                    window(base)

        @block.scalar
        def _(sc):
            nc_s = nc.scalar
            me = Count(act)

            def link(ins):
                sc.wait_ge(act, me.inc(ins))

            sc.dma_start(g_mix[:, :], a["g_mix"]).then_inc(g_mix_in, 16)
            sc.dma_start(table[0:32, :], a["table"]).then_inc(t5_in, 16)
            sc.dma_start(onehot[0:33, :], a["onehot"]).then_inc(t5_in, 16)
            for name, tile in (("g_ffn", g_ffn), ("g_attn", g_attn), ("g_ssm", g_ssm),
                               ("d_skip", d_skip), ("b_glu", b_glu)):
                sc.dma_start(tile[:, :], a[name]).then_inc(small_in, 16)
            sc.dma_start(lam_r[:, :], a["lam_re"]).then_inc(ssm_in, 16)
            sc.dma_start(lam_i[:, :], a["lam_im"]).then_inc(ssm_in, 16)
            for g in range(2):
                sc.dma_start(dt[64 * g:64 * g + 64, :], a["log_dt"][g:g + 1, :].partition_broadcast(64)).then_inc(ssm_in, 16)
            for name, tile in (("b_re", braw_r), ("b_im", braw_i), ("c_re", craw_r), ("c_im", craw_i)):
                sc.dma_start(tile[:, :, :], a[name]).then_inc(ssm_in, 16)
            sc.dma_start(sinks[:, :], a["sinks"].partition_broadcast(P)).then_inc(small_in, 16)
            sc.dma_start(b_rt[:, :], a["b_router"].partition_broadcast(P)).then_inc(small_in, 16)

            sc.wait_ge(row_done, 1)
            nc_s.copy(bias_row[0:NH, :], psum[0:NH, 7, 0:384]).then_inc(row_out, 1)
            for b in range(TB):
                sc.wait_ge(x_in[b], 16)
                nc_s.activation(x_squares[b], x1[:, b, :], ACT.Square, accum_out=stat[:, b:b + 1]).then_inc(x_sq, 1)
            sc.wait_ge(h_ready, 1)
            nc_s.activation(stat[:, 4:6], stat[:, 2:4], ACT.Sqrt).then_inc(x_sq, 1)
            sc.wait_ge(ssm_in, 16 * 8)
            nc_s.activation(dt[:, :], dt[:, :], ACT.Exp).then_inc(dt_ready, 1)
            sc.wait_ge(ssm_mag, 1)
            nc_s.activation(mag[:, :], mag[:, :], ACT.Exp).then_inc(ssm_mag, 1)
            sc.wait_ge(ang_ready, 1)
            nc_s.activation(sn[:, :], ang[:, :], ACT.Sin).then_inc(ssm_sin, 1)
            nc_s.activation(cs[:, :], ang[:, :], ACT.Sin, scale=0.5).then_inc(ssm_sin, 1)
            for n in range(4):
                sc.wait_ge(consumed, n + 1)
                nc_s.copy(uT[:, 2 * n:2 * n + 2, :], psum[:, n % 2, :].rearrange("p (a b) -> p a b", a=2)).then_inc(proj_out, 1)
            sc.wait_ge(proj_out, 4)
            for q in range(2, 4):
                for s in range(Q):
                    nc_s.copy(u4v[32 * s:32 * s + 32, q], uTs[32 * q:32 * q + 32, s]).then_inc(u4_act, 1)

            def kv_piece():
                sc.wait_ge(consumed, 5)
                for half in range(2):
                    for g in range(2):
                        link(nc_s.copy(kk[64 * half:64 * half + 64, g, :], psum[64 * g:64 * g + 64, 0, 0:T]))
                nc_s.copy(vv[:, :, :], psum[:, 0, T:2 * T].rearrange("p (a b) -> p a b", a=2)).then_inc(proj_out, 1)

            def transposed_b(half):
                if half == 1:
                    sc.wait_ge(w_ready, 1)
                for k in range(8):
                    sc.wait_ge(bt_t, 8 * half + k + 1)
                    dst = (bt_r if k % 2 == 0 else bt_i)[:, 4 * (k // 2):4 * (k // 2) + 4, :]
                    nc_s.copy(dst, psum[:, 2 + k % 4, :].rearrange("p (a b) -> p a b", a=4)).then_inc(bt_out, 1)

            def toeplitz(half):
                sc.wait_ge(toep_zero, half + 1)
                sc.wait_ge(toep_mm, half + 1)
                tv = toep.rearrange("p (k i) t c -> p i k t c", i=4)
                for i in range(4):
                    src = psum[32 * i:32 * i + 32, 6 if half == 0 else 0, :].rearrange("p (k t c) -> p k t c", k=4, t=Q)
                    for s in range(Q):
                        nc_s.copy(tv[32 * s:32 * s + 32, i, :, s:Q, :].rearrange("p k t c -> p k (t c)"),
                                  src[:, :, 0:Q - s, :].rearrange("p k t c -> p k (t c)")).then_inc(toep_out, 1)

            def q_pieces(n0, n1):
                for n in range(n0, n1):
                    sc.wait_ge(consumed, n + 1)
                    c = 2 * (n - 5)
                    nc_s.mul(qT[:, c:c + 2, :], psum[:, proj_bank(n), :].rearrange("p (a b) -> p a b", a=2), HD ** -0.5).then_inc(proj_out, 1)

            def ssm_outputs(half):
                sc.wait_ge(y_mm, half + 1)
                bank = 6 if half == 0 else 2
                src = psum[:, bank:bank + 2, :].rearrange("p b (c q t) -> p q (b c) t", q=4, t=NCH)
                y = y_first if half == 0 else ssm[:, 4:8, :]
                for q in range(4):
                    for t in range(Q):
                        dst = y[32 * q:32 * q + 32, :, :].rearrange("p c (t s) -> p s c t", s=Q)[:, t]
                        nc_s.copy(dst, src[32 * t:32 * t + 32, q]).then_inc(y_out, 1)

            def exps(b):
                sc.wait_ge(sc_ready, b + 1)
                s2, m2, a2, e2 = scores[b % 3], mxs[b % 2], sums[b % 2], esink[b % 2]
                for h in range(2):
                    nc_s.activation(s2[:, h, 0:W], s2[:, h, 0:W], ACT.Exp, bias=m2[:, h, 0:1], accum_out=a2[:, h, 0:1]).then_inc(probs, 1)
                    nc_s.activation(s2[:, h, W:3 * W], s2[:, h, W:3 * W], ACT.Exp, bias=m2[:, h, 1:2], accum_out=a2[:, h, 1:2]).then_inc(probs, 1)
                nc_s.activation(e2[:, :, :], e2[:, :, :], ACT.Exp).then_inc(probs, 1)

            def probs_back(b):
                for h in range(2):
                    sc.wait_ge(pt_t, 2 * b + h + 1)
                    nc_s.copy(scores[b % 3][:, h, :], psum[:, 6 + h, 0:3 * W]).then_inc(pt_out, 1)

            def attn_rows(b):
                sc.wait_ge(pv_mm, b + 1)
                nc_s.copy(attnT[:, b, :], psum[:, 1, 0:T]).then_inc(pv_out, 1)

            def gelu(half):
                sc.wait_ge(gelu_in, half + 1)
                ys = ssm[:, 4 * half:4 * half + 4, :]
                nc_s.activation(ys, ys, ACT.Gelu_apprx_tanh).then_inc(gelu_out, 1)

            sc.wait_ge(small_in, 16 * 7)
            kv_piece()
            transposed_b(0)
            toeplitz(0)
            q_pieces(5, 7)
            transposed_b(1)
            ssm_outputs(0)
            for b in range(10):
                if b < 8:
                    exps(b)
                if b in (2, 4):
                    q_pieces(6 + b // 2, 7 + b // 2)
                if b == 7:
                    toeplitz(1)
                if b == 8:
                    gelu(0)
                if 1 <= b < 9:
                    probs_back(b - 1)
                if b >= 2:
                    attn_rows(b - 2)
            ssm_outputs(1)
            gelu(1)
            sc.wait_ge(asq_mm, 2)
            nc_s.activation(attn_rs[:, :], attn_rs[:, :], ACT.Sqrt).then_inc(asq_rt, 1)

            def split_weights(k):
                n = N_WIN + N_GLU + k
                sc.wait_ge(landed[n % PRE], 16 * (n // PRE + 1))
                if k >= 2:
                    sc.wait_ge(consumed, n - 1)
                for i in range(2):
                    half = slice(8 * i, 8 * i + 8)
                    nc_s.copy(w_hi[k % 2][:, half, :], slot3(n % PRE, DC)[:, half, :]).then_inc(w_hi_ready, 1)

            for i in range(2):
                sc.wait_ge(attn_out, 4 * i + 4)
                nc_s.copy(mix_hi[:, 4 * i:4 * i + 4, :], mixT[:, 4 * i:4 * i + 4, :]).then_inc(mix_hi_ready, 1)
            for c in range(8):
                sc.wait_ge(glu_mm, c + 1)
                nc_s.activation(sgate[:, c, :], psum[:, GLU_BANKS[c % 4], 0:T], ACT.Sigmoid, bias=b_glu[:, c:c + 1]).then_inc(glu_sig, 1)
                if c == 4:
                    split_weights(0)
            sc.wait_ge(ssq_mm, 2)
            nc_s.activation(ssm_rs[:, :], ssm_rs[:, :], ACT.Sqrt).then_inc(ssq_rt, 1)
            for i in range(4):
                sc.wait_ge(ssm_out, 2 * i + 2)
                nc_s.copy(mix_hi[:, 8 + 2 * i:10 + 2 * i, :], mixT[:, 8 + 2 * i:10 + 2 * i, :]).then_inc(mix_hi_ready, 1)
            split_weights(1)
            sc.wait_ge(ssm_out, 8)
            sc.dma_start(wr[:, :, :], a["w_router"]).then_inc(router_in, 16)

            for k in range(N_OUT):
                if k + 2 < N_OUT:
                    split_weights(k + 2)
                sc.wait_ge(x1_out, k + 1)
                for b in range(TB):
                    cols = slice(256 * k, 256 * (k + 1))
                    nc_s.activation(x1_squares[:, b, cols], x1[:, b, cols], ACT.Square, accum_out=tok_sq[:, b, k:k + 1]).then_inc(x1_sq, 1)
            sc.wait_ge(x1_rt, 1)
            nc_s.activation(stat[:, 20:22], stat[:, 18:20], ACT.Sqrt).then_inc(x1_sq, 1)
            for c in (c for c in range(DC) if c // 2 % 2 == 0):
                sc.wait_ge(x1_t, c // 2 + 1)
                nc_s.activation(x1T[:, c, :], psum[:, c // 2, T * (c % 2):T * (c % 2) + T], ACT.Copy, scale=g_ffn[:, c:c + 1]).then_inc(x1T_out, 1)
            sc.wait_ge(router_mm, 1)
            for b in range(TB):
                sc.wait_ge(h2_ready, b + 1)
                nc_s.copy(h2_hi[:, b, :], h2[:, b, :]).then_inc(hi_ready, 1)
            sc.wait_ge(eexp, 1)
            nc_s.activation(gl_exp[:, :, :], gl_exp[:, :, :], ACT.Exp).then_inc(gexp, 1)
            nc_s.activation(m_diff[:, :, :], m_diff[:, :, :], ACT.Exp).then_inc(gexp, 1)
            for c in range(DC):
                sc.wait_ge(gather_mm, c + 1)
                nc_s.activation(h_sorted[:, c, 0:SLOTS], psum[:, GATHER_BANKS[c % 6], :], ACT.Copy, scale=g_ffn[:, c:c + 1]).then_inc(gather_act, 1)

            sc.wait_ge(gather_mm, DC)
            sc.dma_start(g_fin[:, :], a["g_final"].partition_broadcast(P)).then_inc(gfin_in, 16)

            def expert(block_no):
                sc.wait_ge(consumed, RING * block_no + (NPRE + 4))
                nc_s.activation(gated_h[64:128, :], psum[0:64, 0, :], ACT.Silu).then_inc(silu_ready, 1)
                sc.wait_ge(consumed, RING * block_no + (NPRE + 6))
                nc_s.copy(y_rows[:, 0, :], psum[:, 2, :]).then_inc(y_copied, 1)

            with sc.Fori(0, NE) as e:
                expert(e)
            sc.wait_ge(routed, 1)
            nx = sc.value_load(nx_i[0:1, :], min_val=0, max_val=XMAX - 1)
            with sc.If(nx > 0):
                with sc.Fori(0, nx) as j:
                    expert(j + NE)
            for b in range(TB):
                sc.wait_ge(summed, 8 * nx + (8 * NE - 4 + 4 * b))
                nc_s.activation(result[:, b, :], x1[:, b, :], ACT.Square, accum_out=stat[:, 24 + b:25 + b]).then_inc(fin_sq, 1)
                sc.wait_ge(fin_rt, b + 1)
                nc_s.activation(stat[:, 28 + b:29 + b], stat[:, 26 + b:27 + b], ACT.Sqrt).then_inc(fin_sq, 1)

        @block.vector
        def _(v):
            me = Count(dve)
            nv = nc.vector

            def link(ins):
                v.wait_ge(dve, me.inc(ins))

            TT, TS, STT = nv.tensor_tensor, nv.tensor_scalar, nv.scalar_tensor_tensor

            v.wait_ge(t5_in, 32)
            nv.memset(table[32:33, :], NEG).then_inc(table_ready, 1)
            for c in range(DC):
                v.wait_ge(xT_t, c // 2 + 1)
                nv.tensor_copy(hT[:, c, :], psum[:, c // 2, T * (c % 2):T * (c % 2) + T]).then_inc(xT_out, 1)
            v.wait_ge(x_sq, 2)
            TS(stat[:, 2:4], stat[:, 0:2], 1.0 / D, EPS, ALU.mult, ALU.add).then_inc(h_ready, 1)
            v.wait_ge(x_sq, 3)
            link(nv.reciprocal(stat[:, 6:8], stat[:, 4:6]))
            v.wait_ge(const_ready, 1)
            for b in range(TB):
                TS(rstd_diag[:, b, :], ident[:, :], stat[:, 6 + b:7 + b], None, ALU.mult).then_inc(h_ready, 1)
            v.wait_ge(g_mix_in, 16)
            v.wait_ge(xT_out, DC)
            v.wait_ge(rstd_mm, 1)
            for c in range(DC):
                STT(hT[:, c, :], hT[:, c, :], g_mix[:, c:c + 1], psum[:, 7, 0:T], ALU.mult, ALU.mult).then_inc(hT_ready, 1)

            v.wait_ge(dt_ready, 1)
            TT(mag[:, :], lam_r[:, :], dt[:, :], ALU.mult).then_inc(ssm_mag, 1)
            link(TT(ang[:, :], lam_i[:, :], dt[:, :], ALU.mult))
            link(TS(c1[:, :], ang[:, :], 1.0 / (2 * PI), MAGIC, ALU.mult, ALU.add))
            link(TS(c1[:, :], c1[:, :], MAGIC, None, ALU.subtract))
            link(STT(ang[:, :], c1[:, :], -TWO_PI_HI, ang[:, :], ALU.mult, ALU.add))
            link(STT(ang[:, :], c1[:, :], -TWO_PI_LO, ang[:, :], ALU.mult, ALU.add))
            TS(ang[:, :], ang[:, :], 3.1415925, -3.1415925, ALU.min, ALU.max).then_inc(ang_ready, 1)
            v.wait_ge(ssm_sin, 2)
            v.wait_ge(ssm_mag, 2)
            link(TT(cs[:, :], cs[:, :], cs[:, :], ALU.mult))
            link(TS(cs[:, :], cs[:, :], -2.0, 1.0, ALU.mult, ALU.add))
            link(nv.memset(pw_r[:, 0, :], 1.0))
            link(nv.memset(pw_i[:, 0, :], 0.0))
            link(TT(pw_r[:, 1, :], mag[:, :], cs[:, :], ALU.mult))
            link(TT(pw_i[:, 1, :], mag[:, :], sn[:, :], ALU.mult))

            def cmul(or_, oi, ar, ai, br, bi, t1, t2):
                link(TT(t1, ai, bi, ALU.mult))
                link(TT(t2, ar, bi, ALU.mult))
                link(TT(oi, ai, br, ALU.mult))
                link(TT(or_, ar, br, ALU.mult))
                link(TT(or_, or_, t1, ALU.subtract))
                link(TT(oi, oi, t2, ALU.add))

            for k in range(2, Q + 1):
                cmul(pw_r[:, k, :], pw_i[:, k, :], pw_r[:, k - 1, :], pw_i[:, k - 1, :], pw_r[:, 1, :], pw_i[:, 1, :],
                     c1[:, :], c2[:, :])
            for k in range(Q):
                link(nv.tensor_copy(rev_r[:, k, :], pw_r[:, Q - k, :]))
                link(nv.tensor_copy(rev_i[:, k, :], pw_i[:, Q - k, :]))
            cmul(c3[:, :], c4[:, :], cs[:, :], sn[:, :], cs[:, :], sn[:, :], c1[:, :], c2[:, :])
            cmul(e_r[:, 0, :], e_i[:, 0, :], c3[:, :], c4[:, :], c3[:, :], c4[:, :], c1[:, :], c2[:, :])
            for k in range(1, 6):
                cmul(e_r[:, k, :], e_i[:, k, :], e_r[:, k - 1, :], e_i[:, k - 1, :], e_r[:, k - 1, :], e_i[:, k - 1, :],
                     c1[:, :], c2[:, :])
            link(TT(c1[:, :], lam_r[:, :], lam_r[:, :], ALU.mult))
            link(TT(c2[:, :], lam_i[:, :], lam_i[:, :], ALU.mult))
            link(TT(c1[:, :], c1[:, :], c2[:, :], ALU.add))
            link(nv.reciprocal(c1[:, :], c1[:, :]))
            link(TS(c2[:, :], pw_r[:, 1, :], -1.0, None, ALU.add))
            link(TT(rot[:, :], c2[:, :], lam_r[:, :], ALU.mult))
            link(TT(c3[:, :], pw_i[:, 1, :], lam_i[:, :], ALU.mult))
            link(TT(rot[:, :], rot[:, :], c3[:, :], ALU.add))
            link(TT(rot[:, :], rot[:, :], c1[:, :], ALU.mult))
            link(TT(sn[:, :], pw_i[:, 1, :], lam_r[:, :], ALU.mult))
            link(TT(c3[:, :], c2[:, :], lam_i[:, :], ALU.mult))
            link(TT(sn[:, :], sn[:, :], c3[:, :], ALU.subtract))
            link(TT(sn[:, :], sn[:, :], c1[:, :], ALU.mult))
            link(TT(mag[:, :], mag[:, :], mag[:, :], ALU.mult))
            link(TT(mag[:, :], mag[:, :], mag[:, :], ALU.mult))

            v.wait_ge(const_ready, 13)
            for g in range(2):
                ps, cols = slice(64 * g, 64 * g + 64), slice(SC * g, SC * g + SC)
                fr, fi = bcast(rot[ps, :], 2, SC), bcast(sn[ps, :], 2, SC)
                tmp = full_tmp[ps]
                link(TT(tmp, braw_i[ps], fi, ALU.mult))
                link(TT(bbar_r[ps, :, cols], braw_r[ps], fr, ALU.mult))
                link(TT(bbar_r[ps, :, cols], bbar_r[ps, :, cols], tmp, ALU.subtract))
                link(TT(tmp, braw_r[ps], fi, ALU.mult))
                link(TT(bbar_i[ps, :, cols], braw_i[ps], fr, ALU.mult))
                link(TT(bbar_i[ps, :, cols], bbar_i[ps, :, cols], tmp, ALU.add))
            link(nv.memset(cp_r[:], 0.0))

            def input_matrix(half):
                js = slice(HP * half, HP * half + HP)
                for g in range(2):
                    ps, cols = slice(64 * g, 64 * g + 64), slice(SC * g, SC * g + SC)

                    def steps(m):
                        return bcast(m, 2, Q)

                    def chans(m):
                        return bcast(m[ps, :, js].rearrange("p k j -> p j k"), 3, SC)

                    br, bi = steps(bbar_r[ps, js, cols]), steps(bbar_i[ps, js, cols])
                    tmp = (cp_i[ps, :, :, cols] if half == 0 else spare[ps])
                    o_r, o_i = bp_r[half][ps, :, :, cols], bp_i[half][ps, :, :, cols]
                    link(TT(tmp, bi, chans(rev_i), ALU.mult))
                    link(TT(o_r, br, chans(rev_r), ALU.mult))
                    link(TT(o_r, o_r, tmp, ALU.subtract))
                    link(TT(tmp, br, chans(rev_i), ALU.mult))
                    link(TT(o_i, bi, chans(rev_r), ALU.mult))
                    last = TT(o_i, o_i, tmp, ALU.add)
                    last.then_inc(bp_ready, 1)

            def output_matrix(half, g):
                js = slice(HP * half, HP * half + HP)
                if half == 1:
                    v.wait_ge(y_mm, 1)
                ps, cols = slice(64 * g, 64 * g + 64), slice(SC * g, SC * g + SC)
                cr, ci = bcast(craw_r[ps, js], 2, Q), bcast(craw_i[ps, js], 2, Q)
                pr = bcast(pw_r[ps, 0:Q, js].rearrange("p k j -> p j k"), 3, SC)
                pi = bcast(pw_i[ps, 0:Q, js].rearrange("p k j -> p j k"), 3, SC)
                tmp, o_r, o_i = toep[ps, :, :, cols], cp_r[ps, :, :, cols], cp_i[ps, :, :, cols]
                link(TT(tmp, ci, pi, ALU.mult))
                link(TT(o_r, cr, pr, ALU.mult))
                link(TT(o_r, o_r, tmp, ALU.subtract))
                link(TT(tmp, ci, pr, ALU.mult))
                link(TT(o_i, cr, pi, ALU.mult))
                STT(o_i, o_i, -1.0, tmp, ALU.mult, ALU.subtract).then_inc(cp_ready, 1)

            def turn_tables(half):
                js = slice(HP * half, HP * half + HP)
                if half == 0:
                    v.wait_ge(bp_ready, 4)
                else:
                    v.wait_ge(w_ready, 1)
                link(nv.memset(cos_t[:, :, 0:1], 1.0))
                link(nv.memset(sin_t[:, :, 0:1], 0.0))
                for k in range(6):
                    n = 1 << k
                    er, ei = bcast(e_r[:, k, js], 2, n), bcast(e_i[:, k, js], 2, n)
                    c0, s0 = cos_t[:, :, 0:n], sin_t[:, :, 0:n]
                    c1_, s1_ = cos_t[:, :, n:2 * n], sin_t[:, :, n:2 * n]
                    link(TT(turn_a[:, :, 0:n], s0, ei, ALU.mult))
                    link(TT(turn_b[:, :, 0:n], c0, ei, ALU.mult))
                    link(TT(c1_, c0, er, ALU.mult))
                    link(TT(s1_, s0, er, ALU.mult))
                    link(TT(c1_, c1_, turn_a[:, :, 0:n], ALU.subtract))
                    link(TT(s1_, s1_, turn_b[:, :, 0:n], ALU.add))

            def scan(half):
                js = slice(HP * half, HP * half + HP)
                zr0, zi0, ta0, tb0 = z_r[half], z_i[half], tmp_a[half], tmp_b[half]
                v.wait_ge(v_mm, half + 1)
                link(nv.memset(zr0[:, :, 0:1], 0.0))
                link(nv.memset(zi0[:, :, 0:1], 0.0))
                vr = psum[:, 2:4, :].rearrange("p b (j c) -> p (b j) c", c=NCH)[:, :, 0:NCH - 1]
                vi = psum[:, 4:6, :].rearrange("p b (j c) -> p (b j) c", c=NCH)[:, :, 0:NCH - 1]
                co, si = cos_t[:, :, 1:NCH], sin_t[:, :, 1:NCH]
                zr, zi, ta, tb = (m[:, :, 1:NCH] for m in (zr0, zi0, ta0, tb0))
                link(TT(zr, vr, co, ALU.mult))
                link(TT(ta, vi, si, ALU.mult))
                link(TT(zi, vi, co, ALU.mult))
                TT(tb, vr, si, ALU.mult).then_inc(v_read, 1)
                v.wait_ge(v_read, half + 1)
                link(TT(zr, zr, ta, ALU.add))
                link(TT(zi, zi, tb, ALU.subtract))
                link(nv.memset(decay[:, :, 0:1], 0.0))
                link(nv.tensor_copy(decay[:, :, 1:NCH], bcast(mag[:, js], 2, NCH - 1)))
                flat = lambda m: m.rearrange("p j c -> p (j c)")
                link(nv.tensor_tensor_scan(flat(ta0), flat(decay), flat(zr0), 0.0, ALU.mult, ALU.add))
                link(nv.tensor_tensor_scan(flat(tb0), flat(decay), flat(zi0), 0.0, ALU.mult, ALU.add))
                link(TT(zr0, ta0, cos_t, ALU.mult))
                link(TT(decay, tb0, sin_t, ALU.mult))
                link(TT(zr0, zr0, decay, ALU.subtract))
                link(TT(zi0, ta0, sin_t, ALU.mult))
                link(TT(decay, tb0, cos_t, ALU.mult))
                TT(zi0, zi0, decay, ALU.add).then_inc(w_ready, 1)

            def maxima(b):
                v.wait_ge(sc_mm, b + 1)
                if b == 0:
                    v.wait_ge(bias_in, 64)
                if b >= 3:
                    v.wait_ge(pv_mm, b - 2)
                hs2 = slice(2 * b, 2 * b + 2)
                bank, s2, m2 = psum[:, 2 + 2 * (b % 2):4 + 2 * (b % 2), :], scores[b % 3], mxs[b % 2]
                link(TT(s2[:, :, 0:W], bank[:, :, 0:W], bias[:, hs2, W:2 * W], ALU.add))
                TT(s2[:, :, W:3 * W], bank[:, :, W:3 * W], bias[:, hs2, :], ALU.add).then_inc(sc_read, 1)
                v.wait_ge(sc_read, b + 1)
                link(nv.tensor_reduce(m2[:, :, 0], s2[:, :, 0:W], AX, ALU.max))
                link(nv.tensor_reduce(m2[:, :, 1], s2[:, :, W:3 * W], AX, ALU.max))
                sk = bcast(sinks[:, hs2], 2, 2)
                link(TT(m2[:, :, :], m2[:, :, :], sk, ALU.max))
                link(TT(esink[b % 2][:, :, :], sk, m2[:, :, :], ALU.subtract))
                TS(m2[:, :, :], m2[:, :, :], -1.0, None, ALU.mult).then_inc(sc_ready, 1)

            def normalise(b):
                s2, a2, r2 = scores[b % 3], sums[b % 2], recs[b % 2]
                v.wait_ge(probs, 5 * (b + 1))
                link(TT(a2[:, :, :], a2[:, :, :], esink[b % 2][:, :, :], ALU.add))
                link(nv.reciprocal(r2[:, :, :], a2[:, :, :]))
                for h in range(2):
                    TS(s2[:, h, 0:W], s2[:, h, 0:W], r2[:, h, 0:1], None, ALU.mult).then_inc(normed, 1)
                    TS(s2[:, h, W:3 * W], s2[:, h, W:3 * W], r2[:, h, 1:2], None, ALU.mult).then_inc(normed, 1)

            def skip(half):
                v.wait_ge(y_out, 16 * (half + 1))
                if half == 0:
                    v.wait_ge(consumed, N_WIN)
                for c in range(4 * half, 4 * half + 4):
                    y = y_first[:, c, :] if half == 0 else ssm[:, c, :]
                    ins = STT(ssm[:, c, :], uT[:, c, :], d_skip[:, c:c + 1], y, ALU.mult, ALU.add)
                    if c % 4 < 3:
                        link(ins)
                    else:
                        ins.then_inc(gelu_in, 1)

            spare = view(M0 + 16384, [HP, Q, SC])
            def square(c):
                v.wait_ge(pv_out, c + 1)
                TT(attn_sq[:, c, :], attnT[:, c, :], attnT[:, c, :], ALU.mult).then_inc(asq_ready, 1)

            input_matrix(0)
            output_matrix(0, 0)
            output_matrix(0, 1)
            input_matrix(1)
            turn_tables(0)
            scan(0)
            turn_tables(1)
            scan(1)
            v.wait_ge(small_in, 16 * 7)
            for b in range(9):
                if b < 8:
                    maxima(b)
                if b >= 1:
                    normalise(b - 1)
                if b in (1, 3):
                    output_matrix(1, b // 2)
                if b == 6:
                    skip(0)
                if b >= 3:
                    square(b - 3)
            square(6)
            square(7)
            skip(1)

            v.wait_ge(asq_mm, 1)
            TS(attn_rs[:, :], psum[:, 6, 0:T], 1.0 / (NH * HD), EPS, ALU.mult, ALU.add).then_inc(asq_mm, 1)
            v.wait_ge(asq_rt, 1)
            link(nv.reciprocal(attn_rs[:, :], attn_rs[:, :]))
            for c in range(8):
                STT(mixT[:, c, :], attnT[:, c, :], g_attn[:, c:c + 1], attn_rs[:, :], ALU.mult, ALU.mult).then_inc(attn_out, 1)
            def mix_rest(c0, n, count):
                v.wait_ge(mix_hi_ready, count)
                TT(mix_lo[:, c0:c0 + n, :], mixT[:, c0:c0 + n, :], mix_hi[:, c0:c0 + n, :], ALU.subtract).then_inc(mix_lo_ready, 1)

            def weights_rest(k):
                n = N_WIN + N_GLU + k
                v.wait_ge(landed[n % PRE], 16 * (n // PRE + 1))
                for i in range(2):
                    half = slice(8 * i, 8 * i + 8)
                    v.wait_ge(w_hi_ready, 2 * k + i + 1)
                    TT(w_lo[k % 2][:, half, :], slot3(n % PRE, DC)[:, half, :], w_hi[k % 2][:, half, :], ALU.subtract
                       ).then_inc(w_lo_ready, 1)

            for i in range(2):
                mix_rest(4 * i, 4, i + 1)
            for c in range(8):
                v.wait_ge(glu_sig, c + 1)
                link(TT(sgate[:, c, :], ssm[:, c, :], sgate[:, c, :], ALU.mult))
                TT(ysq[:, c, :], sgate[:, c, :], sgate[:, c, :], ALU.mult).then_inc(ssq_ready, 1)
                if c == 4:
                    weights_rest(0)
            v.wait_ge(ssq_mm, 1)
            TS(ssm_rs[:, :], psum[:, 7, 0:T], 1.0 / (G * SC), EPS, ALU.mult, ALU.add).then_inc(ssq_mm, 1)
            v.wait_ge(glu_mm, 8)
            v.wait_ge(ssq_rt, 1)
            link(nv.reciprocal(ssm_rs[:, :], ssm_rs[:, :]))
            for c in range(8):
                STT(mixT[:, 8 + c, :], sgate[:, c, :], g_ssm[:, c:c + 1], ssm_rs[:, :], ALU.mult, ALU.mult).then_inc(ssm_out, 1)
            for i in range(4):
                mix_rest(8 + 2 * i, 2, 3 + i)
            weights_rest(1)

            v.wait_ge(x_again, 32)
            for k in range(N_OUT):
                v.wait_ge(consumed, N_WIN + N_GLU + k + 1)
                xs = x1[:, :, 256 * k:256 * (k + 1)]
                TT(xs, psum[:, 2 * (k % 2):2 * (k % 2) + TB, 0:256], xs, ALU.add).then_inc(x1_out, 1)
                if k + 2 < N_OUT:
                    weights_rest(k + 2)
            v.wait_ge(x1_sq, TB * N_OUT)
            link(nv.tensor_reduce(stat[:, 16:18], tok_sq[:, :, :], AX, ALU.add))
            TS(stat[:, 18:20], stat[:, 16:18], 1.0 / D, EPS, ALU.mult, ALU.add).then_inc(x1_rt, 1)
            for c in (c for c in range(DC) if c // 2 % 2 == 1):
                v.wait_ge(x1_t, c // 2 + 1)
                TS(x1T[:, c, :], psum[:, c // 2, T * (c % 2):T * (c % 2) + T], g_ffn[:, c:c + 1], None, ALU.mult).then_inc(x1T_out, 1)
            v.wait_ge(x1_sq, TB * N_OUT + 1)
            link(nv.reciprocal(stat[:, 22:24], stat[:, 20:22]))
            for b in range(TB):
                TS(h2[:, b, :], x1[:, b, :], stat[:, 22 + b:23 + b], None, ALU.mult).then_inc(h2_ready, 1)

            v.wait_ge(router_mm, 1)
            for b in range(TB):
                link(STT(lg[:, b, :], psum[:, 0, 36 * b:36 * b + 36], stat[:, 22 + b:23 + b], b_rt[:, :], ALU.mult, ALU.add))

            def first_max(dst, src, m, tmp, n):
                link(nv.tensor_reduce(m, src, AX, ALU.max))
                link(TT(tmp, src, bcast(m, 2, n), ALU.is_equal))
                r = bcast(rev_iota[:, 0:n], 1, TB)
                link(TT(tmp, tmp, r, ALU.mult))
                link(nv.tensor_reduce(slot_t[:, :, 0], tmp, AX, ALU.max))
                link(TT(dst, r, bcast(slot_t[:, :, 0], 2, n), ALU.is_equal))

            first_max(g_one[:, :, :], lg[:, :, 0:NG], g_max[:, :, 0], t_a[:, :, :], NG)
            link(TT(gl_exp[:, :, :], lg[:, :, 0:NG], bcast(g_max[:, :, 0], 2, NG), ALU.subtract))
            link(TT(prod4.rearrange("p b e g -> p b g e"), lg[:, :, NG:].rearrange("p b (g e) -> p b g e", g=NG),
                    bcast(g_one[:, :, :], 3, EG), ALU.mult))
            link(nv.tensor_reduce(e_sel[:, :, :], prod4[:, :, :, :], AX, ALU.add))
            first_max(k_one[0][:, :, :], e_sel[:, :, :], m_top[:, :, 0], t_b[:, :, :], EG)
            link(STT(e_sel[:, :, :], k_one[0][:, :, :], NEG, e_sel[:, :, :], ALU.mult, ALU.add))
            first_max(k_one[1][:, :, :], e_sel[:, :, :], m_top[:, :, 1], t_b[:, :, :], EG)
            TT(m_diff[:, :, 0], m_top[:, :, 1], m_top[:, :, 0], ALU.subtract).then_inc(eexp, 1)
            for k in range(2):
                link(TT(one32[k].rearrange("p b (g e) -> p b g e", g=NG), bcast(g_one[:, :, :], 3, EG),
                        bcast(k_one[k][:, :, :], 2, NG), ALU.mult))
            TT(both[:, :, :], one32[0][:, :, :], one32[1][:, :, :], ALU.add).then_inc(onehot_ready, 1)
            v.wait_ge(gexp, 2)
            link(nv.tensor_reduce(g_p[:, :, 0], gl_exp[:, :, :], AX, ALU.add))
            link(nv.reciprocal(g_p[:, :, :], g_p[:, :, :]))
            link(TS(w_top[:, :, 0], m_diff[:, :, 0], 1.0, None, ALU.add))
            link(nv.reciprocal(w_top[:, :, 0], w_top[:, :, 0]))
            link(TT(w_top[:, :, 0], w_top[:, :, 0], g_p[:, :, 0], ALU.mult))
            link(TT(w_top[:, :, 1], w_top[:, :, 0], m_diff[:, :, 0], ALU.mult))
            v.wait_ge(count_mm, 1)
            v.wait_ge(logit, 5)
            link(nv.tensor_copy(counts[:, :], psum[:, 1, 0:NE]))
            link(nv.tensor_tensor_scan(base_end[:, :], ones[:, 0:NE], counts[:, :], 0.0, ALU.mult, ALU.add))
            link(TT(nxt[:, :], base_end[:, :], counts[:, :], ALU.subtract))
            link(nv.tensor_copy(base_i[:, :], nxt[:, :]))
            link(TT(slot_e[:, :, :], psum[:, 1, 64:64 + TB * NE].rearrange("p (b e) -> p b e", b=TB), bcast(nxt[:, :], 1, TB), ALU.add))
            for k in range(2):
                link(TT(one32[k][:, :, :], one32[k][:, :, :], slot_e[:, :, :], ALU.mult))
                link(nv.tensor_reduce(slot_t[:, :, k], one32[k][:, :, :], AX, ALU.add))
            for b in range(TB):
                link(TS(sel[:, b, :], iota_s[:, :], slot_t[:, b, 0:1], None, ALU.is_equal))
            for b in range(TB):
                STT(sel_r[:, b, :], iota_s[:, :], slot_t[:, b, 1:2], sel[:, b, :], ALU.is_equal, ALU.add).then_inc(sel_ready, 1)
            for b in range(TB):
                if b > 0:
                    v.wait_ge(selw_ready, b)
                link(TS(y_tmp[:, :], iota_s[:, :], slot_t[:, b, 0:1], w_top[:, b, 0:1], ALU.is_equal, ALU.mult))
                link(TS(selw[:, b, :], iota_s[:, :], slot_t[:, b, 1:2], w_top[:, b, 1:2], ALU.is_equal, ALU.mult))
                TT(selw[:, b, :], selw[:, b, :], y_tmp[:, :], ALU.add).then_inc(selw_ready, 1)
            for k in range(2):
                for b in range(TB):
                    TS(slot_diag[:, k, b, :], ident[:, :], slot_t[:, b, k:k + 1], None, ALU.mult).then_inc(diag_ready, 1)
            b0 = big[:, 0, :]
            link(TS(xcum[:, :], counts[:, :], float(CAP), None, ALU.is_gt))
            for m in (2, 3):
                link(TS(b0, counts[:, :], float(m * CAP), None, ALU.is_gt))
                link(TT(xcum[:, :], xcum[:, :], b0, ALU.add))
            ends = big[:, 1, :]
            link(nv.tensor_tensor_scan(ends, ones[:, 0:NE], xcum[:, :], 0.0, ALU.mult, ALU.add))
            link(nv.tensor_copy(nx_i[:, :], ends[:, NE - 1:NE]))
            link(nv.tensor_copy(iota_e2[:, :], ends))
            link(TT(xcum[:, :], ends, xcum[:, :], ALU.subtract))
            jrow = bcast(iota_e[:, 0:XMAX], 2, NE)
            link(TT(big[:, :, :], bcast(xcum[:, :], 1, XMAX), jrow, ALU.is_le))
            link(TT(big2[:, :, :], bcast(iota_e2[:, :], 1, XMAX), jrow, ALU.is_gt))
            link(TT(big[:, :, :], big[:, :, :], big2[:, :, :], ALU.mult))
            link(TT(big2[:, :, :], big[:, :, :], bcast(iota_e[:, :], 1, XMAX), ALU.mult))
            link(nv.tensor_reduce(rowf[:, 0, :], big2[:, :, :], AX, ALU.add))
            link(nv.tensor_copy(xexp_i[:, :], rowf[:, 0, :]))
            link(TT(big2[:, :, :], jrow, bcast(xcum[:, :], 1, XMAX), ALU.subtract))
            link(TS(big2[:, :, :], big2[:, :, :], float(CAP), float(CAP), ALU.mult, ALU.add))
            link(TT(big2[:, :, :], big2[:, :, :], big[:, :, :], ALU.mult))
            link(nv.tensor_reduce(rowf[:, 1, :], big2[:, :, :], AX, ALU.add))
            link(TT(big2[:, :, :], big[:, :, :], bcast(counts[:, :], 1, XMAX), ALU.mult))
            link(nv.tensor_reduce(rowf[:, 2, :], big2[:, :, :], AX, ALU.add))
            link(TT(xlim[:, :], rowf[:, 2, :], rowf[:, 1, :], ALU.subtract))
            link(TT(big2[:, :, :], big[:, :, :], bcast(nxt[:, :], 1, XMAX), ALU.mult))
            link(nv.tensor_reduce(rowf[:, 2, :], big2[:, :, :], AX, ALU.add))
            link(TT(rowf[:, 2, :], rowf[:, 2, :], rowf[:, 1, :], ALU.add))
            link(nv.tensor_copy(xbase_i[:, :], rowf[:, 2, :]))
            v.wait_ge(wrow_mm, 1)
            link(nv.tensor_copy(wrow[:, 0:SLOTS], psum[:, 2, :]))
            link(TS(row_of[:, :], nxt[:, :], row_in[:, :], None, ALU.add))
            link(TS(row_of_x[:, :], rowf[:, 2, :], row_in[:, :], None, ALU.add))
            v.wait_ge(slots_mm, 1)
            nv.tensor_copy(slot_row[:, :, :], psum[:, 3, :].rearrange("p (k t) -> p k t", k=2)).then_inc(routed, 1)
            v.wait_ge(gather_mm, DC)
            v.wait_ge(zeroed, 2)
            v.wait_ge(routed, 1)

            def expert(block_no, base, limit, row):
                TS(place[:, :], slot_row[:, 0, :], row, None, ALU.is_equal).then_inc(place_ready, 1)
                v.wait_ge(place_ready, 2 * block_no + 1)
                STT(place[:, :], slot_row[:, 1, :], row, place[:, :], ALU.is_equal, ALU.add).then_inc(place_ready, 1)
                STT(wmask[:, :], iota_c[:, :], limit, wrow[:, bass.ds(base, CAP)], ALU.is_lt, ALU.mult).then_inc(mask_ready, 1)
                v.wait_ge(silu_ready, block_no + 1)
                TT(gated_h[64:128, :], psum[64:128, 0, :], gated_h[64:128, :], ALU.mult).then_inc(gated, 1)
                v.wait_ge(hidT_mm, block_no + 1)
                v.wait_ge(mask_ready, block_no + 1)
                TT(hid[:, :, :], psum[:, 1, :].rearrange("p (m t) -> p m t", m=4)[:, :, P - CAP:P], bcast(wmask[:, :], 1, 4),
                   ALU.mult).then_inc(hid_ready, 1)
                v.wait_ge(consumed, RING * block_no + (NPRE + 6))
                nv.tensor_copy(y_rows[:, 1, :], psum[:, 3, :]).then_inc(y_copied2, 1)
                for b in range(TB):
                    for n in range(4):
                        v.wait_ge(comb_mm, 8 * block_no + (4 * b + n + 1))
                        xs = x1[:, b, 512 * n:512 * n + 512]
                        TT(xs, psum[:, 4 + n, :], xs, ALU.add).then_inc(summed, 1)

            with v.Fori(0, NE) as e:
                base = v.value_load(base_i[0:1, bass.ds(e, 1)], min_val=0, max_val=SLOTS)
                expert(e, base, counts[:, bass.ds(e, 1)], row_of[:, bass.ds(e, 1)])
            nx = v.value_load(nx_i[0:1, :], min_val=0, max_val=XMAX - 1)
            with v.If(nx > 0):
                with v.Fori(0, nx) as j:
                    base = v.value_load(xbase_i[0:1, bass.ds(j, 1)], min_val=0, max_val=SLOTS)
                    expert(j + NE, base, xlim[:, bass.ds(j, 1)], row_of_x[:, bass.ds(j, 1)])

            for b in range(TB):
                v.wait_ge(fin_sq, 2 * b + 1)
                TS(stat[:, 26 + b:27 + b], stat[:, 24 + b:25 + b], 1.0 / D, EPS, ALU.mult, ALU.add).then_inc(fin_rt, 1)
                v.wait_ge(fin_sq, 2 * b + 2)
                link(nv.reciprocal(stat[:, 30 + b:31 + b], stat[:, 28 + b:29 + b]))
                if b == 0:
                    v.wait_ge(gfin_in, 16)
                STT(result[:, b, :], x1[:, b, :], stat[:, 30 + b:31 + b], g_fin[:, :], ALU.mult, ALU.mult).then_inc(fin_ready, 1)

        @block.tensor
        def _(pe):
            mm, tr = nc.tensor.matmul, nc.tensor.transpose

            pe.wait_ge(table_ready, 1)
            mm(psum[0:NH, 7, 0:384], table[0:33, :], onehot[0:33, :], start=True, stop=True).then_inc(row_done, 1)
            pe.wait_ge(const_ready, 2)
            for b in range(TB):
                pe.wait_ge(x_in[b], 16)
            hv = x1.rearrange("p b (q c) -> p b c q", c=DC)
            for c in range(DC):
                if c == 14:
                    pe.wait_ge(row_out, 1)
                for b in range(TB):
                    last = tr(psum[:, c // 2, T * (c % 2) + P * b:T * (c % 2) + P * b + P], hv[:, b, c, :], ident[:, :])
                if c % 2:
                    last.then_inc(xT_t, 1)
            pe.wait_ge(xT_out, DC)
            pe.wait_ge(h_ready, 3)
            for b in range(TB):
                last = mm(psum[:, 7, P * b:P * b + P], ones[:, :], rstd_diag[:, b, :], start=True, stop=True)
            last.then_inc(rstd_mm, 1)

            piece = [0]

            def take():
                n = piece[0]
                piece[0] += 1
                k = n % PRE
                pe.wait_ge(landed[k], 16 * (n // PRE + 1))
                return ring[k]

            def project(n):
                w = take().rearrange("p (c n) -> p c n", c=DC)
                if n >= 2:
                    pe.wait_ge(proj_out, n if n > 6 else n - 1)
                for m in range(2):
                    if n == 4 and m == 1:
                        break
                    for k in range(DC):
                        if n == m == 0:
                            pe.wait_ge(hT_ready, k + 1)
                        last = mm(psum[:, proj_bank(n), T * m:T * m + T], w[:, k, P * m:P * m + P], hT[:, k, :],
                                  start=(k == 0), stop=(k == DC - 1))
                if n == 4:
                    for b in range(TB):
                        for k in range(DC):
                            last = mm(psum[:, 0, T + P * b:T + P * b + P], hT[:, k, P * b:P * b + P], w[:, k, P:2 * P],
                                      start=(k == 0), stop=(k == DC - 1))
                last.then_inc(consumed, 1)

            for n in range(4):
                project(n)

            def ssm_transposes(half):
                pe.wait_ge(bp_ready, 2 * half + 2)
                for k in range(8):
                    if k >= 4:
                        pe.wait_ge(bt_out, 8 * half + k - 3)
                    elif half == 1:
                        pe.wait_ge(v_read, 1)
                    src = (bp_r if k % 2 == 0 else bp_i)[half]
                    for i in range(4):
                        last = tr(psum[:, 2 + k % 4, P * i:P * i + P],
                                  src[:, 4 * (k // 2) + i, :, :].rearrange("p s c -> p (s c)"), ident[:, :])
                    last.then_inc(bt_t, 1)

            def ssm_toeplitz(half):
                pe.wait_ge(cp_ready, 2 * half + 2)
                if half == 1:
                    pe.wait_ge(proj_out, 9)
                for k in range(4):
                    for part, (bb, cc) in enumerate(((bbar_r, cp_r), (bbar_i, cp_i))):
                        for i in range(4):
                            j = 4 * k + i
                            last = mm(psum[32 * i:32 * i + 32, 6 if half == 0 else 0, P * k:P * k + P], bb[:, HP * half + j, :],
                                      cc[:, j].rearrange("p s c -> p (s c)"), start=(part == 0), stop=(part == 1))
                last.then_inc(toep_mm, 1)

            def ssm_inject(half):
                pe.wait_ge(u4_ready, 8)
                pe.wait_ge(u4_act, 8)
                pe.wait_ge(bt_out, 8 * half + 8)
                for part, bt in enumerate((bt_r, bt_i)):
                    for j in range(HP):
                        last = mm(psum[:, 2 + 2 * part + j // 8, NCH * (j % 8):NCH * (j % 8) + NCH], bt[:, j, :],
                                  u4[:, HP * half + j, :], start=True, stop=True)
                last.then_inc(v_mm, 1)

            def ssm_output(half):
                pe.wait_ge(w_ready, half + 1)
                pe.wait_ge(toep_out, 16 * (half + 1))
                if half == 1:
                    pe.wait_ge(sc_read, 7)
                for j in range(HP):
                    o = psum[:, (6 if half == 0 else 2) + j // 8, NCH * (j % 8):NCH * (j % 8) + NCH]
                    mm(o, cp_r[:, j].rearrange("p s c -> p (s c)"), z_r[half][:, j, :], start=True, stop=False)
                    mm(o, cp_i[:, j].rearrange("p s c -> p (s c)"), z_i[half][:, j, :], start=False, stop=False)
                    last = mm(o, toep[:, j].rearrange("p s c -> p (s c)"), u4[:, HP * half + j, :], start=False, stop=True)
                last.then_inc(y_mm, 1)

            def attn_scores(b):
                pe.wait_ge(proj_out, 6 + b // 2)
                if b < 2:
                    pe.wait_ge(v_read, 2)
                else:
                    pe.wait_ge(sc_read, b - 1)
                for q0, n0, k0, n in ((0, 0, 0, W), (W, W, 0, 2 * W)):
                    for h in range(2):
                        ps = slice(64 * h, 64 * h + 64)
                        last = mm(psum[:, 2 + 2 * (b % 2) + h, n0:n0 + n], qT[ps, b, q0:q0 + W], kk[ps, b // 4, k0:k0 + n],
                                  start=True, stop=True)
                last.then_inc(sc_mm, 1)

            def attn_transposes(b):
                if b == 0:
                    pe.wait_ge(y_out, 16)
                for h in range(2):
                    pe.wait_ge(normed, 4 * b + 2 * h + 2)
                    for i in range(3):
                        last = tr(psum[:, 6 + h, W * i:W * i + W], scores[b % 3][:, h, W * i:W * i + W], ident[:, :])
                    last.then_inc(pt_t, 1)

            def attn_values(b):
                pe.wait_ge(pt_out, 2 * b + 2)
                if b >= 1:
                    pe.wait_ge(pv_out, b)
                kv = slice(HD * (b // 4), HD * (b // 4) + HD)
                for h in range(2):
                    mm(psum[64 * h:64 * h + 64, 1, 0:T], vv[:, 0, kv], scores[b % 3][:, h, 0:T], start=True, stop=False)
                for h in range(2):
                    last = mm(psum[64 * h:64 * h + 64, 1, W:T], vv[:, 1, kv], scores[b % 3][:, h, T:T + W],
                              start=False, stop=True)
                last.then_inc(pv_mm, 1)

            project(4)
            ssm_transposes(0)
            ssm_toeplitz(0)
            ssm_inject(0)
            project(5)
            project(6)
            ssm_transposes(1)
            ssm_inject(1)
            ssm_output(0)
            attn_scores(0)
            attn_scores(1)
            for b in range(8):
                if b + 2 < 8:
                    attn_scores(b + 2)
                attn_transposes(b)
                if b == 7:
                    ssm_output(1)
                attn_values(b)
                if b in (0, 2):
                    project(7 + b // 2)
                if b == 5:
                    ssm_toeplitz(1)
            for c in range(8):
                pe.wait_ge(asq_ready, c + 1)
                last = mm(psum[:, 6, 0:T], ones[:, :], attn_sq[:, c, :], start=(c == 0), stop=(c == 7))
            last.then_inc(asq_mm, 1)

            def glu(w, c, k0, k1):
                for k in range(k0, k1):
                    last = mm(psum[:, GLU_BANKS[c % 4], 0:T], w[:, k, P * (c % 4):P * (c % 4) + P], ssm[:, k, :],
                              start=(k == 0), stop=(k == 7))
                return last

            w = take().rearrange("p (c n) -> p c n", c=8)
            pe.wait_ge(toep_out, 32)
            pe.wait_ge(pv_out, 8)
            pe.wait_ge(sc_read, 8)
            for k0, half in ((0, 0), (4, 1)):
                pe.wait_ge(gelu_out, half + 1)
                for c in range(4):
                    last = glu(w, c, k0, k0 + 4)
                    if half == 1:
                        last.then_inc(glu_mm, 1)
            pe.wait_ge(glu_mm, 4)
            pe.nop().then_inc(consumed, 1)
            w = take().rearrange("p (c n) -> p c n", c=8)
            for c in range(4, 8):
                pe.wait_ge(glu_sig, c - 3)
                glu(w, c, 0, 8).then_inc(glu_mm, 1)
            pe.wait_ge(glu_mm, 8)
            pe.nop().then_inc(consumed, 1)
            for c in range(8):
                pe.wait_ge(ssq_ready, c + 1)
                last = mm(psum[:, 7, 0:T], ones[:, :], ysq[:, c, :], start=(c == 0), stop=(c == 7))
            last.then_inc(ssq_mm, 1)
            pe.wait_ge(attn_out, 8)
            pe.wait_ge(y_out, 32)
            pe.wait_ge(glu_sig, 8)

            def w_out(n, b, k0, k1):
                hi, lo = w_hi[n % 2], w_lo[n % 2]
                o = psum[:, 2 * (n % 2) + b, 0:256]
                for k in range(k0, k1):
                    t = slice(P * b, P * b + P)
                    mm(o, mix_hi[:, k, t], hi[:, k, :], start=(k == 0), stop=False)
                    mm(o, mix_hi[:, k, t], lo[:, k, :], start=False, stop=False)
                    last = mm(o, mix_lo[:, k, t], hi[:, k, :], start=False, stop=(k == DC - 1))
                return last

            for n in range(N_OUT):
                pe.wait_ge(w_lo_ready, 2 * n + 2)
                if n >= 2:
                    pe.wait_ge(x1_out, n - 1)
                if n == 0:
                    pe.wait_ge(mix_lo_ready, 2)
                    for b in range(TB):
                        w_out(n, b, 0, 8)
                    pe.wait_ge(mix_lo_ready, 6)
                for b in range(TB):
                    last = w_out(n, b, 8 if n == 0 else 0, DC)
                last.then_inc(consumed, 1)

            pe.wait_ge(x1_out, N_OUT)
            xv = x1.rearrange("p b (q c) -> p b c q", c=DC)
            for c in range(DC):
                for b in range(TB):
                    last = tr(psum[:, c // 2, T * (c % 2) + P * b:T * (c % 2) + P * b + P], xv[:, b, c, :], ident[:, :])
                if c % 2:
                    last.then_inc(x1_t, 1)
            pe.wait_ge(x1T_out, DC)
            pe.wait_ge(router_in, 16)
            for b in range(TB):
                for k in range(DC):
                    last = mm(psum[:, 0, 36 * b:36 * b + 36], x1T[:, k, P * b:P * b + P], wr[:, k, :],
                              start=(k == 0), stop=(k == DC - 1))
            last.then_inc(router_mm, 1)
            pe.wait_ge(onehot_ready, 1)
            pe.wait_ge(const_ready, 14)
            mm(psum[:, 1, 0:NE], ones[:, :], both[:, 0, :], start=True, stop=False)
            mm(psum[:, 1, 0:NE], ones[:, :], both[:, 1, :], start=False, stop=True)
            mm(psum[:, 1, 64:64 + NE], tri[:, :], both[:, 0, :], start=True, stop=True)
            mm(psum[:, 1, 96:96 + NE], tri[:, :], both[:, 1, :], start=True, stop=False)
            mm(psum[:, 1, 96:96 + NE], ones[:, :], both[:, 0, :], start=False, stop=True).then_inc(count_mm, 1)
            pe.wait_ge(sel_ready, 2)
            pe.wait_ge(hi_ready, TB)
            h2_split = [m.rearrange("p b (q c) -> p b c q", c=DC) for m in (h2_hi, h2_lo)]
            for c in range(DC):
                if c % 4 == 0:
                    pe.wait_ge(lo_ready, c // 4 + 1)
                if c >= 6:
                    pe.wait_ge(gather_act, c - 5)
                for k, m in enumerate(h2_split):
                    for b in range(TB):
                        last = mm(psum[:, GATHER_BANKS[c % 6], :], m[:, b, c, :], sel_r[:, b, :], start=(k == b == 0), stop=(k == b == 1))
                last.then_inc(gather_mm, 1)
                if c == 7:
                    pe.wait_ge(selw_ready, 2)
                    mm(psum[:, 2, :], ones[:, :], selw[:, 0, :], start=True, stop=False)
                    mm(psum[:, 2, :], ones[:, :], selw[:, 1, :], start=False, stop=True).then_inc(wrow_mm, 1)
                    pe.wait_ge(diag_ready, 4)
                    for k in range(2):
                        for b in range(TB):
                            last = mm(psum[:, 3, T * k + P * b:T * k + P * b + P], ones[:, :], slot_diag[:, k, b, :],
                                      start=True, stop=True)
                    last.then_inc(slots_mm, 1)
            pe.wait_ge(gather_act, DC)
            pe.wait_ge(routed, 1)
            pe.wait_ge(zeroed, 1)

            def expert(block_no):
                def weights(k):
                    pre = 16 * len([m for m in range(NPRE) if m % PRE == ring_of(k)]) if ring_of(k) < PRE else 0
                    pe.wait_ge(landed[ring_of(k)], 16 * block_no + (pre + 16))
                    return ring[ring_of(k)]

                pe.wait_ge(hs_ready, block_no + 1)
                for half, (kg, ku) in enumerate(((GATE_A, UP_A), (GATE_B, UP_B))):
                    wg = weights(kg).rearrange("p (c n) -> p c n", c=8)
                    wu = weights(ku).rearrange("p (c n) -> p c n", c=8)
                    for c in range(8):
                        st, sp_ = half == 0 and c == 0, half == 1 and c == 7
                        g = mm(psum[0:64, 0, :], hs[:, 8 * half + c, :], wg[:, c, :], start=st, stop=sp_)
                        u = mm(psum[64:128, 0, :], hs[:, 8 * half + c, :], wu[:, c, :], start=st, stop=sp_)
                    g.then_inc(consumed, 1)
                    u.then_inc(consumed, 1)
                pe.wait_ge(gated, block_no + 1)
                gv = gated_h[:, :].rearrange("p (q c) -> p c q", c=4)
                for c in range(4):
                    last = tr(psum[:, 1, P * c:P * c + P], gv[:, c, :], ident[:, :])
                last.then_inc(hidT_mm, 1)
                pe.wait_ge(hid_ready, block_no + 1)
                for half, k in enumerate((DOWN_A, DOWN_B)):
                    w = weights(k).rearrange("p (c n) -> p c n", c=2)
                    for c in range(2):
                        for n in range(4):
                            last = mm(psum[64 * (n % 2):64 * (n % 2) + 64, 2 + n // 2, :], hid[:, 2 * half + c, :],
                                      w[:, c, 512 * n:512 * n + 512], start=(half == 0 and c == 0), stop=(half == 1 and c == 1))
                    last.then_inc(consumed, 1)
                pe.wait_ge(y_copied, block_no + 1)
                pe.wait_ge(y_copied2, block_no + 1)
                pe.wait_ge(place_ready, 2 * block_no + 2)
                for b in range(TB):
                    for n in range(4):
                        if b > 0:
                            pe.wait_ge(summed, 8 * block_no + (4 * (b - 1) + n + 1))
                        ps = slice(64 * (n % 2), 64 * (n % 2) + 64)
                        mm(psum[:, 4 + n, :], place[ps, P * b:P * b + P], y_rows[ps, n // 2, :],
                           start=True, stop=True).then_inc(comb_mm, 1)

            with pe.Fori(0, NE) as e:
                expert(e)
            nx = pe.value_load(nx_i[0:1, :], min_val=0, max_val=XMAX - 1)
            with pe.If(nx > 0):
                with pe.Fori(0, nx) as j:
                    expert(j + NE)


def t5_onehot():
    import math
    import numpy as np

    buckets, half = 32, 16
    oh = np.zeros((buckets + 1, 3 * W), np.float32)
    for m in range(3 * W):
        n = 2 * W - 1 - m
        if not 0 <= n < W:
            oh[buckets, m] = 1.0
        elif n < half:
            oh[n, m] = 1.0
        else:
            oh[min(buckets - 1, half + int(math.log(n / half) / math.log(W / half) * half)), m] = 1.0
    return oh


def kernel(**inputs):
    import numpy as np
    import concourse.bacc as bacc
    from concourse.bass_utils import run_bass_kernel_spmd

    x = {k: np.asarray(v) for k, v in inputs.items()}
    col = lambda v: v.reshape(P, -1)
    chan = lambda v: v.reshape(-1, P).T
    state = lambda v: v.reshape(NPAIR, P).T
    arrays = {
        "x": x["x"].reshape(T, D), "table": x["rel_bias_table"], "onehot": t5_onehot(),
        "g_mix": col(x["g_norm_mix"]), "g_ffn": col(x["g_norm_ffn"]), "g_attn": chan(x["g_attn_out"]),
        "g_ssm": chan(x["g_ssm_out"]), "d_skip": chan(x["ssm_d"]), "b_glu": chan(x["b_glu"]),
        "lam_re": state(x["lam_re"]), "lam_im": state(x["lam_im"]), "log_dt": x["log_dt"].reshape(NPAIR, 2).T,
        "b_re": x["ssm_b_re"].reshape(NPAIR, P, SC).transpose(1, 0, 2),
        "b_im": x["ssm_b_im"].reshape(NPAIR, P, SC).transpose(1, 0, 2),
        "c_re": x["ssm_c_re"].reshape(NPAIR, 2, SC, NS).transpose(1, 3, 0, 2).reshape(P, NPAIR, SC),
        "c_im": x["ssm_c_im"].reshape(NPAIR, 2, SC, NS).transpose(1, 3, 0, 2).reshape(P, NPAIR, SC),
        "sinks": x["attn_sinks"].reshape(NH),
        "w_router": np.concatenate([x["w_router_group"][0], x["w_router_expert"][0].transpose(1, 0, 2).reshape(D, NE)],
                                   axis=1).reshape(P, DC, NG + NE),
        "b_router": np.concatenate([x["b_router_group"].reshape(-1), x["b_router_expert"].reshape(-1)]),
        "w_in": x["w_in"][0], "w_glu": x["w_glu"][0], "w_out": x["w_out"][0],
        "w_gate": x["w_gate"].reshape(NE, D, FF), "w_up": x["w_up"].reshape(NE, D, FF),
        "w_down": x["w_down"].reshape(NE, FF, D), "g_final": x["g_final"],
    }
    nc = bacc.Bacc("TRN2", target_bir_lowering=False, num_devices=1)
    feed, aps = {}, {}
    for name, v in arrays.items():
        v = np.ascontiguousarray(v)
        feed[f"in_{name}"] = v
        aps[name] = nc.dram_tensor(f"in_{name}", v.shape, mybir.dt.from_np(v.dtype), kind="ExternalInput").ap()
    out = nc.dram_tensor("out_block", (T, D), F32, kind="ExternalOutput").ap()
    hymba_block(nc, aps, out)
    r = run_bass_kernel_spmd(nc, [feed], core_ids=[0])
    return r.results[0]["out_block"].reshape(1, T, D)
```
